# Optimizing a Trainium2 kernel written in Bass

```python
import math
import jax
import jax.numpy as jnp
from jax import lax
import numpy as np
import jax, jax.numpy as jnp

D_MODEL = 1024
BATCH = 1
SEQ = 512
DEPTH = 1

HEAD_DIM = 64
A_HEADS = 8
DIL_PATTERNS = ((128, 1), (512, 4), (2048, 16))
DIL_BLOCK = 128
B_HEADS = 8
B_KV_HEADS = 2
B_GROUP = B_HEADS // B_KV_HEADS
CMP_LEN = 32
CMP_STRIDE = 16
CMP_HIDDEN = 128
SEL_BLOCK = 64
SEL_TOPN = 16
SEL_Q_CHUNK = 64
CMP_OVERLAP = (1.0, 2.0, 2.0, 2.0, 1.0)
WIN_LEN = 512
WIN_BLOCK = 128
N_BRANCH = 3
REL_BUCKETS = 32
REL_MAX_DIST = 2048
N_HEADS_TOTAL = A_HEADS + B_HEADS
FFN_HIDDEN = ((-(-8 * D_MODEL // 3)) + 255) // 256 * 256
RMS_EPS = 1e-6
A_WIDTH = A_HEADS * HEAD_DIM
B_WIDTH = B_HEADS * HEAD_DIM
KV_WIDTH = B_KV_HEADS * HEAD_DIM
GATE_WIDTH = B_HEADS * N_BRANCH
IN_SPLITS = (A_WIDTH, A_WIDTH, A_WIDTH, B_WIDTH, KV_WIDTH, KV_WIDTH, KV_WIDTH, KV_WIDTH, KV_WIDTH, KV_WIDTH, GATE_WIDTH)
IN_WIDTH = sum(IN_SPLITS)
SCALE = HEAD_DIM ** -0.5


def rms_norm(x, g):
    xf = x.astype(jnp.float32)
    y = xf * lax.rsqrt(jnp.mean(xf * xf, axis=-1, keepdims=True) + RMS_EPS)
    return (y * g.astype(jnp.float32)).astype(x.dtype)

def t5_bucket(dist):
    max_exact = REL_BUCKETS // 2
    df = jnp.maximum(dist, 1).astype(jnp.float32)
    large = max_exact + (jnp.log(df / max_exact) / math.log(REL_MAX_DIST / max_exact)
                         * (REL_BUCKETS - max_exact)).astype(jnp.int32)
    large = jnp.minimum(large, REL_BUCKETS - 1)
    return jnp.where(dist < max_exact, dist, large)

def masked_softmax(logits, mask):
    logits = jnp.where(mask, logits, -jnp.inf)
    m = jnp.max(logits, axis=-1, keepdims=True)
    m = jnp.where(jnp.isfinite(m), m, 0.0)
    p = jnp.exp(logits - m)
    den = jnp.sum(p, axis=-1, keepdims=True)
    return p / jnp.maximum(den, 1e-30)

def split_columns(t):
    out, start = [], 0
    for w in IN_SPLITS:
        out.append(t[..., start:start + w])
        start += w
    return out

def to_heads(t, n):
    b, s, _ = t.shape
    return t.reshape(b, s, n, HEAD_DIM).transpose(0, 2, 1, 3)

def dilated_attention(q, k, v, table, window, dil):
    b, h, s, dh = q.shape
    steps = window // dil
    unit = dil * DIL_BLOCK
    sp = -(-s // unit) * unit
    length = sp // dil
    nb = length // DIL_BLOCK

    def to_blocks(t):
        t = jnp.pad(t, ((0, 0), (0, 0), (0, sp - s), (0, 0)))
        t = t.reshape(b, h, length, dil, dh).transpose(0, 1, 3, 2, 4)
        return t.reshape(b, h, dil, nb, DIL_BLOCK, dh)

    def with_prev(t):
        prev = jnp.pad(t[:, :, :, :-1], ((0, 0), (0, 0), (0, 0), (1, 0), (0, 0), (0, 0)))
        return jnp.concatenate([prev, t], axis=4)

    qb = to_blocks(q)
    kk = with_prev(to_blocks(k))
    vv = with_prev(to_blocks(v))
    i = jnp.arange(DIL_BLOCK)[:, None]
    j = jnp.arange(2 * DIL_BLOCK)[None, :]
    dist = i + DIL_BLOCK - j
    mask = (dist >= 0) & (dist <= steps)
    first = (jnp.arange(nb)[:, None, None] > 0) | (j[None] >= DIL_BLOCK)
    mask = mask[None] & first
    bias = table[:, t5_bucket(jnp.maximum(dist, 0) * dil)]
    sc = jnp.einsum('bhrnqd,bhrnkd->bhrnqk', qb, kk, preferred_element_type=jnp.float32) * SCALE
    sc = jnp.where(mask, sc + bias[None, :, None, None], -jnp.inf)
    m = jnp.max(sc, axis=-1, keepdims=True)
    p = jnp.exp(sc - m)
    den = jnp.sum(p, axis=-1, keepdims=True)
    o = jnp.einsum('bhrnqk,bhrnkd->bhrnqd', p, vv.astype(jnp.float32)) / den
    lse = (m + jnp.log(den))[..., 0]
    o = o.reshape(b, h, dil, length, dh).transpose(0, 1, 3, 2, 4).reshape(b, h, sp, dh)[:, :, :s]
    lse = lse.reshape(b, h, dil, length).transpose(0, 1, 3, 2).reshape(b, h, sp)[:, :, :s]
    return o, lse

def mixer_dilated(q, k, v, table):
    outs, lses = [], []
    for window, dil in DIL_PATTERNS:
        o, lse = dilated_attention(q, k, v, table, window, dil)
        outs.append(o)
        lses.append(lse)
    w = jax.nn.softmax(jnp.stack(lses, axis=0), axis=0)
    return jnp.sum(w[..., None] * jnp.stack(outs, axis=0), axis=0)

def nsa_compress(kraw, pos, w1, b1, w2):
    b, g, s, dh = kraw.shape
    ch = kraw.reshape(b, g, s // CMP_STRIDE, CMP_STRIDE, dh)
    blk = jnp.concatenate([ch[:, :, :-1], ch[:, :, 1:]], axis=3) + pos
    hid = jax.nn.gelu(jnp.einsum('bgnld,ldh->bgnh', blk, w1) + b1)
    return hid @ w2

def nsa_compressed_branch(q, kc, vc):
    s = q.shape[3]
    nc = kc.shape[2]
    t = jnp.arange(s)
    block_end = jnp.arange(nc) * CMP_STRIDE + CMP_LEN - 1
    mask = block_end[None, :] <= t[:, None]
    sc = jnp.einsum('bgrqd,bgnd->bgrqn', q, kc, preferred_element_type=jnp.float32) * SCALE
    p = masked_softmax(sc, mask)
    o = jnp.einsum('bgrqn,bgnd->bgrqd', p, vc.astype(jnp.float32))
    return o, jnp.sum(p, axis=2)

def block_importance(pc, nb):
    ratio = SEL_BLOCK // CMP_STRIDE
    pp = jnp.pad(pc, ((0, 0), (0, 0), (0, 0), (1, 1)))
    imp = 0.0
    for off, w in zip(range(-1, ratio), CMP_OVERLAP):
        imp = imp + w * pp[..., off + 1: off + 2 + ratio * (nb - 1): ratio]
    return imp

def nsa_selected_branch(q, k, v, imp, table):
    b, g, r, s, dh = q.shape
    nb = s // SEL_BLOCK
    topn = min(SEL_TOPN, nb)
    t = jnp.arange(s)
    cur = (t // SEL_BLOCK)[:, None]
    j = jnp.arange(nb)[None, :]
    forced = (j == 0) | (j == cur) | (j == cur - 1)
    imp = jnp.where(j > cur, -jnp.inf, jnp.where(forced, jnp.inf, imp))
    _, idx = lax.top_k(imp, topn)
    kblk = k.reshape(b, g, nb, SEL_BLOCK * dh)
    vblk = v.reshape(b, g, nb, SEL_BLOCK * dh)
    nch = s // SEL_Q_CHUNK
    qc = q.reshape(b, g, r, nch, SEL_Q_CHUNK, dh).transpose(3, 0, 1, 2, 4, 5)
    ic = idx.reshape(b, g, nch, SEL_Q_CHUNK, topn).transpose(2, 0, 1, 3, 4)
    tab = table.transpose(0, 2, 1)
    b_idx = jnp.arange(b)[:, None, None]
    g_idx3 = jnp.arange(g)[None, :, None]
    g_idx4 = jnp.arange(g)[None, :, None, None]
    nkey = topn * SEL_BLOCK

    def chunk(args):
        qq, ii, c = args
        flat = ii.reshape(b, g, SEL_Q_CHUNK * topn)
        kg = kblk[b_idx, g_idx3, flat].reshape(b, g, SEL_Q_CHUNK, nkey, dh)
        vg = vblk[b_idx, g_idx3, flat].reshape(b, g, SEL_Q_CHUNK, nkey, dh)
        kpos = (ii[..., None] * SEL_BLOCK + jnp.arange(SEL_BLOCK)).reshape(b, g, SEL_Q_CHUNK, nkey)
        tq = c * SEL_Q_CHUNK + jnp.arange(SEL_Q_CHUNK)
        dist = tq[None, None, :, None] - kpos
        bias = tab[g_idx4, t5_bucket(jnp.maximum(dist, 0))].transpose(0, 1, 4, 2, 3)
        sc = jnp.einsum('bgrqd,bgqkd->bgrqk', qq, kg, preferred_element_type=jnp.float32) * SCALE + bias
        p = masked_softmax(sc, (dist >= 0)[:, :, None])
        return jnp.einsum('bgrqk,bgqkd->bgrqd', p, vg.astype(jnp.float32))

    out = lax.map(chunk, (qc, ic, jnp.arange(nch)))
    return out.transpose(1, 2, 3, 0, 4, 5).reshape(b, g, r, s, dh)

def nsa_window_branch(q, k, v, table):
    b, g, r, s, dh = q.shape
    nb = s // WIN_BLOCK
    nw = WIN_LEN // WIN_BLOCK
    qb = q.reshape(b, g, r, nb, WIN_BLOCK, dh)

    def band(t):
        tb = jnp.pad(t.reshape(b, g, nb, WIN_BLOCK, dh), ((0, 0), (0, 0), (nw, 0), (0, 0), (0, 0)))
        return jnp.concatenate([tb[:, :, o:o + nb] for o in range(nw + 1)], axis=3)

    kk, vv = band(k), band(v)
    i = jnp.arange(WIN_BLOCK)[:, None]
    j = jnp.arange((nw + 1) * WIN_BLOCK)[None, :]
    dist = i + nw * WIN_BLOCK - j
    kpos = jnp.arange(nb)[:, None, None] * WIN_BLOCK + j[None] - nw * WIN_BLOCK
    mask = ((dist >= 0) & (dist < WIN_LEN))[None] & (kpos >= 0)
    bias = table[:, :, t5_bucket(jnp.maximum(dist, 0))]
    sc = jnp.einsum('bgrnqd,bgnkd->bgrnqk', qb, kk, preferred_element_type=jnp.float32) * SCALE
    p = masked_softmax(sc + bias[None, :, :, None], mask)
    o = jnp.einsum('bgrnqk,bgnkd->bgrnqd', p, vv.astype(jnp.float32))
    return o.reshape(b, g, r, s, dh)

def first_inputs(seed: int = 0) -> dict:
    key = jax.random.key(seed)
    ks = jax.random.split(key, 18)
    f32 = jnp.float32
    nrm = lambda k, shape, scale: jax.random.normal(k, shape, f32) * scale
    return {
        "x": nrm(ks[0], (BATCH, SEQ, D_MODEL), 1.0),
        "norm1_g": 1.0 + nrm(ks[1], (DEPTH, D_MODEL), 0.02),
        "w_in": nrm(ks[2], (DEPTH, D_MODEL, IN_WIDTH), D_MODEL ** -0.5),
        "rel_bias": nrm(ks[3], (REL_BUCKETS, N_HEADS_TOTAL), 0.1),
        "cmp_pos": nrm(ks[4], (DEPTH, CMP_LEN, HEAD_DIM), 0.2),
        "cmp_k_w1": nrm(ks[5], (DEPTH, CMP_LEN, HEAD_DIM, CMP_HIDDEN), (CMP_LEN * HEAD_DIM) ** -0.5),
        "cmp_k_b1": nrm(ks[6], (DEPTH, CMP_HIDDEN), 0.02),
        "cmp_k_w2": nrm(ks[7], (DEPTH, CMP_HIDDEN, HEAD_DIM), CMP_HIDDEN ** -0.5),
        "cmp_v_w1": nrm(ks[8], (DEPTH, CMP_LEN, HEAD_DIM, CMP_HIDDEN), (CMP_LEN * HEAD_DIM) ** -0.5),
        "cmp_v_b1": nrm(ks[9], (DEPTH, CMP_HIDDEN), 0.02),
        "cmp_v_w2": nrm(ks[10], (DEPTH, CMP_HIDDEN, HEAD_DIM), CMP_HIDDEN ** -0.5),
        "w_out": nrm(ks[11], (DEPTH, A_WIDTH + B_WIDTH, D_MODEL), (A_WIDTH + B_WIDTH) ** -0.5),
        "norm2_g": 1.0 + nrm(ks[12], (DEPTH, D_MODEL), 0.02),
        "w_gate": nrm(ks[13], (DEPTH, D_MODEL, FFN_HIDDEN), D_MODEL ** -0.5),
        "w_up": nrm(ks[14], (DEPTH, D_MODEL, FFN_HIDDEN), D_MODEL ** -0.5),
        "w_down": nrm(ks[15], (DEPTH, FFN_HIDDEN, D_MODEL), FFN_HIDDEN ** -0.5),
        "norm_f_g": 1.0 + nrm(ks[16], (D_MODEL,), 0.02),
    }

def first_block(x, norm1_g, w_in, rel_bias, cmp_pos, cmp_k_w1, cmp_k_b1, cmp_k_w2,
              cmp_v_w1, cmp_v_b1, cmp_v_w2, w_out, norm2_g, w_gate, w_up, w_down, norm_f_g):
    b, s, _ = x.shape
    tab_a = rel_bias[:, :A_HEADS].T
    tab_b = rel_bias[:, A_HEADS:].T.reshape(B_KV_HEADS, B_GROUP, REL_BUCKETS)
    h = x
    for layer in range(DEPTH):
        xn = rms_norm(h, norm1_g[layer])
        aq, ak, av, bq, kc, vc, ksl, vsl, kw, vw, gl = split_columns(xn @ w_in[layer])
        o_a = mixer_dilated(to_heads(aq, A_HEADS), to_heads(ak, A_HEADS), to_heads(av, A_HEADS), tab_a)
        q_b = to_heads(bq, B_HEADS).reshape(b, B_KV_HEADS, B_GROUP, s, HEAD_DIM)
        k_cmp = nsa_compress(to_heads(kc, B_KV_HEADS), cmp_pos[layer], cmp_k_w1[layer], cmp_k_b1[layer], cmp_k_w2[layer])
        v_cmp = nsa_compress(to_heads(vc, B_KV_HEADS), cmp_pos[layer], cmp_v_w1[layer], cmp_v_b1[layer], cmp_v_w2[layer])
        o_cmp, p_cmp = nsa_compressed_branch(q_b, k_cmp, v_cmp)
        imp = block_importance(p_cmp, s // SEL_BLOCK)
        o_slc = nsa_selected_branch(q_b, to_heads(ksl, B_KV_HEADS), to_heads(vsl, B_KV_HEADS), imp, tab_b)
        o_win = nsa_window_branch(q_b, to_heads(kw, B_KV_HEADS), to_heads(vw, B_KV_HEADS), tab_b)
        gate = jax.nn.sigmoid(gl.astype(jnp.float32)).reshape(b, s, B_KV_HEADS, B_GROUP, N_BRANCH).transpose(0, 2, 3, 1, 4)
        o_b = gate[..., 0:1] * o_cmp + gate[..., 1:2] * o_slc + gate[..., 2:3] * o_win
        mix = jnp.concatenate([
            o_a.transpose(0, 2, 1, 3).reshape(b, s, A_WIDTH),
            o_b.reshape(b, B_HEADS, s, HEAD_DIM).transpose(0, 2, 1, 3).reshape(b, s, B_WIDTH),
        ], axis=-1).astype(h.dtype)
        h = h + mix @ w_out[layer]
        hn = rms_norm(h, norm2_g[layer])
        h = h + (jax.nn.silu(hn @ w_gate[layer]) * (hn @ w_up[layer])) @ w_down[layer]
    return rms_norm(h, norm_f_g)


DEPTH_2 = 2

GRID_W = 64
CTX_LEN = 256
AXIS_DIM = HEAD_DIM // 2
ROPE_THETA = 10000.0
EPS = 1e-6
Q_BLOCK = 128
N_MOD = 6

GLA_HEADS = 4
GLA_DK = 64
GLA_DV = 128
GLA_GATE_RANK = 16
GLA_GATE_NORM = 16.0
GLA_CHUNK = 64
ATT_HEADS = 8
ATT_KV_HEADS = 2
SWA_HEADS = 16
SWA_KV_HEADS = 2
SWA_WINDOW = 128
MOE_GROUPS = 4
MOE_EXPERTS_PER_GROUP = 4
MOE_TOPK = 2
D_EXPERT = 256

EVEN_WIDTHS = (GLA_HEADS * GLA_DK, GLA_HEADS * GLA_DK, GLA_HEADS * GLA_DV, GLA_HEADS * GLA_DV,
               2 * GLA_GATE_RANK, ATT_HEADS * HEAD_DIM, ATT_KV_HEADS * HEAD_DIM, ATT_KV_HEADS * HEAD_DIM)
EVEN_IN = sum(EVEN_WIDTHS)
EVEN_MIX = GLA_HEADS * GLA_DV + ATT_HEADS * HEAD_DIM
ODD_Q = SWA_HEADS * HEAD_DIM
ODD_KV = SWA_KV_HEADS * HEAD_DIM
ODD_IN = ODD_Q + 2 * ODD_KV
ODD_MIX = ODD_Q
N_EVEN = (DEPTH_2 + 1) // 2
N_ODD = DEPTH_2 // 2


def _split(z, widths):
    return jnp.split(z, np.cumsum(widths)[:-1].tolist(), axis=-1)

def rms_norm_2(x, gain):
    xf = x.astype(jnp.float32)
    y = xf * lax.rsqrt(jnp.mean(xf * xf, axis=-1, keepdims=True) + EPS)
    return (y * gain.astype(jnp.float32)).astype(x.dtype)

def modulate(x, gain, shift, scale):
    return rms_norm_2(x, gain) * (1 + scale) + shift

def axial_rope_tables(n):
    rows = n // GRID_W
    row = jnp.repeat(jnp.arange(rows, dtype=jnp.int32), GRID_W)
    col = jnp.tile(jnp.arange(GRID_W, dtype=jnp.int32), rows)
    inv_freq = ROPE_THETA ** (-jnp.arange(0, AXIS_DIM, 2, dtype=jnp.float32) / AXIS_DIM)
    ang = jnp.stack([row[:, None] * inv_freq, col[:, None] * inv_freq], axis=1)
    return jnp.cos(ang), jnp.sin(ang)

def apply_axial_rope(x, cos, sin):
    B, n, H, _ = x.shape
    xs = x.reshape(B, n, H, 2, 2, AXIS_DIM // 2)
    x1, x2 = xs[..., 0, :], xs[..., 1, :]
    c = cos[None, :, None].astype(x.dtype)
    s = sin[None, :, None].astype(x.dtype)
    out = jnp.stack([x1 * c - x2 * s, x2 * c + x1 * s], axis=-2)
    return out.reshape(B, n, H, HEAD_DIM)

def heads(z, n_heads, gain):
    B, L, _ = z.shape
    return rms_norm_2(z.reshape(B, L, n_heads, HEAD_DIM), gain)

def group_q(q, n_kv):
    B, L, H, Dh = q.shape
    return q.reshape(B, L, n_kv, H // n_kv, Dh)

def softmax_attend(q, k, v, mask=None, sink=None):
    B, Q, KV, G, Dh = q.shape
    s = jnp.einsum('bqhgd,bkhd->bhgqk', q, k).astype(jnp.float32) * (Dh ** -0.5)
    if mask is not None:
        s = jnp.where(mask, s, -jnp.inf)
    if sink is not None:
        sink_col = jnp.broadcast_to(sink.reshape(1, KV, G, 1, 1).astype(jnp.float32), s.shape[:-1] + (1,))
        p = jax.nn.softmax(jnp.concatenate([s, sink_col], axis=-1), axis=-1)[..., :-1]
    else:
        p = jax.nn.softmax(s, axis=-1)
    o = jnp.einsum('bhgqk,bkhd->bqhgd', p.astype(v.dtype), v)
    return o.reshape(B, Q, KV * G * Dh)

def blocked_dense_attention(q, k, v):
    B, S = q.shape[:2]
    nb = S // Q_BLOCK
    qb = jnp.moveaxis(q.reshape(B, nb, Q_BLOCK, *q.shape[2:]), 1, 0)
    ob = lax.map(lambda qi: softmax_attend(qi, k, v), qb)
    return jnp.moveaxis(ob, 0, 1).reshape(B, S, -1)

def banded_window_attention(q, k, v, k_ctx, v_ctx, sink):
    B, S = q.shape[:2]
    nb = S // Q_BLOCK
    span = Q_BLOCK + 2 * SWA_WINDOW
    pad = ((0, 0), (SWA_WINDOW, SWA_WINDOW), (0, 0), (0, 0))
    kp = jnp.pad(k, pad)
    vp = jnp.pad(v, pad)
    qb = jnp.moveaxis(q.reshape(B, nb, Q_BLOCK, *q.shape[2:]), 1, 0)
    ctx_ok = jnp.ones((Q_BLOCK, k_ctx.shape[1]), dtype=bool)

    def block(args):
        qi, bi = args
        start = bi * Q_BLOCK
        kb = lax.dynamic_slice_in_dim(kp, start, span, axis=1)
        vb = lax.dynamic_slice_in_dim(vp, start, span, axis=1)
        qpos = start + jnp.arange(Q_BLOCK, dtype=jnp.int32)
        kpos = start - SWA_WINDOW + jnp.arange(span, dtype=jnp.int32)
        band = (kpos[None, :] >= 0) & (kpos[None, :] < S) & (jnp.abs(kpos[None, :] - qpos[:, None]) <= SWA_WINDOW)
        mask = jnp.concatenate([band, ctx_ok], axis=1)
        return softmax_attend(qi, jnp.concatenate([kb, k_ctx], axis=1), jnp.concatenate([vb, v_ctx], axis=1), mask, sink)

    ob = lax.map(block, (qb, jnp.arange(nb, dtype=jnp.int32)))
    return jnp.moveaxis(ob, 0, 1).reshape(B, S, -1)

def gla_chunk_scan(q, k, v, g, s0):
    B, H, L, DK = q.shape
    DV = v.shape[-1]
    n = L // GLA_CHUNK

    def chunks(t):
        return jnp.moveaxis(t.reshape(B, H, n, GLA_CHUNK, t.shape[-1]), 2, 0)

    lower_tri = jnp.tril(jnp.ones((GLA_CHUNK, GLA_CHUNK), dtype=bool))[:, :, None]

    def step(s, blk):
        qc, kc, vc, gc = blk
        b = jnp.cumsum(gc, axis=2)
        o = jnp.einsum('bhtk,bhkv->bhtv', qc * jnp.exp(b), s)
        diff = b[:, :, :, None, :] - b[:, :, None, :, :]
        decay = jnp.exp(jnp.where(lower_tri, diff, -jnp.inf))
        att = jnp.einsum('bhtk,bhsk,bhtsk->bhts', qc, kc, decay)
        o = o + jnp.einsum('bhts,bhsv->bhtv', att, vc)
        b_end = b[:, :, -1:, :]
        s = jnp.exp(b_end[:, :, 0, :, None]) * s + jnp.einsum('bhsk,bhsv->bhkv', kc * jnp.exp(b_end - b), vc)
        return s, o

    s_fin, o = lax.scan(step, s0, (chunks(q), chunks(k), chunks(v), chunks(g)))
    return jnp.moveaxis(o, 0, 2).reshape(B, H, L, DV), s_fin

def gla_inputs(q, k, v, lr, gate_w, gate_b):
    B, L, _ = q.shape

    def hd(t, d):
        return t.reshape(B, L, GLA_HEADS, d).transpose(0, 2, 1, 3).astype(jnp.float32)

    z = jnp.einsum('blzr,zrk->zblk', lr.reshape(B, L, 2, GLA_GATE_RANK), gate_w) + gate_b[:, None, None, :]
    g = jax.nn.log_sigmoid(z.astype(jnp.float32)) / GLA_GATE_NORM
    g = g.reshape(2, B, L, GLA_HEADS, GLA_DK).transpose(0, 1, 3, 2, 4)
    return hd(q, GLA_DK) * (GLA_DK ** -0.5), hd(k, GLA_DK), hd(v, GLA_DV), g

def gla_bidirectional(lat, ctx):
    ql, kl, vl, gl = lat
    qc, kc, vc, gc = ctx
    B = ql.shape[0]
    s0 = jnp.zeros((B, GLA_HEADS, GLA_DK, GLA_DV), jnp.float32)

    def rev(t):
        return jnp.flip(t, axis=2)

    oc_f, sc_f = gla_chunk_scan(qc, kc, vc, gc[0], s0)
    oc_b, sc_b = gla_chunk_scan(rev(qc), rev(kc), rev(vc), rev(gc[1]), s0)
    ol_f, _ = gla_chunk_scan(ql, kl, vl, gl[0], sc_f)
    ol_b, _ = gla_chunk_scan(rev(ql), rev(kl), rev(vl), rev(gl[1]), sc_b)
    return ol_f + rev(ol_b), oc_f + rev(oc_b)

def gla_output(o, r, gain):
    B, H, L, _ = o.shape
    o = rms_norm_2(o.transpose(0, 2, 1, 3), gain).astype(r.dtype)
    return (o * jax.nn.silu(r.reshape(B, L, H, GLA_DV))).reshape(B, L, H * GLA_DV)

def even_mixer(h_lat, h_ctx, w_in, w_out, gate_w, gate_b, gla_norm, q_norm, k_norm, cos, sin):
    B, S, _ = h_lat.shape
    Lc = h_ctx.shape[1]
    z_l = _split(h_lat @ w_in, EVEN_WIDTHS)
    z_c = _split(h_ctx @ w_in, EVEN_WIDTHS)
    o_gla_l, o_gla_c = gla_bidirectional(gla_inputs(z_l[0], z_l[1], z_l[2], z_l[4], gate_w, gate_b),
                                         gla_inputs(z_c[0], z_c[1], z_c[2], z_c[4], gate_w, gate_b))
    a_l = gla_output(o_gla_l, z_l[3], gla_norm)
    a_c = gla_output(o_gla_c, z_c[3], gla_norm)
    q_l = group_q(apply_axial_rope(heads(z_l[5], ATT_HEADS, q_norm), cos, sin), ATT_KV_HEADS)
    k_l = apply_axial_rope(heads(z_l[6], ATT_KV_HEADS, k_norm), cos, sin)
    v_l = z_l[7].reshape(B, S, ATT_KV_HEADS, HEAD_DIM)
    q_c = group_q(heads(z_c[5], ATT_HEADS, q_norm), ATT_KV_HEADS)
    k_c = heads(z_c[6], ATT_KV_HEADS, k_norm)
    v_c = z_c[7].reshape(B, Lc, ATT_KV_HEADS, HEAD_DIM)
    b_l = blocked_dense_attention(q_l, jnp.concatenate([k_l, k_c], axis=1), jnp.concatenate([v_l, v_c], axis=1))
    b_c = softmax_attend(q_c, k_c, v_c)
    return jnp.concatenate([a_l, b_l], axis=-1) @ w_out, jnp.concatenate([a_c, b_c], axis=-1) @ w_out

def odd_mixer(h_lat, h_ctx, w_in, w_out, sink, q_norm, k_norm, cos, sin, need_ctx):
    B, S, _ = h_lat.shape
    Lc = h_ctx.shape[1]
    q_l, k_l, v_l = _split(h_lat @ w_in, (ODD_Q, ODD_KV, ODD_KV))
    k_c, v_c = _split(h_ctx @ w_in[:, ODD_Q:], (ODD_KV, ODD_KV))
    q = group_q(apply_axial_rope(heads(q_l, SWA_HEADS, q_norm), cos, sin), SWA_KV_HEADS)
    k = apply_axial_rope(heads(k_l, SWA_KV_HEADS, k_norm), cos, sin)
    v = v_l.reshape(B, S, SWA_KV_HEADS, HEAD_DIM)
    kc = heads(k_c, SWA_KV_HEADS, k_norm)
    vc = v_c.reshape(B, Lc, SWA_KV_HEADS, HEAD_DIM)
    m_l = banded_window_attention(q, k, v, kc, vc, sink) @ w_out
    if not need_ctx:
        return m_l, None
    qc = group_q(heads(h_ctx @ w_in[:, :ODD_Q], SWA_HEADS, q_norm), SWA_KV_HEADS)
    return m_l, softmax_attend(qc, kc, vc, None, sink) @ w_out

def hier_moe(h, wg, bg, we, be, w_gate, w_up, w_down):
    N = h.shape[0]
    g_logits = (h @ wg + bg).astype(jnp.float32)
    g_prob = jax.nn.softmax(g_logits, axis=-1)
    g_idx = jnp.argmax(g_logits, axis=-1)
    g_weight = jnp.take_along_axis(g_prob, g_idx[:, None], axis=-1)
    e_logits = (h @ we + be).astype(jnp.float32).reshape(N, MOE_GROUPS, MOE_EXPERTS_PER_GROUP)
    e_sel = jnp.take_along_axis(e_logits, g_idx[:, None, None], axis=1)[:, 0]
    top_p, top_i = lax.top_k(jax.nn.softmax(e_sel, axis=-1), MOE_TOPK)
    top_p = top_p / jnp.sum(top_p, axis=-1, keepdims=True)
    e_weight = jnp.sum(jax.nn.one_hot(top_i, MOE_EXPERTS_PER_GROUP, dtype=jnp.float32) * top_p[..., None], axis=1)
    combine = (jax.nn.one_hot(g_idx, MOE_GROUPS, dtype=jnp.float32)[:, :, None]
               * (g_weight * e_weight)[:, None, :]).astype(h.dtype)
    out = jnp.zeros_like(h)
    for g in range(MOE_GROUPS):
        a = jnp.einsum('nd,edf->nef', h, w_gate[g])
        u = jnp.einsum('nd,edf->nef', h, w_up[g])
        hid = jax.nn.silu(a) * u * combine[:, g, :, None]
        out = out + jnp.einsum('nef,efd->nd', hid, w_down[g])
    return out

def second_inputs(seed: int = 0) -> dict:
    key = jax.random.key(seed)
    ks = iter(jax.random.split(key, 32))
    D = D_MODEL
    G, E = MOE_GROUPS, MOE_EXPERTS_PER_GROUP

    def nrm(shape, scale):
        return scale * jax.random.normal(next(ks), shape, jnp.float32)

    def gain(shape):
        return 1.0 + 0.02 * jax.random.normal(next(ks), shape, jnp.float32)

    return {
        'x': nrm((BATCH, SEQ, D), 1.0),
        'c': nrm((BATCH, D), 1.0),
        'ctx': nrm((BATCH, CTX_LEN, D), 1.0),
        'c_ctx': nrm((D,), 1.0),
        'mod_w': nrm((DEPTH_2, D, N_MOD * D), 0.5 * D ** -0.5),
        'mod_b': nrm((DEPTH_2, N_MOD * D), 0.02),
        'norm_mix': gain((DEPTH_2, D)),
        'norm_ffn': gain((DEPTH_2, D)),
        'ev_w_in': nrm((N_EVEN, D, EVEN_IN), D ** -0.5),
        'ev_w_out': nrm((N_EVEN, EVEN_MIX, D), EVEN_MIX ** -0.5),
        'gla_gate_w': nrm((N_EVEN, 2, GLA_GATE_RANK, GLA_HEADS * GLA_DK), GLA_GATE_RANK ** -0.5),
        'gla_gate_b': nrm((N_EVEN, 2, GLA_HEADS * GLA_DK), 0.1),
        'gla_out_norm': gain((N_EVEN, GLA_DV)),
        'att_q_norm': gain((N_EVEN, HEAD_DIM)),
        'att_k_norm': gain((N_EVEN, HEAD_DIM)),
        'od_w_in': nrm((N_ODD, D, ODD_IN), D ** -0.5),
        'od_w_out': nrm((N_ODD, ODD_MIX, D), ODD_MIX ** -0.5),
        'swa_sink': nrm((N_ODD, SWA_HEADS), 1.0),
        'swa_q_norm': gain((N_ODD, HEAD_DIM)),
        'swa_k_norm': gain((N_ODD, HEAD_DIM)),
        'router_group_w': nrm((DEPTH_2, D, G), D ** -0.5),
        'router_group_b': nrm((DEPTH_2, G), 0.01),
        'router_expert_w': nrm((DEPTH_2, D, G * E), D ** -0.5),
        'router_expert_b': nrm((DEPTH_2, G * E), 0.01),
        'exp_w_gate': nrm((DEPTH_2, G, E, D, D_EXPERT), D ** -0.5),
        'exp_w_up': nrm((DEPTH_2, G, E, D, D_EXPERT), D ** -0.5),
        'exp_w_down': nrm((DEPTH_2, G, E, D_EXPERT, D), D_EXPERT ** -0.5),
    }

def second_block(x, c, ctx, c_ctx, mod_w, mod_b, norm_mix, norm_ffn, ev_w_in, ev_w_out, gla_gate_w, gla_gate_b,
              gla_out_norm, att_q_norm, att_k_norm, od_w_in, od_w_out, swa_sink, swa_q_norm, swa_k_norm,
              router_group_w, router_group_b, router_expert_w, router_expert_b, exp_w_gate, exp_w_up, exp_w_down):
    B, S, D = x.shape
    cos, sin = axial_rope_tables(S)
    sc = jax.nn.silu(c)
    scc = jax.nn.silu(c_ctx)[None]
    for i in range(DEPTH_2):
        last = i == DEPTH_2 - 1
        j = i // 2
        mod_l = jnp.split((sc @ mod_w[i] + mod_b[i])[:, None, :], N_MOD, axis=-1)
        mod_c = jnp.split((scc @ mod_w[i] + mod_b[i])[:, None, :], N_MOD, axis=-1)
        h_l = modulate(x, norm_mix[i], mod_l[0], mod_l[1])
        h_c = modulate(ctx, norm_mix[i], mod_c[0], mod_c[1])
        if i % 2 == 0:
            m_l, m_c = even_mixer(h_l, h_c, ev_w_in[j], ev_w_out[j], gla_gate_w[j], gla_gate_b[j],
                                  gla_out_norm[j], att_q_norm[j], att_k_norm[j], cos, sin)
        else:
            m_l, m_c = odd_mixer(h_l, h_c, od_w_in[j], od_w_out[j], swa_sink[j], swa_q_norm[j],
                                 swa_k_norm[j], cos, sin, not last)
        x = x + mod_l[2] * m_l
        moe_p = (router_group_w[i], router_group_b[i], router_expert_w[i], router_expert_b[i],
                 exp_w_gate[i], exp_w_up[i], exp_w_down[i])
        if last:
            f_l = hier_moe(modulate(x, norm_ffn[i], mod_l[3], mod_l[4]).reshape(B * S, D), *moe_p)
            x = x + mod_l[5] * f_l.reshape(B, S, D)
        else:
            ctx = ctx + mod_c[2] * m_c
            tok = jnp.concatenate([modulate(x, norm_ffn[i], mod_l[3], mod_l[4]).reshape(B * S, D),
                                   modulate(ctx, norm_ffn[i], mod_c[3], mod_c[4]).reshape(-1, D)], axis=0)
            f = hier_moe(tok, *moe_p)
            x = x + mod_l[5] * f[:B * S].reshape(B, S, D)
            ctx = ctx + mod_c[5] * f[B * S:].reshape(ctx.shape)
    return x


def setup_inputs(seed=0):
    out = dict(first_inputs(seed))
    for name, value in second_inputs(seed + 1).items():
        if name != "x":
            out[name + "_2"] = value
    return out


def reference(
    x, norm1_g, w_in, rel_bias, cmp_pos, cmp_k_w1, cmp_k_b1, cmp_k_w2, cmp_v_w1, cmp_v_b1,
    cmp_v_w2, w_out, norm2_g, w_gate, w_up, w_down, norm_f_g, c_2, ctx_2, c_ctx_2, mod_w_2,
    mod_b_2, norm_mix_2, norm_ffn_2, ev_w_in_2, ev_w_out_2, gla_gate_w_2, gla_gate_b_2,
    gla_out_norm_2, att_q_norm_2, att_k_norm_2, od_w_in_2, od_w_out_2, swa_sink_2, swa_q_norm_2,
    swa_k_norm_2, router_group_w_2, router_group_b_2, router_expert_w_2, router_expert_b_2,
    exp_w_gate_2, exp_w_up_2, exp_w_down_2,
):
    x = first_block(
        x, norm1_g, w_in, rel_bias, cmp_pos, cmp_k_w1, cmp_k_b1, cmp_k_w2, cmp_v_w1, cmp_v_b1,
        cmp_v_w2, w_out, norm2_g, w_gate, w_up, w_down, norm_f_g,
    )
    return second_block(
        x, c_2, ctx_2, c_ctx_2, mod_w_2, mod_b_2, norm_mix_2, norm_ffn_2, ev_w_in_2, ev_w_out_2,
        gla_gate_w_2, gla_gate_b_2, gla_out_norm_2, att_q_norm_2, att_k_norm_2, od_w_in_2,
        od_w_out_2, swa_sink_2, swa_q_norm_2, swa_k_norm_2, router_group_w_2, router_group_b_2,
        router_expert_w_2, router_expert_b_2, exp_w_gate_2, exp_w_up_2, exp_w_down_2,
    )


_drawn_inputs = setup_inputs


def setup_inputs(seed=0):
    import zlib

    import numpy as np

    out = dict(_drawn_inputs(seed))
    spreads = {}
    factors = {'norm1_g': 4.904,
     'rel_bias': 3.523,
     'cmp_k_b1': 8.0,
     'cmp_v_b1': 5.941,
     'norm2_g': 3.127,
     'norm_mix_2': 5.705,
     'norm_ffn_2': 3.452,
     'gla_gate_b_2': 4.685,
     'gla_out_norm_2': 8.0,
     'att_q_norm_2': 8.0,
     'att_k_norm_2': 8.0,
     'swa_sink_2': 8.0,
     'swa_q_norm_2': 8.0,
     'swa_k_norm_2': 8.0,
     'router_group_b_2': 7.654,
     'router_expert_b_2': 7.583}
    for name, (base, spread) in spreads.items():
        noise = np.random.default_rng([zlib.crc32(name.encode()), seed]).standard_normal(out[name].shape)
        drawn = base * np.exp(spread * noise) if base else spread * noise
        out[name] = jnp.asarray(drawn.astype(out[name].dtype))
    for name, factor in factors.items():
        out[name] = (out[name] * factor).astype(out[name].dtype)
    return out
```

```python
from contextlib import ExitStack

import numpy as np

import concourse.bass as bass
from concourse import mybir

F32 = mybir.dt.float32
U8 = mybir.dt.uint8
ALU = mybir.AluOpType
ACT = mybir.ActivationFunctionType
AXX = mybir.AxisListType.X

P = 128
D = 1024
DK = D // P
SEQ, CTX = 512, 256
ST, CT = SEQ // P, CTX // P
NT = ST + CT
HD = 64
NEG = -1e30
EPS = 1e-6

A_HEADS, B_HEADS, B_KV = 8, 8, 2
IN_W = 3 * 512 + 512 + 6 * 128 + 24
AQ, AK, AV, BQ = 0, 512, 1024, 1536
KC, VC, KSL, VSL, KW, VW, GL = (2048 + 128 * i for i in range(7))
CMP_LEN, CMP_STRIDE, CMP_HID = 32, 16, 128
NCMP = SEQ // CMP_STRIDE - 1
FFN = 2816
BUCKETS, MAX_DIST = 32, 2048
ROW = 640

EV_W = 256 + 256 + 512 + 512 + 32 + 512 + 128 + 128
GQ, GK, GV, GR, LR, EQ, EK, EVV = 0, 256, 512, 1024, 1536, 1568, 2080, 2208
GH, GDK, GDV = 4, 64, 128
OD_W = 1024 + 256
OQ, OK_, OV = 0, 1024, 1152
SWA_HEADS = 16
NEXP, NGRP, EXH = 16, 4, 256
SLOTS = 6
SLOT = 2048


def _t5_bucket(dist):
    half = BUCKETS // 2
    df = np.maximum(dist, 1).astype(np.float32)
    large = half + (np.log(df / np.float32(half)) / np.float32(np.log(MAX_DIST / half))
                    * np.float32(BUCKETS - half)).astype(np.int32)
    return np.where(dist < half, dist, np.minimum(large, BUCKETS - 1))


def shape_constants():
    c = {}
    c["ident"] = np.eye(P, dtype=np.float32)
    d = 511 - np.arange(ROW)
    hot = np.zeros((BUCKETS + 1, 2, ROW), np.float32)
    b = _t5_bucket(np.maximum(d, 0))
    for j in range(ROW):
        if d[j] >= 0:
            hot[b[j], :, j] = 1.0
    count = (d <= 128).astype(int) + (d % 4 == 0) + (d % 16 == 0)
    hot[BUCKETS, 0] = np.where((d >= 0) & (count > 0), np.log(np.maximum(count, 1)), NEG)
    hot[BUCKETS, 1] = np.where(d >= 0, 0.0, NEG)
    c["hot"] = hot
    t = np.arange(SEQ)
    ends = np.arange(NCMP) * CMP_STRIDE + CMP_LEN - 1
    m = np.where(ends[None, :] <= t[:, None], 0.0, NEG).astype(np.float32)
    c["cmpmask"] = np.ascontiguousarray(m.reshape(ST, P, NCMP).transpose(1, 0, 2))
    c["cmpvalid"] = np.ascontiguousarray((t >= CMP_LEN - 1).astype(np.float32).reshape(ST, P).T)
    inv = np.float32(10000.0) ** (-np.arange(0, 32, 2, dtype=np.float32) / np.float32(32))
    ang = np.stack([(t // 64)[:, None].astype(np.float32) * inv, (t % 64)[:, None].astype(np.float32) * inv], 1)
    co, si = np.cos(ang), np.sin(ang)
    full = np.stack([np.stack([co, co], 2), np.stack([-si, si], 2)], 1).reshape(SEQ, 2, HD)
    c["rope"] = np.ascontiguousarray(full.reshape(ST, P, 2, HD).transpose(1, 0, 2, 3)).astype(np.float32)
    y, p = np.arange(384)[None, :], np.arange(P)[:, None]
    band = np.where((y - p >= 0) & (y - p <= 256), 0.0, NEG)
    c["band"] = np.concatenate([np.zeros((P, CTX)), band, np.zeros((P, CTX))], 1).astype(np.float32)
    s, t = np.arange(P)[:, None], np.arange(P)[None, :]
    g = np.zeros((P, 2, 7, P), np.float32)
    for lv in range(7):
        h = 1 << lv
        same = (s // (2 * h)) == (t // (2 * h))
        g[:, 0, lv] = same & ((s // h) % 2 == 0) & ((t // h) % 2 == 1)
        g[:, 1, lv] = same & ((s // h) % 2 == 1) & ((t // h) % 2 == 0)
    c["glamask"] = g
    return c


class Tally:

    def __init__(self, sem):
        self.sem, self.total = sem, 0

    def reserve(self, n):
        base = self.total
        self.total += n
        return base


class Chain:

    def __init__(self, eng, sem):
        self.eng, self.sem, self.n = eng, sem, 0

    def step(self, ins):
        ins.then_inc(self.sem, 1)
        self.n += 1

    def wait(self):
        if self.n:
            self.eng.wait_ge(self.sem, self.n)


class Banks:

    def __init__(self, k, owners, first=0, count=8, lane=0):
        self.k, self.owners, self.first, self.count = k, owners, first, count
        self.full_sem, self.taken_sems = k.lanes[lane]
        self.full = self.full_sem.reserve(len(owners))
        self.base = {e: self.taken_sems[e].reserve(sum(o == e for o in owners)) for e in ("act", "dve")}

    def bank(self, u):
        return self.k.ps[:, self.first + u % self.count, :]

    def may_fill(self, pe, u):
        if u >= self.count:
            self.taken(pe, u - self.count)

    def taken(self, eng, v):
        o = self.owners[v]
        eng.wait_ge(self.taken_sems[o].sem, self.base[o] + self.owners[:v + 1].count(o))

    def filled(self, ins):
        ins.then_inc(self.full_sem.sem, 1)

    def await_full(self, eng, u):
        eng.wait_ge(self.full_sem.sem, self.full + u + 1)

    def take(self, u, ins):
        ins.then_inc(self.taken_sems[self.owners[u]].sem, 1)


class K:
    pass


class Stage:

    def __init__(self, k):
        self.k = k

    def tensor(self, pe):
        pass

    def vector(self, dve, ch):
        pass

    def scalar(self, act, ch):
        pass

    def gpsimd(self, pool, ch):
        pass


def alternate(n):
    return ["act" if i % 2 else "dve" for i in range(n)]


class Ring:
    def __init__(self, k):
        self.k, self.loads, self.next = k, [], 0
        self.landed_at, self.count = [], [0] * SLOTS

    def plan(self, parts):
        r = len(self.loads) % SLOTS
        self.count[r] += 16 * len(parts)
        self.landed_at.append(self.count[r])
        self.loads.append(parts)
        return len(self.loads) - 1

    def slot(self, n):
        return self.k.ring[:, n % SLOTS, :]

    def await_landed(self, pe, n):
        pe.wait_ge(self.k.landed[n % SLOTS], self.landed_at[n])

    def released(self, ins):
        ins.then_inc(self.k.weights_used, 1)

    def fill(self, sp):
        for n, parts in enumerate(self.loads):
            if n >= SLOTS:
                sp.wait_ge(self.k.weights_used, n - SLOTS + 1)
            for place, src in parts:
                sp.dma_start(place(self.slot(n)), src).then_inc(self.k.landed[n % SLOTS], 16)


def plan_columns(k, w, k0, kn, c0, cn):
    src = w[k0 * P:(k0 + kn) * P, c0:c0 + cn].rearrange("(c p) n -> p c n", p=P)
    return k.rg.plan([(lambda s: s[:, 0:kn * cn].rearrange("p (c n) -> p c n", c=kn), src)])


class Linear(Stage):

    def __init__(self, k, lhs, nk, w, width, tiles, take, owners=None, rows=P):
        super().__init__(k)
        self.lhs, self.tiles, self.take_fn, self.nk, self.rows = lhs, tiles, take, nk, rows
        self.blocks = []
        for c0 in range(0, width, 512):
            cn = min(512, width - c0)
            slots = [(k0, min(4, nk - k0), plan_columns(k, w, k0, min(4, nk - k0), c0, cn)) for k0 in range(0, nk, 4)]
            self.blocks.append((c0, cn, slots))
        n = len(self.blocks) * len(tiles)
        self.banks = Banks(k, owners or alternate(n))

    def tensor(self, pe):
        k, u0 = self.k, 0
        for c0, cn, slots in self.blocks:
            for si, (k0, kn, n) in enumerate(slots):
                k.rg.await_landed(pe, n)
                w = k.rg.slot(n)[:, 0:kn * cn].rearrange("p (c n) -> p c n", c=kn)
                for i, t in enumerate(self.tiles):
                    if si == 0:
                        self.banks.may_fill(pe, u0 + i)
                    for c in range(kn):
                        last = pe.matmul(self.banks.bank(u0 + i)[0:self.rows, 0:cn], self.lhs(k0 + c, t), w[:, c, :],
                                         start=(k0 + c == 0), stop=(k0 + c == self.nk - 1))
                    if si == len(slots) - 1 and i < len(self.tiles) - 1:
                        self.banks.filled(last)
                if si == len(slots) - 1:
                    self.banks.filled(last)
                    pe.drain().then_inc(k.weights_used, 1)
                else:
                    k.rg.released(last)
            u0 += len(self.tiles)

    def _take(self, eng, name, ch):
        u = 0
        for c0, cn, _ in self.blocks:
            for t in self.tiles:
                if self.banks.owners[u] == name:
                    self.banks.await_full(eng, u)
                    self.banks.take(u, self.take_fn(eng, name, ch, t, c0, cn, self.banks.bank(u)[:, 0:cn]))
                u += 1

    def vector(self, dve, ch):
        self._take(dve, "dve", ch)

    def scalar(self, act, ch):
        self._take(act, "act", ch)


def copy(eng, name, out, src, scale=None):
    if name == "act":
        return eng.activation(out, src, ACT.Copy, scale=1.0 if scale is None else scale)
    if scale is None:
        return eng.tensor_copy(out, src)
    return eng.tensor_scalar(out, src, scale, None, ALU.mult)


class Norm(Stage):

    def __init__(self, k, sets):
        super().__init__(k)
        self.sets = sets
        self.tiles = [t for ts, _, _ in sets for t in ts]
        self.units = [(i, c) for i in range(len(sets)) for c in range(DK)]
        self.banks = Banks(k, alternate(len(self.units)))
        self.sq = k.norm_squares.reserve(len(self.tiles))
        self.rt = k.norm_roots.reserve(1)
        self.hn = k.norm_rows.reserve(len(self.tiles))

    def scalar(self, act, ch):
        k = self.k
        for i, t in enumerate(self.tiles):
            act.activation(k.HN[:, t, :], k.X[:, t, :], ACT.Square,
                           accum_out=k.ss[:, t:t + 1]).then_inc(k.norm_squares.sem, 1)
        act.wait_ge(k.norm_mean.sem, self.mean + 1)
        t0, t1 = self.tiles[0], self.tiles[-1] + 1
        act.activation(k.ss2[:, t0:t1], k.ss2[:, t0:t1], ACT.Sqrt).then_inc(k.norm_roots.sem, 1)
        self._take(act, "act")

    def vector(self, dve, ch):
        k = self.k
        t0, t1 = self.tiles[0], self.tiles[-1] + 1
        dve.wait_ge(k.norm_squares.sem, self.sq + len(self.tiles))
        dve.tensor_scalar(k.ss2[:, t0:t1], k.ss[:, t0:t1], 1.0 / D, EPS, ALU.mult, ALU.add).then_inc(k.norm_mean.sem, 1)
        dve.wait_ge(k.norm_roots.sem, self.rt + 1)
        ch.step(dve.reciprocal(k.rstd[:, t0:t1], k.ss2[:, t0:t1]))
        ch.wait()
        for i, t in enumerate(self.tiles):
            dve.tensor_scalar(k.HN[:, t, :], k.X[:, t, :], k.rstd[:, t:t + 1], None, ALU.mult).then_inc(k.norm_rows.sem, 1)
        self._take(dve, "dve")

    def tensor(self, pe):
        k = self.k
        for u, (i, c) in enumerate(self.units):
            ts = self.sets[i][0]
            if c == 0:
                pe.wait_ge(k.norm_rows.sem, self.hn + self.tiles.index(ts[-1]) + 1)
            self.banks.may_fill(pe, u)
            for j, t in enumerate(ts):
                last = pe.transpose(self.banks.bank(u)[:, j * P:(j + 1) * P], k.HN[:, t, c * P:(c + 1) * P], k.ident[:, :])
            self.banks.filled(last)

    def _take(self, eng, name):
        k = self.k
        for u, (i, c) in enumerate(self.units):
            if self.banks.owners[u] != name:
                continue
            ts, gain, shift = self.sets[i]
            out = k.HT[:, c, ts[0] * P:(ts[-1] + 1) * P]
            src = self.banks.bank(u)[:, 0:len(ts) * P]
            self.banks.await_full(eng, u)
            if name == "act":
                ins = eng.activation(out, src, ACT.Identity, scale=gain(c), bias=shift(c) if shift else 0.0)
            elif shift:
                ins = eng.tensor_scalar(out, src, gain(c), shift(c), ALU.mult, ALU.add)
            else:
                ins = eng.tensor_scalar(out, src, gain(c), None, ALU.mult)
            self.banks.take(u, ins)


def norm_stage(k, sets):
    s = Norm(k, sets)
    s.mean = k.norm_mean.reserve(1)
    return s


class Transposes(Stage):

    def __init__(self, k, units):
        super().__init__(k)
        self.units = units
        self.banks = Banks(k, alternate(len(units)))

    def tensor(self, pe):
        for u, (src, rows, tiles, dst, scale) in enumerate(self.units):
            self.banks.may_fill(pe, u)
            for j, t in enumerate(tiles):
                last = pe.transpose(self.banks.bank(u)[0:rows, j * P:(j + 1) * P], src(t), self.k.ident[:, :])
            self.banks.filled(last)

    def _take(self, eng, name):
        for u, (src, rows, tiles, dst, scale) in enumerate(self.units):
            if self.banks.owners[u] == name:
                self.banks.await_full(eng, u)
                self.banks.take(u, copy(eng, name, dst, self.banks.bank(u)[0:rows, 0:len(tiles) * P], scale))

    def vector(self, dve, ch):
        self._take(dve, "dve")

    def scalar(self, act, ch):
        self._take(act, "act")


class Attention(Stage):

    def __init__(self, k, jobs):
        super().__init__(k)
        self.jobs = jobs
        n = len(jobs)
        self.s_full = k.scores_full.reserve(n)
        self.s_top = k.scores_topped.reserve(n)
        self.p_done = k.probs_done.reserve(n)
        self.t_full = k.probsT_full.reserve(n)
        self.t_out = k.probsT_out.reserve(n)
        self.o_full = k.out_full.reserve(n)
        self.o_out = k.out_taken.reserve(n)
        for j in jobs:
            j["nk"] = sum(x[1] for x in j["keys"])

    def S(self, j):
        b = 2 * (j % 2)
        return self.k.ps[:, b:b + 2, :].rearrange("p a b -> p (a b)")

    def T(self, j):
        b = 4 + 2 * (j % 2)
        return self.k.ps[:, b:b + 2, :].rearrange("p a b -> p (a b)")

    def O(self, j):
        return self.k.ps[:, 5 + 2 * (j % 2), 320:320 + HD]

    def tensor(self, pe):
        k, jobs = self.k, self.jobs
        for i in range(len(jobs) + 2):
            if i < len(jobs):
                J = jobs[i]
                if i >= 2:
                    pe.wait_ge(k.probs_done.sem, self.p_done + i - 1)
                    pe.wait_ge(k.scores_topped.sem, self.s_top + i - 1)
                at = 0
                for kT, n in J["keys"]:
                    done = 0
                    while done < n:
                        m = min(n - done, 512 - at % 512)
                        last = pe.matmul(self.S(i)[:, at:at + m], J["q"], kT[:, done:done + m], start=True, stop=True)
                        done += m
                        at += m
                last.then_inc(k.scores_full.sem, 1)
            if 1 <= i <= len(jobs):
                j = i - 1
                J = jobs[j]
                pe.wait_ge(k.probs_done.sem, self.p_done + j + 1)
                if j >= 2:
                    pe.wait_ge(k.out_taken.sem, self.o_out + j - 1)
                at = 0
                for v, kn in J["values"]:
                    last = pe.transpose(self.T(j)[0:kn, at * P:(at + 1) * P], k.Pb[:, j % 2, at * P:at * P + kn], k.ident[:, :])
                    at += 1
                last.then_inc(k.probsT_full.sem, 1)
            if i >= 2:
                j = i - 2
                J = jobs[j]
                pe.wait_ge(k.probsT_out.sem, self.t_out + j + 1)
                for a, (v, kn) in enumerate(J["values"]):
                    last = pe.matmul(self.O(j), k.PT[0:kn, j % 2, a * P:(a + 1) * P], v,
                                     start=(a == 0), stop=(a == len(J["values"]) - 1))
                last.then_inc(k.out_full.sem, 1)

    def scalar(self, act, ch):
        k, jobs = self.k, self.jobs
        for i in range(len(jobs) + 1):
            if i < len(jobs):
                J = jobs[i]
                act.wait_ge(k.scores_topped.sem, self.s_top + i + 1)
                if i >= 2:
                    act.wait_ge(k.probsT_full.sem, self.t_full + i - 1)
                src = k.Pb[:, i % 2, 0:J["nk"]] if J["bias"] is not None else self.S(i)[:, 0:J["nk"]]
                if J["sink"] is not None:
                    ch.step(act.activation(k.es[:, i % 4:i % 4 + 1], J["sink"], ACT.Exp, bias=k.nm[:, i % 4:i % 4 + 1]))
                act.activation(k.Pb[:, i % 2, 0:J["nk"]], src, ACT.Exp, bias=k.nm[:, i % 4:i % 4 + 1],
                               accum_out=k.den[:, i % 4:i % 4 + 1]).then_inc(k.probs_done.sem, 1)
            if i >= 1:
                j = i - 1
                J = jobs[j]
                act.wait_ge(k.probsT_full.sem, self.t_full + j + 1)
                if j >= 2:
                    act.wait_ge(k.out_full.sem, self.o_full + j - 1)
                kn = J["values"][0][1]
                n = P * len(J["values"])
                act.activation(k.PT[0:kn, j % 2, 0:n], self.T(j)[0:kn, 0:n], ACT.Copy).then_inc(k.probsT_out.sem, 1)

    def vector(self, dve, ch):
        k, jobs = self.k, self.jobs
        for i in range(len(jobs) + 2):
            if i < len(jobs):
                J = jobs[i]
                c = slice(i % 4, i % 4 + 1)
                if J.get("load"):
                    dve.wait_ge(*J["load"])
                dve.wait_ge(k.scores_full.sem, self.s_full + i + 1)
                if i >= 2:
                    dve.wait_ge(k.probsT_full.sem, self.t_full + i - 1)
                if J["bias"] is not None:
                    ins = dve.tensor_tensor_reduce(out=k.Pb[:, i % 2, 0:J["nk"]], in0=self.S(i)[:, 0:J["nk"]],
                                                   in1=J["bias"], scale=1.0, scalar=-3e38, op0=ALU.add, op1=ALU.max,
                                                   accum_out=k.mx[:, c])
                else:
                    ins = dve.tensor_reduce(k.mx[:, c], self.S(i)[:, 0:J["nk"]], AXX, ALU.max)
                ch.step(ins)
                ch.wait()
                if J["sink"] is not None:
                    ins = dve.tensor_scalar(k.nm[:, c], k.mx[:, c], J["sink"], -1.0, ALU.max, ALU.mult)
                else:
                    ins = dve.tensor_scalar(k.nm[:, c], k.mx[:, c], -1.0, None, ALU.mult)
                ins.then_inc(k.scores_topped.sem, 1)
                if J.get("frees"):
                    ch.step(dve.tensor_copy(k.mx[:, c], k.mx[:, c]))
                    dve.drain().then_inc(k.bias_used.sem, 1)
            if 1 <= i <= len(jobs):
                j = i - 1
                J = jobs[j]
                c = slice(j % 4, j % 4 + 1)
                dve.wait_ge(k.probs_done.sem, self.p_done + j + 1)
                if J["sink"] is not None:
                    ch.step(dve.tensor_tensor(k.den[:, c], k.den[:, c], k.es[:, c], ALU.add))
                    ch.wait()
                ch.step(dve.reciprocal(k.rd[:, c], k.den[:, c]))
                if J["gate"] is not None:
                    ch.wait()
                    ch.step(dve.tensor_tensor(k.rd[:, c], k.rd[:, c], J["gate"], ALU.mult))
            if i >= 2:
                j = i - 2
                J = jobs[j]
                c = slice(j % 4, j % 4 + 1)
                dve.wait_ge(k.out_full.sem, self.o_full + j + 1)
                ch.wait()
                if J["first"]:
                    ins = dve.tensor_scalar(J["out"], self.O(j), k.rd[:, c], None, ALU.mult)
                else:
                    dve.wait_ge(k.out_taken.sem, self.o_out + j)
                    ins = dve.scalar_tensor_tensor(J["out"], self.O(j), k.rd[:, c], J["out"], ALU.mult, ALU.add)
                ins.then_inc(k.out_taken.sem, 1)


class Load(Stage):

    def __init__(self, k, pairs):
        super().__init__(k)
        self.pairs = pairs
        self.base = k.small_landed.reserve(16 * len(pairs))

    def gpsimd(self, pool, ch):
        for dst, src in self.pairs:
            pool.dma_start(dst, src).then_inc(self.k.small_landed.sem, 16)
        pool.wait_ge(self.k.small_landed.sem, self.base + 16 * len(self.pairs))


class ModVectors(Stage):

    def __init__(self, k, A):
        super().__init__(k)
        self.silu = k.step_done.reserve(1)
        self.rows = k.Z[0:2, 0:2 * 6144].rearrange("p (l n) -> p l n", l=2)
        self.layers = []
        for l in range(2):
            self.layers.append(Linear(k, lambda c, t: k.sc[:, c, :], DK, A["mod_w_2"][l], 6144, [0],
                                      self.take(l), owners=["dve"] * 12, rows=2))

    def take(self, l):
        k = self.k

        def fn(eng, name, ch, t, c0, cn, ps):
            return eng.tensor_tensor(self.rows[:, l, c0:c0 + cn], ps[0:2, :], k.modb(l)[:, c0:c0 + cn], ALU.add)
        return fn

    def scalar(self, act, ch):
        k = self.k
        act.activation(k.sc[:, :, :], k.cc[:, :, :], ACT.Silu).then_inc(k.step_done.sem, 1)

    def tensor(self, pe):
        pe.wait_ge(self.k.step_done.sem, self.silu + 1)
        self.layers[0].tensor(pe)
        self.layers[0].banks.taken(pe, 11)
        self.layers[1].tensor(pe)

    def vector(self, dve, ch):
        for d in range(2):
            dve.tensor_copy(self.k.glamask[:, d], self.k.maskf[:, d])
        for lin in self.layers:
            lin.vector(dve, ch)


class ModColumns(Stage):

    def __init__(self, k, rows, dram):
        super().__init__(k)
        self.rows, self.dram = rows, dram
        self.stored = k.small_landed.reserve(32)
        self.banks = Banks(k, ["dve", "dve"])
        self.n = 48

    def tensor(self, pe):
        for l in range(2):
            for c in range(self.n):
                last = pe.transpose(self.banks.bank(l)[:, 2 * c:2 * c + 2], self.rows[:, l, c * P:(c + 1) * P],
                                    self.k.ident[0:2, 0:2])
            self.banks.filled(last)

    def vector(self, dve, ch):
        k = self.k
        for l in range(2):
            self.banks.await_full(dve, l)
            ins = dve.tensor_copy(k.mc[:, l, :, :].rearrange("p n r -> p (n r)"), self.banks.bank(l)[:, 0:2 * self.n])
            self.banks.take(l, ins)
            self.banks.taken(dve, l)
            for w, m in ((0, 1), (1, 4)):
                for r in range(2):
                    dve.scalar_tensor_tensor(k.mg[:, l, w, r, :], k.mc[:, l, m * DK:(m + 1) * DK, r], 1.0,
                                             k.gains[:, 2 + 2 * w + l, :], ALU.add, ALU.mult)

    def gpsimd(self, pool, ch):
        k = self.k
        for l in range(2):
            pool.dma_start(self.dram[l], self.rows[:, l, :]).then_inc(k.small_landed.sem, 16)
        pool.wait_ge(k.small_landed.sem, self.stored + 32)


class BiasRows(Stage):

    def __init__(self, k, table, hot, dram, spread):
        super().__init__(k)
        self.table, self.hot, self.dram, self.spread = table, hot, dram, spread
        self.banks = Banks(k, ["dve"] * 4)
        self.stored = k.small_landed.reserve(16)
        self.units = [(s, c0, min(512, ROW - c0)) for s in range(2) for c0 in (0, 512)]

    def tensor(self, pe):
        for u, (s, c0, cn) in enumerate(self.units):
            self.banks.filled(pe.matmul(self.banks.bank(u)[0:8, 0:cn], self.table[:, 8 * s:8 * s + 8],
                                        self.hot[:, s, c0:c0 + cn], start=True, stop=True))

    def vector(self, dve, ch):
        for u, (s, c0, cn) in enumerate(self.units):
            self.banks.await_full(dve, u)
            self.banks.take(u, dve.tensor_copy(self.buf[:, s, c0:c0 + cn], self.banks.bank(u)[0:8, 0:cn]))

    def gpsimd(self, pool, ch):
        self.banks.taken(pool, 3)
        pool.dma_start(self.dram.rearrange("(a h) n -> h a n", a=2), self.buf).then_inc(self.k.small_landed.sem, 16)
        pool.wait_ge(self.k.small_landed.sem, self.stored + 16)
        rows = bass.AP(tensor=self.dram.tensor, offset=self.dram.offset, ap=[[ROW, 16], [0, P], [1, ROW]])
        pool.dma_start(self.spread, rows).then_inc(self.k.bias_spread, 16)


class Compress(Stage):

    def __init__(self, k, A, kraw, vraw):
        super().__init__(k)
        self.raw = [kraw, vraw]
        self.slots = []
        for w1 in (A["cmp_k_w1"][0], A["cmp_v_w1"][0]):
            for l0 in (0, 16):
                src = w1[l0:l0 + 16].rearrange("l d h -> d l h")
                parts = [((lambda s, g=g: s[64 * g:64 * g + 64, :].rearrange("p (l h) -> p l h", l=16)), src) for g in range(2)]
                self.slots.append(k.rg.plan(parts))
        self.blk_ready = k.step_done.reserve(2)
        self.hid_full = k.psum_full.reserve(2)
        self.hid_done = k.gates_done.reserve(2)
        self.kc_full = k.psum_full.reserve(2)
        self.blk = [k.cmpblk(i) for i in range(2)]
        self.hid = k.cmphid

    def tensor(self, pe):
        k = self.k
        for i in range(2):
            pe.wait_ge(k.step_done.sem, self.blk_ready + i + 1)
            for half in range(2):
                n = self.slots[2 * i + half]
                k.rg.await_landed(pe, n)
                w = k.rg.slot(n).rearrange("p (l h) -> p l h", l=16)
                for l in range(16):
                    for g in range(2):
                        ll = 16 * half + l
                        last = pe.matmul(k.ps[:, 2 * i + g, 0:NCMP], w[64 * g:64 * g + 64, l, :],
                                         self.blk[i][64 * g:64 * g + 64, :, ll], start=(ll == 0), stop=(ll == 31))
                k.rg.released(last)
            pe.drain().then_inc(k.psum_full.sem, 1)
        pe.wait_ge(k.gates_done.sem, self.hid_done + 2)
        for g in range(2):
            last = pe.matmul(k.ps[64 * g:64 * g + 64, 4, 0:NCMP], k.w2[:, 0, :], self.hid[:, 0, g * NCMP:(g + 1) * NCMP],
                             start=True, stop=True)
        last.then_inc(k.psum_full.sem, 1)
        for g in range(2):
            last = pe.matmul(k.ps[0:NCMP, 5, g * HD:(g + 1) * HD], self.hid[:, 1, g * NCMP:(g + 1) * NCMP], k.w2[:, 1, :],
                             start=True, stop=True)
        last.then_inc(k.psum_full.sem, 1)

    def vector(self, dve, ch):
        k = self.k
        for i in range(2):
            c16 = self.raw[i].rearrange("p (c l) -> p c l", l=CMP_STRIDE)
            pos = k.posT[:, :].unsqueeze(1)
            dve.tensor_tensor(self.blk[i][:, :, 0:16], c16[:, 0:NCMP, :], pos[:, :, 0:16].to_broadcast((P, NCMP, 16)), ALU.add)
            dve.tensor_tensor(self.blk[i][:, :, 16:32], c16[:, 1:NCMP + 1, :], pos[:, :, 16:32].to_broadcast((P, NCMP, 16)), ALU.add)
            dve.drain().then_inc(k.step_done.sem, 1)
        dve.wait_ge(k.psum_full.sem, self.kc_full + 1)
        dve.tensor_copy(k.kcmp[:, :], k.ps[:, 4, 0:NCMP])
        dve.wait_ge(k.psum_full.sem, self.kc_full + 2)
        dve.tensor_copy(k.vcmp[0:NCMP, :], k.ps[0:NCMP, 5, 0:2 * HD])

    def scalar(self, act, ch):
        k = self.k
        for i in range(2):
            act.wait_ge(k.psum_full.sem, self.hid_full + i + 1)
            for g in range(2):
                act.activation(self.hid[:, i, g * NCMP:(g + 1) * NCMP], k.ps[:, 2 * i + g, 0:NCMP],
                               ACT.Gelu_apprx_tanh, bias=k.b1[:, i:i + 1])
            act.drain().then_inc(k.gates_done.sem, 1)


class Bias(Stage):

    def __init__(self, k, jobs_of, heads, dram):
        super().__init__(k)
        self.heads, self.dram = heads, dram
        self.landed = k.bias_landed.reserve(16 * len(heads))
        self.used = k.bias_used.reserve(len(heads))
        jobs = []
        for i, h in enumerate(heads):
            js = jobs_of(h, k.bias[:, i % 2, :])
            js[0]["load"] = (k.bias_landed.sem, self.landed + 16 * (i + 1))
            js[-1]["frees"] = True
            jobs += js
        self.att = Attention(k, jobs)

    def gpsimd(self, pool, ch):
        k = self.k
        pool.wait_ge(k.bias_spread, 16)
        for i, h in enumerate(self.heads):
            if i >= 2:
                pool.wait_ge(k.bias_used.sem, self.used + i - 1)
            src = bass.AP(tensor=self.dram.tensor, offset=self.dram.offset + h * P * ROW + 127, ap=[[ROW - 1, P], [1, 512]])
            pool.dma_start(k.bias[:, i % 2, :], src).then_inc(k.bias_landed.sem, 16)
            pool.wait_ge(k.bias_landed.sem, self.landed + 16 * (i + 1))

    def tensor(self, pe):
        self.att.tensor(pe)

    def vector(self, dve, ch):
        self.att.vector(dve, ch)

    def scalar(self, act, ch):
        self.att.scalar(act, ch)


class Sigmoids(Stage):

    def __init__(self, k):
        super().__init__(k)
        self.done = k.step_done.reserve(1)

    def scalar(self, act, ch):
        k = self.k
        act.activation(k.gate3[:, :, :], k.Zb(IN_W)[:, :, GL:GL + 24], ACT.Sigmoid).then_inc(k.step_done.sem, 1)

    def vector(self, dve, ch):
        k = self.k
        dve.wait_ge(k.step_done.sem, self.done + 1)
        g = k.gate3[:, :, :].rearrange("p t (h b) -> p t h b", b=3)[:, :, :, 0]
        v = k.cmpvalid[:, :].unsqueeze(2).to_broadcast((P, ST, 8))
        dve.tensor_tensor(g, g, v, ALU.mult)


class HeadNorm(Stage):

    def __init__(self, k, zw, parts):
        super().__init__(k)
        self.zw, self.parts = zw, parts
        self.asked = k.norm_mean.reserve(len(parts))
        self.got = k.norm_roots.reserve(len(parts))

    def scalar(self, act, ch):
        k = self.k
        for i, (tiles, c0, heads, groups) in enumerate(self.parts):
            act.wait_ge(k.norm_mean.sem, self.asked + i + 1)
            n = len(tiles) * heads
            act.activation(k.hstat[:, 0:n], k.hstat[:, 0:n], ACT.Sqrt).then_inc(k.norm_roots.sem, 1)

    def vector(self, dve, ch):
        k = self.k
        z = k.Zb(self.zw)
        for i, (tiles, c0, heads, groups) in enumerate(self.parts):
            n = len(tiles) * heads
            ch.wait()
            for a, t in enumerate(tiles):
                x = z[:, t, c0:c0 + heads * HD]
                ch.step(dve.tensor_tensor(k.tmp[:, 0:heads * HD], x, x, ALU.mult))
                ch.wait()
                ch.step(dve.tensor_reduce(k.hstat[:, a * heads:(a + 1) * heads],
                                          k.tmp[:, 0:heads * HD].rearrange("p (h d) -> p h d", d=HD), AXX, ALU.add))
                ch.wait()
            dve.tensor_scalar(k.hstat[:, 0:n], k.hstat[:, 0:n], 1.0 / HD, EPS, ALU.mult, ALU.add).then_inc(k.norm_mean.sem, 1)
            dve.wait_ge(k.norm_roots.sem, self.got + i + 1)
            ch.step(dve.reciprocal(k.hstat[:, 0:n], k.hstat[:, 0:n]))
            ch.wait()
            for a, t in enumerate(tiles):
                x = z[:, t, c0:c0 + heads * HD].rearrange("p (h d) -> p h d", d=HD)
                r = k.hstat[:, a * heads:(a + 1) * heads].unsqueeze(2).to_broadcast((P, heads, HD))
                ch.step(dve.tensor_tensor(x, x, r, ALU.mult))
                ch.wait()
                h0 = 0
                for hn, gain in groups:
                    xs = x[:, h0:h0 + hn, :]
                    ch.step(dve.tensor_tensor(xs, xs, gain.unsqueeze(1).to_broadcast((P, hn, HD)), ALU.mult))
                    h0 += hn
                ch.wait()
                if t >= ST:
                    continue
                a2 = k.tmp[:, 0:heads * HD].rearrange("p (h d) -> p h d", d=HD)
                b2 = k.tmp[:, 1152:1152 + heads * HD].rearrange("p (h d) -> p h d", d=HD)
                ch.step(dve.tensor_tensor(a2, x, k.rope[:, t, 0, :].unsqueeze(1).to_broadcast((P, heads, HD)), ALU.mult))
                for ax in range(2):
                    for hf in range(2):
                        o = 32 * ax + 16 * hf
                        s = 32 * ax + 16 * (1 - hf)
                        ch.step(dve.tensor_tensor(b2[:, :, o:o + 16], x[:, :, s:s + 16],
                                                  k.rope[:, t, 1, o:o + 16].unsqueeze(1).to_broadcast((P, heads, 16)), ALU.mult))
                ch.wait()
                ch.step(dve.tensor_tensor(x, a2, b2, ALU.add))
                ch.wait()


class RowNorm(Stage):

    def __init__(self, k, tiles, gain):
        super().__init__(k)
        self.tiles, self.gain = tiles, gain
        self.sq = k.norm_squares.reserve(len(tiles))
        self.mean = k.norm_mean.reserve(1)
        self.rt = k.norm_roots.reserve(1)

    def scalar(self, act, ch):
        k = self.k
        for t in self.tiles:
            act.activation(k.HN[:, t, :], k.X[:, t, :], ACT.Square,
                           accum_out=k.ss[:, t:t + 1]).then_inc(k.norm_squares.sem, 1)
        act.wait_ge(k.norm_mean.sem, self.mean + 1)
        n = len(self.tiles)
        act.activation(k.ss2[:, 0:n], k.ss2[:, 0:n], ACT.Sqrt).then_inc(k.norm_roots.sem, 1)

    def vector(self, dve, ch):
        k = self.k
        n = len(self.tiles)
        dve.wait_ge(k.norm_squares.sem, self.sq + n)
        dve.tensor_scalar(k.ss2[:, 0:n], k.ss[:, 0:n], 1.0 / D, EPS, ALU.mult, ALU.add).then_inc(k.norm_mean.sem, 1)
        dve.wait_ge(k.norm_roots.sem, self.rt + 1)
        ch.step(dve.reciprocal(k.rstd[:, 0:n], k.ss2[:, 0:n]))
        ch.wait()
        for t in self.tiles:
            dve.scalar_tensor_tensor(k.X[:, t, :], k.X[:, t, :], k.rstd[:, t:t + 1], self.gain, ALU.mult, ALU.mult)


class GlaGates(Stage):

    def __init__(self, k):
        super().__init__(k)
        self.units = [(d, p, t0, n) for d in range(2) for p in range(2) for t0, n in ((0, SEQ), (SEQ, CTX))]
        self.banks = Banks(k, ["dve"] * 8)
        self.s = k.step_done.reserve(2)

    def tensor(self, pe):
        k = self.k
        for u, (d, p, t0, n) in enumerate(self.units):
            self.banks.filled(pe.matmul(self.banks.bank(u)[:, 0:n], k.gw[:, d, p * P:(p + 1) * P],
                                        k.lrT[:, t0:t0 + n], start=True, stop=True))

    def scalar(self, act, ch):
        k = self.k
        act.wait_ge(k.step_done.sem, self.s + 1)
        for d in range(2):
            e, z = k.gA if d == 0 else k.gB, k.gb[:, d]
            ch.step(act.activation(e, z, ACT.Abs))
            ch.wait()
            ch.step(act.activation(e, e, ACT.Exp, scale=-1.0))
            ch.wait()
            ch.step(act.activation(e, e, ACT.Ln, bias=1.0))
        ch.wait()
        act.drain().then_inc(k.step_done.sem, 1)

    def vector(self, dve, ch):
        k = self.k
        ch.step(dve.memset(k.gC[:, :, :], 1.0))
        ch.wait()
        ch.step(dve.memset(k.gC.rearrange("p a (n t) -> p (a n) t", t=P)[:, :, 0:1], 0.0))
        for u, (d, p, t0, n) in enumerate(self.units):
            self.banks.await_full(dve, u)
            self.banks.take(u, dve.tensor_scalar(k.gb[:, d, p, t0:t0 + n], self.banks.bank(u)[:, 0:n],
                                                 k.gateb[:, 2 * d + p:2 * d + p + 1], None, ALU.add))
        dve.drain().then_inc(k.step_done.sem, 1)
        dve.wait_ge(k.step_done.sem, self.s + 2)
        for d in range(2):
            e, z = (k.gA, k.gB)[d], k.gb[:, d]
            ch.step(dve.scalar_tensor_tensor(z, z, 0.0, e, ALU.min, ALU.subtract))
            ch.wait()
            ch.step(dve.tensor_scalar(z, z, 1.0 / 16.0, None, ALU.mult))
            ch.wait()
            flat = lambda a: a.rearrange("p a n -> p (a n)")
            ch.step(dve.tensor_tensor_scan(flat(e), flat(k.gC), flat(z), 0.0, ALU.mult, ALU.add))
            ch.wait()
            if d == 0:
                ch.step(dve.tensor_copy(z, e))
            else:
                ch.step(dve.tensor_tensor(z, z, e, ALU.subtract))
                ch.wait()
                zt = z.rearrange("p a (n t) -> p (a n) t", t=P)
                et = e.rearrange("p a (n t) -> p (a n) t", t=P)[:, :, P - 1:P].to_broadcast((P, 12, P))
                ch.step(dve.tensor_tensor(zt, zt, et, ALU.add))
            ch.wait()


class GlaScores(Stage):

    def __init__(self, k, d):
        super().__init__(k)
        self.d = d
        self.banks = Banks(k, ["dve"] * 48)
        self.diff = k.gla_diff.reserve(7)
        self.exp = k.gla_exp.reserve(7)
        self.kpart = k.gla_k.reserve(7)
        self.qk = k.gla_qk.reserve(7)

    def half(self, x, h, side):
        return x.rearrange("p a (n s t) -> p (a n) s t", s=2, t=h)[:, :, side, :]

    def tensor(self, pe):
        k = self.k
        for lv in range(-1, 7):
            if lv >= 0:
                pe.wait_ge(k.gla_qk.sem, self.qk + lv + 1)
                pe.wait_ge(k.gla_k.sem, self.kpart + lv + 1)
            for v in range(NT):
                u, odd = (lv + 1) * NT + v, v % 2
                self.banks.may_fill(pe, u)
                for j in range(4):
                    r, p, t = slice(64 * odd, 64 * odd + 64), j % 2, 2 * (v // 2) + j // 2
                    c = slice(t * P, (t + 1) * P)
                    if lv < 0:
                        a, b = k.gkT[r, p, c], k.gqT[r, p, c]
                    else:
                        x = (k.gB, k.gC)[lv % 2]
                        a = b = x[r, p, c]
                    last = pe.matmul(self.banks.bank(u)[:, j * P:(j + 1) * P], a, b, start=True, stop=True)
                self.banks.filled(last)

    def scalar(self, act, ch):
        k = self.k
        for lv in range(7):
            act.wait_ge(k.gla_diff.sem, self.diff + lv + 1)
            act.activation(k.gA, k.gA, ACT.Exp).then_inc(k.gla_exp.sem, 1)

    def gpsimd(self, pool, ch):
        k = self.k
        s_side = self.d
        for lv in range(7):
            h = 1 << lv
            pool.wait_ge(k.gla_exp.sem, self.exp + lv + 1)
            if lv >= 2:
                self.banks.taken(pool, (lv - 1) * NT + NT - 1)
            x = (k.gB, k.gC)[lv % 2]
            pool.tensor_tensor(self.half(x, h, s_side), self.half(k.gkT, h, s_side), self.half(k.gA, h, s_side),
                               ALU.mult).then_inc(k.gla_k.sem, 1)

    def vector(self, dve, ch):
        k, d = self.k, self.d
        b = k.gb[:, d]
        t_side, s_side = 1 - d, d

        def prepare(lv):
            h = 1 << lv
            if lv >= 1:
                dve.wait_ge(k.gla_k.sem, self.kpart + lv)
            seam = self.half(b, h, s_side)[:, :, h - 1:h] if d == 0 else self.half(b, h, s_side)[:, :, 0:1]
            seam = seam.to_broadcast((P, 2 * NT * P // (2 * h), h))
            ch.wait()
            dve.tensor_tensor(self.half(k.gA, h, t_side), self.half(b, h, t_side), seam, ALU.subtract)
            dve.tensor_tensor(self.half(k.gA, h, s_side), seam, self.half(b, h, s_side), ALU.subtract)
            dve.drain().then_inc(k.gla_diff.sem, 1)
            dve.wait_ge(k.gla_exp.sem, self.exp + lv + 1)
            x = (k.gB, k.gC)[lv % 2]
            if lv >= 2:
                dve.wait_ge(k.psum_full.sem, self.banks.full + lv * NT)
            ch.step(dve.tensor_tensor(self.half(x, h, t_side), self.half(k.gqT, h, t_side), self.half(k.gA, h, t_side), ALU.mult))
            ch.wait()
            dve.drain().then_inc(k.gla_qk.sem, 1)

        prepare(0)
        for lv in range(-1, 7):
            if 0 <= lv < 6:
                prepare(lv + 1)
            for v in range(NT):
                u = (lv + 1) * NT + v
                self.banks.await_full(dve, u)
                for a in range(2):
                    ps = self.banks.bank(u)[:, 256 * a:256 * a + 256].rearrange("p (h t) -> p h t", h=2)
                    acc = k.gacc[:, 2 * (v // 2) + a, v % 2]
                    if lv < 0:
                        ins = dve.tensor_tensor(acc, ps, k.ident[:, :].unsqueeze(1).to_broadcast((P, 2, P)), ALU.mult)
                        continue
                    if v == 0 and a == 0:
                        self.banks.taken(dve, u - 1)
                    ins = dve.copy_predicated(acc, k.glamask[:, d, lv, :].unsqueeze(1).to_broadcast((P, 2, P)), ps)
                self.banks.take(u, dve.drain())


class GlaDecayed(Stage):

    def __init__(self, k, d):
        super().__init__(k)
        self.d = d
        self.s1 = k.gla_diff.reserve(1)
        self.s2 = k.gla_exp.reserve(2)
        self.s3 = k.gla_qk.reserve(2)
        self.banks = Banks(k, alternate(2 * NT))

    def scalar(self, act, ch):
        k, d = self.k, self.d
        act.activation(k.gA, k.gb[:, d], ACT.Exp).then_inc(k.gla_exp.sem, 1)
        act.wait_ge(k.gla_diff.sem, self.s1 + 1)
        act.activation(k.gC, k.gC, ACT.Exp).then_inc(k.gla_exp.sem, 1)
        act.wait_ge(k.gla_qk.sem, self.s3 + 2)
        self._take(act, "act")

    def vector(self, dve, ch):
        k, d = self.k, self.d
        b = k.gb[:, d]
        bt = b.rearrange("p a (n t) -> p (a n) t", t=P)
        end = bt[:, :, P - 1:P] if d == 0 else bt[:, :, 0:1]
        ct = k.gC.rearrange("p a (n t) -> p (a n) t", t=P)
        dve.tensor_tensor(ct, end.to_broadcast((P, 12, P)), bt, ALU.subtract).then_inc(k.gla_diff.sem, 1)
        dve.wait_ge(k.gla_exp.sem, self.s2 + 1)
        at = k.gA.rearrange("p a (n t) -> p (a n) t", t=P)
        dve.tensor_copy(k.gdecay[:, :].unsqueeze(2), at[:, :, P - 1:P] if d == 0 else at[:, :, 0:1])
        dve.tensor_tensor(k.gB, k.gqT, k.gA, ALU.mult)
        dve.wait_ge(k.gla_exp.sem, self.s2 + 2)
        dve.tensor_tensor(k.gC, k.gkT, k.gC, ALU.mult)
        dve.drain().then_inc(k.gla_qk.sem, 2)
        dve.wait_ge(k.gla_qk.sem, self.s3 + 2)
        self._take(dve, "dve")

    def tensor(self, pe):
        k = self.k
        pe.wait_ge(k.gla_qk.sem, self.s3 + 2)
        for u in range(2 * NT):
            t, p = u // 2, u % 2
            self.banks.may_fill(pe, u)
            self.banks.filled(pe.transpose(self.banks.bank(u)[:, 0:P], k.gC[:, p, t * P:(t + 1) * P], k.ident[:, :]))

    def _take(self, eng, name):
        for u in range(2 * NT):
            t, p = u // 2, u % 2
            if self.banks.owners[u] == name:
                self.banks.await_full(eng, u)
                self.banks.take(u, copy(eng, name, self.k.gkh[:, t, p, :], self.banks.bank(u)[:, 0:P]))


class GlaScan(Stage):

    def __init__(self, k, d):
        super().__init__(k)
        self.d = d
        self.order = [4, 5, 0, 1, 2, 3] if d == 0 else [5, 4, 3, 2, 1, 0]
        self.o = Banks(k, ["dve"] * (2 * NT), 4, 4, lane=1)
        self.s = Banks(k, ["dve"] * NT, 2, 2)

    def tensor(self, pe):
        k = self.k
        z = k.Zb(EV_W)
        for i, t in enumerate(self.order):
            v = lambda h: z[:, t, GV + h * GDV:GV + (h + 1) * GDV]
            self.s.may_fill(pe, i)
            for h in range(GH):
                r = 64 * (h % 2)
                last = pe.matmul(self.s.bank(i)[r:r + 64, (h // 2) * P:(h // 2) * P + GDV],
                                 k.gkh[:, t, h // 2, r:r + 64], v(h), start=True, stop=True)
            self.s.filled(last)
            if i:
                self.s.taken(pe, i - 1)
            for odd in range(2):
                self.o.may_fill(pe, 2 * i + odd)
                for p in range(2):
                    r = slice(64 * odd, 64 * odd + 64)
                    out = self.o.bank(2 * i + odd)[:, p * GDV:(p + 1) * GDV]
                    last = pe.matmul(out, k.gacc[:, t, odd, p, :], v(2 * p + odd), start=True, stop=(i == 0))
                    if i:
                        last = pe.matmul(out, k.gB[r, p, t * P:(t + 1) * P], k.gS[r, (i - 1) % 2, p, :],
                                         start=False, stop=True)
                self.o.filled(last)

    def vector(self, dve, ch):
        k = self.k

        def outputs(i):
            t = self.order[i]
            for odd in range(2):
                self.o.await_full(dve, 2 * i + odd)
                to = k.gO[:, t, :].rearrange("p (a o n) -> p a o n", a=2, o=2)[:, :, odd, :]
                new = self.o.bank(2 * i + odd)[:, 0:2 * GDV].rearrange("p (a n) -> p a n", a=2)
                if self.d == 0:
                    ins = dve.tensor_copy(to, new)
                else:
                    ins = dve.tensor_tensor(to, new, to, ALU.add)
                self.o.take(2 * i + odd, ins)

        for i, t in enumerate(self.order):
            if i:
                outputs(i - 1)
                self.s.taken(dve, i - 1)
            self.s.await_full(dve, i)
            for p in range(2):
                new = self.s.bank(i)[:, p * P:(p + 1) * P]
                if i == 0:
                    dve.tensor_copy(k.gS[:, 0, p, :], new)
                else:
                    dve.scalar_tensor_tensor(k.gS[:, i % 2, p, :], k.gS[:, (i - 1) % 2, p, :],
                                             k.gdecay[:, p * NT + t:p * NT + t + 1], new, ALU.mult, ALU.add)
            self.s.take(i, dve.drain())
        outputs(NT - 1)


class GlaOutput(Stage):

    def __init__(self, k):
        super().__init__(k)
        self.s = k.step_done.reserve(2)
        self.r = k.norm_roots.reserve(1)

    def scalar(self, act, ch):
        k = self.k
        z = k.Zb(EV_W)
        act.activation(z[:, :, GR:GR + 512], z[:, :, GR:GR + 512], ACT.Silu).then_inc(k.step_done.sem, 1)
        act.wait_ge(k.step_done.sem, self.s + 2)
        act.activation(k.hstat[:, 0:NT * GH], k.hstat[:, 0:NT * GH], ACT.Sqrt).then_inc(k.norm_roots.sem, 1)

    def vector(self, dve, ch):
        k = self.k
        z = k.Zb(EV_W)
        n = NT * GH
        o = k.gO.rearrange("p t (h d) -> p (t h) d", d=GDV)
        sq = k.T[:, 0:n * GDV].rearrange("p (n d) -> p n d", d=GDV)
        st = k.hstat[:, 0:n]
        ch.step(dve.tensor_tensor(sq, o, o, ALU.mult))
        ch.wait()
        ch.step(dve.tensor_reduce(st, sq, AXX, ALU.add))
        ch.wait()
        ch.step(dve.tensor_scalar(st, st, 1.0 / GDV, EPS, ALU.mult, ALU.add))
        ch.wait()
        dve.wait_ge(k.step_done.sem, self.s + 1)
        dve.drain().then_inc(k.step_done.sem, 1)
        dve.wait_ge(k.norm_roots.sem, self.r + 1)
        ch.step(dve.reciprocal(st, st))
        ch.wait()
        ch.step(dve.tensor_tensor(o, o, st.unsqueeze(2).to_broadcast((P, n, GDV)), ALU.mult))
        ch.wait()
        ch.step(dve.tensor_tensor(o, o, k.ggain[:, :].unsqueeze(1).to_broadcast((P, n, GDV)), ALU.mult))
        ch.wait()
        dve.tensor_tensor(z[:, :, 0:512], k.gO, z[:, :, GR:GR + 512], ALU.mult)


class Router(Stage):

    def __init__(self, k, l, tiles):
        super().__init__(k)
        self.l, self.tiles = l, tiles
        self.banks = Banks(k, ["dve"] * len(tiles))
        self.e = k.step_done.reserve(4)

    def tensor(self, pe):
        k = self.k
        for u, t in enumerate(self.tiles):
            for c in range(DK):
                last = pe.matmul(self.banks.bank(u)[:, 0:20], k.HT[:, c, t * P:(t + 1) * P], k.rw[:, self.l, c, :],
                                 start=(c == 0), stop=(c == DK - 1))
            self.banks.filled(last)

    def scalar(self, act, ch):
        k, n = self.k, len(self.tiles)
        for i in range(2):
            act.wait_ge(k.step_done.sem, self.e + 2 * i + 1)
            x = k.rG[:, 0:n, :] if i == 0 else k.rE[:, 0:n, :]
            act.activation(x, x, ACT.Exp).then_inc(k.step_done.sem, 1)

    def vector(self, dve, ch):
        k, n = self.k, len(self.tiles)

        def do(ins):
            ch.step(ins)
            ch.wait()

        for u, t in enumerate(self.tiles):
            self.banks.await_full(dve, u)
            self.banks.take(u, dve.tensor_tensor(k.rL[:, u, :], self.banks.bank(u)[:, 0:20], k.rb[:, self.l, :], ALU.add))
            self.banks.taken(dve, u)
        m, left = k.rs[:, 0, 0:n], k.rs[:, 2, 0:n]

        def over4(x):
            return x.unsqueeze(2).to_broadcast((P, n, 4))

        def first_max(x, onehot):
            do(dve.tensor_reduce(m, x, AXX, ALU.max))
            do(dve.tensor_tensor(onehot, x, over4(m), ALU.is_equal))
            do(dve.memset(left, 1.0))
            for j in range(4):
                do(dve.tensor_tensor(onehot[:, :, j], onehot[:, :, j], left, ALU.mult))
                do(dve.tensor_tensor(left, left, onehot[:, :, j], ALU.subtract))

        first_max(k.rL[:, 0:n, 0:4], k.rO[:, 0:n, :])
        do(dve.tensor_tensor(k.rG[:, 0:n, :], k.rL[:, 0:n, 0:4], over4(m), ALU.subtract))
        dve.drain().then_inc(k.step_done.sem, 1)
        dve.wait_ge(k.step_done.sem, self.e + 2)
        do(dve.tensor_reduce(k.rs[:, 3, 0:n], k.rG[:, 0:n, :], AXX, ALU.add))
        do(dve.reciprocal(k.rs[:, 3, 0:n], k.rs[:, 3, 0:n]))
        E = k.rE[:, 0:n, :]
        for g in range(4):
            lg = k.rL[:, 0:n, 4 + 4 * g:8 + 4 * g]
            hot = k.rO[:, 0:n, g:g + 1].to_broadcast((P, n, 4))
            if g == 0:
                do(dve.tensor_tensor(E, lg, hot, ALU.mult))
            else:
                do(dve.tensor_tensor(k.rG[:, 0:n, :], lg, hot, ALU.mult))
                do(dve.tensor_tensor(E, E, k.rG[:, 0:n, :], ALU.add))
        do(dve.tensor_reduce(m, E, AXX, ALU.max))
        do(dve.tensor_tensor(E, E, over4(m), ALU.subtract))
        dve.drain().then_inc(k.step_done.sem, 1)
        dve.wait_ge(k.step_done.sem, self.e + 4)
        a, b = k.rA[:, 0:n, :], k.rB[:, 0:n, :]
        first_max(E, a)
        do(dve.scalar_tensor_tensor(k.rG[:, 0:n, :], a, -2.0, E, ALU.mult, ALU.add))
        first_max(k.rG[:, 0:n, :], b)
        do(dve.tensor_tensor(a, a, b, ALU.add))
        do(dve.tensor_tensor(a, a, E, ALU.mult))
        do(dve.tensor_reduce(m, a, AXX, ALU.add))
        do(dve.reciprocal(m, m))
        do(dve.tensor_tensor(m, m, k.rs[:, 3, 0:n], ALU.mult))
        do(dve.tensor_tensor(a, a, over4(m), ALU.mult))
        for g in range(4):
            do(dve.tensor_tensor(k.comb[:, 0:n, 4 * g:4 * g + 4], a, k.rO[:, 0:n, g:g + 1].to_broadcast((P, n, 4)), ALU.mult))


class Gated(Stage):

    def __init__(self, k, blocks, tiles, down, weight):
        super().__init__(k)
        self.tiles, self.down, self.weight = tiles, down, weight
        self.slots = []
        for gate, up, dn in blocks:
            s = []
            for k0 in (0, 4):
                parts = []
                for i, w in enumerate((gate, up)):
                    parts.append(((lambda s, i=i: s.rearrange("p (c a n) -> p c a n", c=4, a=2)[:, :, i, :]),
                                  w[k0 * P:(k0 + 4) * P, :].rearrange("(c p) n -> p c n", p=P)))
                s.append(k.rg.plan(parts))
            if down:
                s.append(k.rg.plan([((lambda s: s.rearrange("p (c n) -> p c n", c=2)),
                                     dn.rearrange("(c p) n -> p c n", p=P))]))
            self.slots.append(s)
        n = self.n = len(blocks) * len(tiles)
        self.gu = Banks(k, ["dve"] * n, 0, 2)
        self.silu = k.silu_done.reserve(n)
        self.hid = k.hid_done.reserve(n)
        if down:
            self.tr = Banks(k, ["act"] * n, 2, 2, lane=1)
            self.dn = Banks(k, ["dve"] * (2 * n), 4, 4, lane=2)

    def tensor(self, pe):
        k, T = self.k, len(self.tiles)
        for i in range(self.n + (2 if self.down else 0)):
            if i < self.n:
                j, t = i // T, self.tiles[i % T]
                s = self.slots[j]
                if i % T == 0:
                    k.rg.await_landed(pe, s[0])
                    k.rg.await_landed(pe, s[1])
                self.gu.may_fill(pe, i)
                for c in range(DK):
                    w = k.rg.slot(s[c // 4]).rearrange("p (c n) -> p c n", c=4)
                    last = pe.matmul(self.gu.bank(i), k.HT[:, c, t * P:(t + 1) * P], w[:, c % 4, :],
                                     start=(c == 0), stop=(c == DK - 1))
                self.gu.filled(last)
                if i % T == T - 1:
                    pe.drain().then_inc(k.weights_used, 2)
            if self.down and 1 <= i <= self.n:
                j = i - 1
                pe.wait_ge(k.hid_done.sem, self.hid + j + 1)
                self.tr.may_fill(pe, j)
                for c in range(2):
                    last = pe.transpose(self.tr.bank(j)[:, c * P:(c + 1) * P], k.hidb[:, j % 2, c * P:(c + 1) * P], k.ident[:, :])
                self.tr.filled(last)
            if self.down and i >= 2:
                j = i - 2
                s = self.slots[j // T]
                if j % T == 0:
                    k.rg.await_landed(pe, s[2])
                self.tr.taken(pe, j)
                w = k.rg.slot(s[2]).rearrange("p (c n) -> p c n", c=2)
                for hf in range(2):
                    self.dn.may_fill(pe, 2 * j + hf)
                    for c in range(2):
                        last = pe.matmul(self.dn.bank(2 * j + hf), k.hidTb[:, j % 2, c, :], w[:, c, hf * 512:(hf + 1) * 512],
                                         start=(c == 0), stop=(c == 1))
                    self.dn.filled(last)
                if j % T == T - 1:
                    pe.drain().then_inc(k.weights_used, 1)

    def scalar(self, act, ch):
        k = self.k
        for i in range(self.n + (1 if self.down else 0)):
            if i < self.n:
                self.gu.await_full(act, i)
                if i >= 2:
                    act.wait_ge(k.hid_done.sem, self.hid + i - 1)
                act.activation(k.silub[:, i % 2, :], self.gu.bank(i)[:, 0:EXH], ACT.Silu).then_inc(k.silu_done.sem, 1)
            if self.down and i >= 1:
                j = i - 1
                self.tr.await_full(act, j)
                if j >= 2:
                    self.dn.await_full(act, 2 * (j - 2) + 1)
                self.tr.take(j, act.activation(k.hidTb[:, j % 2], self.tr.bank(j)[:, 0:EXH].rearrange("p (c n) -> p c n", c=2), ACT.Copy))

    def vector(self, dve, ch):
        k, T = self.k, len(self.tiles)
        for i in range(self.n + (2 if self.down else 0)):
            if i < self.n:
                j, t = i // T, self.tiles[i % T]
                self.gu.await_full(dve, i)
                dve.wait_ge(k.silu_done.sem, self.silu + i + 1)
                up = self.gu.bank(i)[:, EXH:2 * EXH]
                if self.down:
                    if i >= 2:
                        self.tr.await_full(dve, i - 2)
                    dve.scalar_tensor_tensor(k.hidb[:, i % 2, :], up, self.weight(i % T, j), k.silub[:, i % 2, :],
                                             ALU.mult, ALU.mult)
                else:
                    dve.tensor_tensor(k.Zb(FFN)[:, t, j * EXH:(j + 1) * EXH], up, k.silub[:, i % 2, :], ALU.mult)
                dve.drain().then_inc(k.hid_done.sem, 1)
                self.gu.take(i, dve.drain())
            if self.down and i >= 2:
                j = i - 2
                e, t = j // T, j % T
                for hf in range(2):
                    self.dn.await_full(dve, 2 * j + hf)
                    acc = k.macc[:, t, hf * 512:(hf + 1) * 512]
                    if e == 0:
                        ins = dve.tensor_copy(acc, self.dn.bank(2 * j + hf))
                    else:
                        if hf == 0:
                            self.dn.taken(dve, 2 * (j - T) + 1)
                        ins = dve.tensor_tensor(acc, self.dn.bank(2 * j + hf), acc, ALU.add)
                    self.dn.take(2 * j + hf, ins)


class GatedResidual(Stage):

    def __init__(self, k, tiles):
        super().__init__(k)
        self.tiles = tiles

    def vector(self, dve, ch):
        k = self.k
        for i, t in enumerate(self.tiles):
            g = k.gatebc[:, 0 if t < ST else 1, :]
            ch.step(dve.tensor_tensor(k.macc[:, i, :], k.macc[:, i, :], g, ALU.mult))
            ch.wait()
            dve.tensor_tensor(k.X[:, t, :], k.X[:, t, :], k.macc[:, i, :], ALU.add)


def two_blocks(nc, A, C, out, scratch, upto=None, dumps=None):
    ctx = ExitStack()
    with ctx:
        k = K()

        def sb(name, shape, dt=F32):
            return ctx.enter_context(nc.sbuf_tensor(name, shape, dt))

        def sem(name):
            return ctx.enter_context(nc.semaphore(name))

        def tally(name):
            return Tally(sem(name))

        k.ring = sb("ring", [P, SLOTS, SLOT])
        k.X = sb("X", [P, NT, D])
        k.HT = sb("HT", [P, DK, NT * P])
        k.Z = sb("Z", [P, NT * EV_W])
        k.T = sb("T", [P, 22 * 512])
        k.ps = ctx.enter_context(nc.psum_tensor("ps", [P, 8, 512], F32))
        k.ident = sb("ident", [P, P])
        k.cmpmask = sb("cmpmask", [P, ST, NCMP])
        k.cmpvalid = sb("cmpvalid", [P, ST])
        k.glamask = sb("glamask", [P, 2, 7, P], U8)
        k.gains = sb("gains", [P, 6, DK])
        k.mc = sb("mc", [P, 2, 48, 2])
        k.mg = sb("mg", [P, 2, 2, 2, DK])
        k.cc = sb("cc", [P, DK, 2])
        k.sc = sb("sc", [P, DK, 2])
        k.hgain = sb("hgain", [P, 4, HD])
        k.ggain = sb("ggain", [P, GDV])
        k.gateb = sb("gateb", [P, 4])
        k.b1 = sb("b1", [P, 2])
        k.w2 = sb("w2", [P, 2, HD])
        k.posT = sb("posT", [P, CMP_LEN])
        k.sink = sb("sink", [P, SWA_HEADS])
        k.rw = sb("rw", [P, 2, DK, 20])
        k.rb = sb("rb", [P, 2, 20])
        k.gw = sb("gw", [32, 2, 256])
        k.kcmp = sb("kcmp", [P, NCMP])
        k.vcmp = sb("vcmp", [32, 2 * HD])
        k.gate3 = sb("gate3", [P, ST, 24])
        k.comb = sb("comb", [P, NT, NEXP])
        k.rL = sb("rL", [P, NT, 20])
        k.rG, k.rE, k.rO, k.rA, k.rB = (sb(n, [P, NT, 4]) for n in ("rG", "rE", "rO", "rA", "rB"))
        k.rs = sb("rs", [P, 4, NT])
        k.ss, k.ss2, k.rstd = (sb(n, [P, 8]) for n in ("ss", "ss2", "rstd"))
        k.hstat = sb("hstat", [P, 72])
        k.mx, k.nm, k.den, k.rd, k.es = (sb(n, [P, 4]) for n in ("mx", "nm", "den", "rd", "es"))
        k.gdecay = sb("gdecay", [P, 2 * NT])

        def Zb(w):
            n = min(NT, NT * EV_W // w)
            return k.Z[:, 0:n * w].rearrange("p (t w) -> p t w", w=w)
        k.Zb = Zb
        T = k.T
        k.HN = T[:, 0:NT * D].rearrange("p (t n) -> p t n", n=D)
        qkT = T[:, 0:14 * SEQ].rearrange("p (b n) -> p b n", n=SEQ)
        k.Pb = T[:, 7168:8704].rearrange("p (a n) -> p a n", a=2)
        k.PT = T[:, 8704:10240].rearrange("p (a n) -> p a n", a=2)
        k.bias = T[:, 10240:11264].rearrange("p (a n) -> p a n", a=2)
        k.tmp = T[:, 0:2304]
        k.rope = T[:, 9600:10112].rearrange("p (t a n) -> p t a n", t=ST, a=2)
        band = T[:, 10240:11136]
        k.cmpblk = lambda i: T[:, 8192 + i * 992:8192 + (i + 1) * 992].rearrange("p (n l) -> p n l", l=32)
        k.cmphid = T[:, 10176:10300].rearrange("p (a n) -> p a n", a=2)
        rawT = T[:, 7168:8192].rearrange("p (a n) -> p a n", a=2)

        def g3(o):
            return T[:, o:o + 1536].rearrange("p (a n) -> p a n", a=2)
        k.gqT, k.gkT = g3(0), g3(1536)
        k.gb = T[:, 3072:6144].rearrange("p (d a n) -> p d a n", d=2, a=2)
        k.gA, k.gB, k.gC = g3(6144), g3(7680), g3(9216)
        k.lrT = T[0:32, 6144:6912]
        k.gkh = T[:, 6144:7680].rearrange("p (t a n) -> p t a n", t=NT, a=2)
        k.gS = T[:, 10752:11264].rearrange("p (b a n) -> p b a n", b=2, a=2)
        hflat = k.HT[:, :, :].rearrange("p c n -> p (c n)")
        k.gacc = hflat[:, 0:3072].rearrange("p (t o a n) -> p t o a n", t=NT, o=2, a=2)
        k.gO = hflat[:, 3072:6144].rearrange("p (t n) -> p t n", t=NT)
        k.silub = T[:, 6144:6656].rearrange("p (a n) -> p a n", a=2)
        k.hidb = T[:, 6656:7168].rearrange("p (a n) -> p a n", a=2)
        k.hidTb = T[:, 7168:7680].rearrange("p (a c n) -> p a c n", a=2, c=2)
        k.macc = T[:, 0:NT * D].rearrange("p (t n) -> p t n", n=D)
        k.gatebc = T[:, 8192:10240].rearrange("p (a n) -> p a n", a=2)
        k.gtmp = T[:, 0:512]
        hidT = T[:, :].rearrange("p (c n) -> p c n", n=SEQ)
        rowgain = T[:, 8192:9216]
        k.maskf = T[:, 9472:11264].rearrange("p (d l n) -> p d l n", d=2, l=7)
        k.modb = lambda l: T[0:2, 0:6144] if l == 0 else hflat[0:2, 0:6144]

        k.landed = [sem(f"weights_landed_{i}") for i in range(SLOTS)]
        k.weights_used = sem("weights_used")
        k.stage_done = sem("stage_done")
        k.bias_spread = sem("bias_spread")
        k.step_done, k.small_landed = tally("step_done"), tally("small_landed")
        k.norm_squares, k.norm_mean = tally("norm_squares"), tally("norm_mean")
        k.norm_roots, k.norm_rows = tally("norm_roots"), tally("norm_rows")
        k.scores_full, k.scores_topped, k.probs_done = tally("scores_full"), tally("scores_topped"), tally("probs_done")
        k.probsT_full, k.probsT_out = tally("probsT_full"), tally("probsT_out")
        k.out_full, k.out_taken = tally("out_full"), tally("out_taken")
        k.bias_landed, k.bias_used, k.gates_done = tally("bias_landed"), tally("bias_used"), tally("gates_done")
        k.gla_diff, k.gla_exp, k.gla_k, k.gla_qk = tally("gla_diff"), tally("gla_exp"), tally("gla_k"), tally("gla_qk")
        k.silu_done, k.hid_done = tally("silu_done"), tally("hid_done")
        k.lanes = [(tally(f"psum_full_{i}"), {"act": tally(f"psum_taken_by_scalar_{i}"), "dve": tally(f"psum_taken_by_vector_{i}")})
                   for i in range(3)]
        k.psum_full = k.lanes[0][0]
        dve_order, act_order, pool_order = sem("vector_order"), sem("scalar_order"), sem("gpsimd_order")
        k.rg = Ring(k)
        stages = []
        add = stages.append

        def bc(ap, n, off=0, parts=P):
            return bass.AP(tensor=ap.tensor, offset=ap.offset + off, ap=[[0, parts], [1, n]])

        table = T[0:33, 7424:7440]
        hot = T[0:33, 6144:6144 + 2 * ROW].rearrange("p (a n) -> p a n", a=2)
        pairs = [(k.ident[:, :], C["ident"]), (k.cmpmask[:, :, :], C["cmpmask"]), (k.cmpvalid[:, :], C["cmpvalid"]),
                 (k.maskf, C["glamask"]), (k.gains[:, :, :], A["gains"]), (k.cc[:, :, :], A["cc"]),
                 (k.gateb[:, :], A["gateb"]), (k.b1[:, :], A["b1"]), (k.posT[:, :], A["posT"]),
                 (k.X[:, 0:ST, :], A["x"][0].rearrange("(t p) n -> p t n", p=P)),
                 (k.X[:, ST:NT, :], A["ctx_2"][0].rearrange("(t p) n -> p t n", p=P)),
                 (k.ggain[:, :], bc(A["gla_out_norm_2"], GDV)), (k.sink[:, :], bc(A["swa_sink_2"], SWA_HEADS)),
                 (k.w2[:, 0, :], A["cmp_k_w2"][0]), (k.w2[:, 1, :], A["cmp_v_w2"][0]), (k.gw[:, :, :], A["gw"]),
                 (table, A["table"]), (hot, C["hot"]),
                 (k.modb(0), bc(A["mod_b_2"], 6144, 0, 2)), (k.modb(1), bc(A["mod_b_2"], 6144, 6144, 2))]
        for i, n in enumerate(("att_q_norm_2", "att_k_norm_2", "swa_q_norm_2", "swa_k_norm_2")):
            pairs.append((k.hgain[:, i, :], bc(A[n], HD)))
        for l in range(2):
            pairs += [(k.rw[:, l, :, 0:4], A["router_group_w_2"][l].rearrange("(c p) n -> p c n", p=P)),
                      (k.rw[:, l, :, 4:20], A["router_expert_w_2"][l].rearrange("(c p) n -> p c n", p=P)),
                      (k.rb[:, l, 0:4], bc(A["router_group_b_2"], 4, 4 * l)),
                      (k.rb[:, l, 4:20], bc(A["router_expert_b_2"], 16, 16 * l))]
        add(Load(k, pairs))

        mods = ModVectors(k, A)
        add(mods)
        rows = BiasRows(k, table, hot, scratch["bias"], scratch["spread"])
        rows.buf = T[0:8, 7440:7440 + 2 * ROW].rearrange("p (a n) -> p a n", a=2)
        add(rows)
        add(ModColumns(k, mods.rows, scratch["mods"]))

        seq, allt, ctxt = list(range(ST)), list(range(NT)), list(range(ST, NT))

        def cols_of(ts):
            return slice(ts[0] * P, (ts[-1] + 1) * P)

        def gain(i):
            return lambda c: k.gains[:, i, c:c + 1]

        def hT(c, t):
            return k.HT[:, c, t * P:(t + 1) * P]

        def to_z(w, off=0):
            z = k.Zb(w)
            return lambda eng, name, ch, t, c0, cn, ps: copy(eng, name, z[:, t, off + c0:off + c0 + cn], ps)

        def cols(z, c, n=P):
            return lambda t: z[:, t, c:c + n]

        def head_pair(z, c0, r):
            return cols(z, c0 + r * P)

        scale = HD ** -0.5
        add(norm_stage(k, [(seq, gain(0), None)]))
        add(Linear(k, hT, DK, A["w_in"][0], IN_W, seq, to_z(IN_W)))
        z = k.Zb(IN_W)
        units = [(cols(z, AQ + b * P), P, seq, qkT[:, b, :], scale) for b in range(4)]
        units += [(cols(z, AK + b * P), P, seq, qkT[:, 4 + b, :], None) for b in range(4)]
        units += [(head_pair(z, BQ, r), P, seq, qkT[:, 8 + r, :], scale) for r in range(4)]
        units += [(cols(z, KSL), P, seq, qkT[:, 12, :], None), (cols(z, KW), P, seq, qkT[:, 13, :], None),
                  (cols(z, KC), P, seq, rawT[:, 0, :], None), (cols(z, VC), P, seq, rawT[:, 1, :], None)]
        add(Transposes(k, units))
        add(Sigmoids(k))
        add(Compress(k, A, rawT[:, 0, :], rawT[:, 1, :]))

        def first_jobs(h, tile):
            jobs = []
            for i in range(ST):
                n = (i + 1) * P
                base = dict(bias=tile[:, 384 - i * P:512], sink=None, gate=None, first=True)
                if h < A_HEADS:
                    r = slice(64 * (h % 2), 64 * (h % 2) + 64)
                    jobs.append(dict(base, q=qkT[r, h // 2, i * P:n], keys=[(qkT[r, 4 + h // 2, 0:n], n)],
                                     values=[(z[:, t, AV + h * HD:AV + (h + 1) * HD], P) for t in range(i + 1)],
                                     out=z[:, i, AQ + h * HD:AQ + (h + 1) * HD]))
                    continue
                hb = h - A_HEADS
                g, rr = hb // 4, hb % 4
                r = slice(64 * g, 64 * g + 64)
                q = qkT[r, 8 + rr, i * P:n]
                at = BQ + (2 * rr + g) * HD
                o = z[:, i, at:at + HD]
                gates = [k.gate3[:, i, hb * 3 + b:hb * 3 + b + 1] for b in range(3)]
                jobs.append(dict(base, q=q, keys=[(k.kcmp[r, :], NCMP)], values=[(k.vcmp[0:NCMP, g * HD:(g + 1) * HD], NCMP)],
                                 bias=k.cmpmask[:, i, :], gate=gates[0], out=o))
                for b, kk, vv in ((1, 12, VSL), (2, 13, VW)):
                    jobs.append(dict(base, q=q, keys=[(qkT[r, kk, 0:n], n)], gate=gates[b], first=False,
                                     values=[(z[:, t, vv + g * HD:vv + (g + 1) * HD], P) for t in range(i + 1)], out=o))
            return jobs
        add(Bias(k, first_jobs, list(range(16)), scratch["spread"]))

        def mixT_units(w, starts, tiles):
            zz = k.Zb(w)
            return [(cols(zz, c0), P, ts, k.HT[:, c, cols_of(ts)], None) for c, c0 in enumerate(starts)
                    for ts in ([t for t in tiles if t < ST], [t for t in tiles if t >= ST]) if ts]
        add(Transposes(k, mixT_units(IN_W, [AQ + P * b for b in range(4)] + [BQ + P * b for b in range(4)], seq)))

        def residual(eng, name, ch, t, c0, cn, ps):
            x = k.X[:, t, c0:c0 + cn]
            return eng.tensor_tensor(x, ps, x, ALU.add)
        add(Linear(k, hT, DK, A["w_out"][0], D, seq, residual, ["dve"] * 8))

        add(norm_stage(k, [(seq, gain(1), None)]))
        wg, wu = A["w_gate"][0], A["w_up"][0]
        add(Gated(k, [(wg[:, j * EXH:(j + 1) * EXH], wu[:, j * EXH:(j + 1) * EXH], None) for j in range(FFN // EXH)],
                  seq, False, None))
        zf = k.Zb(FFN)
        add(Transposes(k, [(cols(zf, c * P), P, seq, hidT[:, c, :], None) for c in range(FFN // P)]))
        add(Linear(k, lambda c, t: hidT[:, c, t * P:(t + 1) * P], FFN // P, A["w_down"][0], D, seq, residual, ["dve"] * 8))
        add(Load(k, [(rowgain, bc(A["norm_f_g"], D))]))
        add(RowNorm(k, seq, rowgain))

        def mod_sets(l, w, both):
            m = (0, 3)[w]

            def col(buf, r, at):
                return lambda c: buf[:, at + c, r:r + 1]

            def gcol(r):
                return lambda c: k.mg[:, l, w, r, c:c + 1]
            sets = [(seq, gcol(0), col(k.mc[:, l], 0, m * DK))]
            return sets + ([(ctxt, gcol(1), col(k.mc[:, l], 1, m * DK))] if both else [])

        def gated_take(eng, name, ch, t, c0, cn, ps):
            g = k.gatebc[:, 0 if t < ST else 1, c0:c0 + cn]
            x = k.X[:, t, c0:c0 + cn]
            ch.wait()
            ch.step(eng.tensor_tensor(k.gtmp[:, 0:cn], ps, g, ALU.mult))
            ch.wait()
            ch.step(eng.tensor_tensor(x, x, k.gtmp[:, 0:cn], ALU.add))
            return eng.drain()

        def gate_loads(l, m, n):
            return [(k.gatebc[:, r, :], bc(scratch["mods"], D, (l * 2 + r) * 6144 + m * D)) for r in range(n)]

        def moe(l, tiles):
            both = len(tiles) > ST
            add(norm_stage(k, mod_sets(l, 1, both)))
            add(Router(k, l, tiles))
            add(Gated(k, [(A["exp_w_gate_2"][l][e // 4][e % 4], A["exp_w_up_2"][l][e // 4][e % 4],
                           A["exp_w_down_2"][l][e // 4][e % 4]) for e in range(NEXP)], tiles, True,
                      lambda i, e: k.comb[:, i, e:e + 1]))
            add(Load(k, gate_loads(l, 5, 1 + both)))
            add(GatedResidual(k, tiles))

        add(norm_stage(k, mod_sets(0, 0, True)))
        add(Linear(k, hT, DK, A["ev_w_in_2"][0], EV_W, allt, to_z(EV_W)))
        ze = k.Zb(EV_W)
        units = []
        for ts in (seq, ctxt):
            c = cols_of(ts)
            for p in range(2):
                units.append((cols(ze, GQ + p * P), P, ts, k.gqT[:, p, c], GDK ** -0.5))
                units.append((cols(ze, GK + p * P), P, ts, k.gkT[:, p, c], None))
            units.append((cols(ze, LR, 32), 32, ts, k.lrT[:, c], None))
        add(Transposes(k, units))
        add(GlaGates(k))
        for d in range(2):
            add(GlaScores(k, d))
            add(GlaDecayed(k, d))
            add(GlaScan(k, d))
        add(GlaOutput(k))
        add(Load(k, [(k.rope, C["rope"])]))
        qk_gain = [(8, k.hgain[:, 0, :]), (2, k.hgain[:, 1, :])]
        add(HeadNorm(k, EV_W, [(seq, EQ, 10, qk_gain), (ctxt, EQ, 10, qk_gain)]))
        eqT = T[:, 0:4 * 768].rearrange("p (b n) -> p b n", n=768)
        ekT = T[:, 3072:3840]
        units = []
        for ts in (seq, ctxt):
            units += [(head_pair(ze, EQ, r), P, ts, eqT[:, r, cols_of(ts)], scale) for r in range(4)]
            units.append((cols(ze, EK), P, ts, ekT[:, cols_of(ts)], None))
        add(Transposes(k, units))
        jobs = []
        for h in range(8):
            g, rr = h // 4, h % 4
            r = slice(64 * g, 64 * g + 64)
            for i in allt:
                ks = [(ekT[r, 0:768], 768)] if i < ST else [(ekT[r, 512:768], 256)]
                jobs.append(dict(q=eqT[r, rr, i * P:(i + 1) * P], keys=ks, bias=None, sink=None, gate=None, first=True,
                                 values=[(ze[:, t, EVV + g * HD:EVV + (g + 1) * HD], P) for t in (allt if i < ST else ctxt)],
                                 out=ze[:, i, EQ + (2 * rr + g) * HD:EQ + (2 * rr + g + 1) * HD]))
        add(Attention(k, jobs))
        add(Transposes(k, mixT_units(EV_W, [P * b for b in range(4)] + [EQ + P * b for b in range(4)], allt)))
        add(Load(k, gate_loads(0, 2, 2)))
        add(Linear(k, hT, DK, A["ev_w_out_2"][0], D, allt, gated_take, ["dve"] * 12))
        moe(0, allt)

        add(norm_stage(k, mod_sets(1, 0, True)))
        add(Linear(k, hT, DK, A["od_w_in_2"][0][:, 0:1024], 1024, seq, to_z(OD_W)))
        add(Linear(k, hT, DK, A["od_w_in_2"][0][:, 1024:OD_W], 256, allt, to_z(OD_W, 1024)))
        zo = k.Zb(OD_W)
        add(Load(k, [(k.rope, C["rope"])]))
        add(HeadNorm(k, OD_W, [(seq, OQ, 18, [(16, k.hgain[:, 2, :]), (2, k.hgain[:, 3, :])]),
                               (ctxt, OK_, 2, [(2, k.hgain[:, 3, :])])]))
        oqT = T[:, 0:8 * SEQ].rearrange("p (b n) -> p b n", n=SEQ)
        okT = T[:, 4096:4864]
        units = [(head_pair(zo, OQ, r), P, seq, oqT[:, r, :], scale) for r in range(8)]
        units += [(cols(zo, OK_), P, ts, okT[:, cols_of(ts)], None) for ts in (seq, ctxt)]
        add(Load(k, [(band, C["band"])]))
        add(Transposes(k, units))
        jobs = []
        for h in range(SWA_HEADS):
            g, rr = h // 8, h % 8
            r = slice(64 * g, 64 * g + 64)
            for i in seq:
                ts = [t for t in (i - 1, i, i + 1) if 0 <= t < ST]
                n = len(ts) * P
                near, far = [(okT[r, cols_of(ts)], n)], [(okT[r, SEQ:SEQ + CTX], CTX)]
                keys, vt, bias = (near + far, ts + ctxt, band[:, CTX + P:896]) if i == 0 else (far + near, ctxt + ts, band[:, 0:CTX + n])
                jobs.append(dict(q=oqT[r, rr, i * P:(i + 1) * P], keys=keys, bias=bias, sink=k.sink[:, h:h + 1], gate=None,
                                 first=True, values=[(zo[:, t, OV + g * HD:OV + (g + 1) * HD], P) for t in vt],
                                 out=zo[:, i, (2 * rr + g) * HD:(2 * rr + g + 1) * HD]))
        add(Attention(k, jobs))
        add(Transposes(k, mixT_units(OD_W, [P * b for b in range(8)], seq)))
        add(Load(k, gate_loads(1, 2, 1)))
        add(Linear(k, hT, DK, A["od_w_out_2"][0], D, seq, gated_take, ["dve"] * 8))
        moe(1, seq)
        if upto is not None:
            stages = stages[:upto]
            k.small_landed = tally("dumped")
            k.rg.loads = k.rg.loads[:dumps["loads"](k, stages)] if "loads" in dumps else k.rg.loads
        result = Load(k, [(out[0].rearrange("(t p) n -> p t n", p=P), k.X[:, 0:ST, :])] + (dumps["pairs"](k) if dumps else []))
        stages.append(result)

        def meet(eng, i):
            eng.drain().then_inc(k.stage_done, 1)
            eng.wait_ge(k.stage_done, 4 * (i + 1))

        block = ctx.enter_context(nc.Block())

        @block.sync
        def _(sp):
            k.rg.fill(sp)

        @block.tensor
        def _(pe):
            for i, s in enumerate(stages):
                s.tensor(pe)
                meet(pe, i)

        @block.vector
        def _(dve):
            ch = Chain(dve, dve_order)
            for i, s in enumerate(stages):
                s.vector(dve, ch)
                meet(dve, i)

        @block.scalar
        def _(act):
            ch = Chain(act, act_order)
            for i, s in enumerate(stages):
                s.scalar(act, ch)
                meet(act, i)

        @block.gpsimd
        def _(pool):
            ch = Chain(pool, pool_order)
            for i, s in enumerate(stages):
                s.gpsimd(pool, ch)
                meet(pool, i)
        return stages


RAW = ["x", "ctx_2", "w_in", "cmp_k_w1", "cmp_k_w2", "cmp_v_w1", "cmp_v_w2", "w_out", "w_gate", "w_up", "w_down",
       "norm_f_g", "mod_w_2", "mod_b_2", "ev_w_in_2", "ev_w_out_2", "gla_out_norm_2", "att_q_norm_2", "att_k_norm_2",
       "od_w_in_2", "od_w_out_2", "swa_sink_2", "swa_q_norm_2", "swa_k_norm_2", "router_group_w_2", "router_group_b_2",
       "router_expert_w_2", "router_expert_b_2", "exp_w_gate_2", "exp_w_up_2", "exp_w_down_2"]


def lay_out(inputs):
    a = {n: np.ascontiguousarray(inputs[n]) for n in RAW}

    def by_pair(w, at, per, axis):
        w = np.asarray(w)
        idx = np.arange(w.shape[axis])
        idx[at:at + 2 * per * HD] = at + np.arange(2 * per * HD).reshape(2, per, HD).transpose(1, 0, 2).ravel()
        return np.ascontiguousarray(np.take(w, idx, axis))
    a["w_in"] = by_pair(a["w_in"], BQ, 4, 2)
    a["w_out"] = by_pair(a["w_out"], 512, 4, 1)
    a["ev_w_in_2"] = by_pair(a["ev_w_in_2"], EQ, 4, 2)
    a["ev_w_out_2"] = by_pair(a["ev_w_out_2"], 512, 4, 1)
    a["od_w_in_2"] = by_pair(a["od_w_in_2"], OQ, 8, 2)
    a["od_w_out_2"] = by_pair(a["od_w_out_2"], 0, 8, 1)

    def column(v):
        return np.asarray(v).reshape(DK, P).T
    a["gains"] = np.ascontiguousarray(np.stack(
        [column(inputs["norm1_g"][0]), column(inputs["norm2_g"][0])]
        + [column(inputs["norm_mix_2"][l]) for l in range(2)] + [column(inputs["norm_ffn_2"][l]) for l in range(2)], 1))
    a["cc"] = np.ascontiguousarray(np.stack([column(inputs["c_2"][0]), column(inputs["c_ctx_2"])], 2))
    a["gateb"] = np.ascontiguousarray(np.asarray(inputs["gla_gate_b_2"]).reshape(4, P).T)
    a["b1"] = np.ascontiguousarray(np.stack([inputs["cmp_k_b1"][0], inputs["cmp_v_b1"][0]], 1))
    pos = np.asarray(inputs["cmp_pos"][0]).T
    a["posT"] = np.ascontiguousarray(np.concatenate([pos, pos], 0))
    gw = np.zeros((32, 2, 256), np.float32)
    for d in range(2):
        gw[16 * d:16 * d + 16, d] = inputs["gla_gate_w_2"][0, d]
    a["gw"] = gw
    a["table"] = np.ascontiguousarray(np.concatenate([inputs["rel_bias"], np.ones((1, 16), np.float32)], 0))
    return a


def build(nc, inputs, upto=None, dumps=None):
    arrays, A, C = {}, {}, {}
    for dst, src, tag in ((A, lay_out(inputs), "in"), (C, shape_constants(), "const")):
        for n, v in src.items():
            arrays[f"{tag}_{n}"] = v
            dst[n] = nc.dram_tensor(f"{tag}_{n}", v.shape, mybir.dt.from_np(v.dtype), kind="ExternalInput").ap()
    out = nc.dram_tensor("out_x", (1, SEQ, D), F32, kind="ExternalOutput").ap()
    scratch = {"bias": nc.dram_tensor("bias_rows", (16, ROW), F32, kind="Internal").ap(),
               "spread": nc.dram_tensor("bias_spread", (16, P, ROW), F32, kind="Internal").ap(),
               "mods": nc.dram_tensor("mod_rows", (2, 2, 6144), F32, kind="Internal").ap()}
    d = dumps(nc) if dumps else None
    stages = two_blocks(nc, A, C, out, scratch, upto, d)
    return arrays, stages


def kernel(**inputs):
    import concourse.bacc as bacc
    from concourse.bass_utils import run_bass_kernel_spmd

    nc = bacc.Bacc("TRN2", target_bir_lowering=False, num_devices=1)
    arrays, _ = build(nc, inputs)
    r = run_bass_kernel_spmd(nc, [arrays], core_ids=[0])
    return r.results[0]["out_x"]
```

```python
from contextlib import ExitStack

import numpy as np

import concourse.bass as bass
from concourse import mybir

F32 = mybir.dt.float32
U8, U32, I32 = mybir.dt.uint8, mybir.dt.uint32, mybir.dt.int32
ALU = mybir.AluOpType
ACT = mybir.ActivationFunctionType
AXX = mybir.AxisListType.X

P = 128
D = 1024
DK = D // P
SEQ, CTX = 512, 256
ST, CT = SEQ // P, CTX // P
NT = ST + CT
HD = 64
NEG = -1e30
EPS = 1e-6

A_HEADS, B_HEADS, B_KV = 8, 8, 2
IN_W = 3 * 512 + 512 + 6 * 128 + 24
AQ, AK, AV, BQ = 0, 512, 1024, 1536
KC, VC, KSL, VSL, KW, VW, GL = (2048 + 128 * i for i in range(7))
CMP_LEN, CMP_STRIDE, CMP_HID = 32, 16, 128
NCMP = SEQ // CMP_STRIDE - 1
FFN = 2816
BUCKETS, MAX_DIST = 32, 2048
ROW = 640

EV_W = 256 + 256 + 512 + 512 + 32 + 512 + 128 + 128
GQ, GK, GV, GR, LR, EQ, EK, EVV = 0, 256, 512, 1024, 1536, 1568, 2080, 2208
GH, GDK, GDV = 4, 64, 128
OD_W = 1024 + 256
OQ, OK_, OV = 0, 1024, 1152
SWA_HEADS = 16
NEXP, NGRP, EXH = 16, 4, 256
SLOTS = 6
SLOT = 2048


def _t5_bucket(dist):
    half = BUCKETS // 2
    df = np.maximum(dist, 1).astype(np.float32)
    large = half + (np.log(df / np.float32(half)) / np.float32(np.log(MAX_DIST / half))
                    * np.float32(BUCKETS - half)).astype(np.int32)
    return np.where(dist < half, dist, np.minimum(large, BUCKETS - 1))


def shape_constants():
    c = {}
    c["ident"] = np.eye(P, dtype=np.float32)
    d = 511 - np.arange(ROW)
    hot = np.zeros((BUCKETS + 1, 2, ROW), np.float32)
    b = _t5_bucket(np.maximum(d, 0))
    for j in range(ROW):
        if d[j] >= 0:
            hot[b[j], :, j] = 1.0
    count = (d <= 128).astype(int) + (d % 4 == 0) + (d % 16 == 0)
    hot[BUCKETS, 0] = np.where((d >= 0) & (count > 0), np.log(np.maximum(count, 1)), NEG)
    hot[BUCKETS, 1] = np.where(d >= 0, 0.0, NEG)
    c["hot"] = hot
    t = np.arange(SEQ)
    ends = np.arange(NCMP) * CMP_STRIDE + CMP_LEN - 1
    m = np.where(ends[None, :] <= t[:, None], 0.0, NEG).astype(np.float32)
    c["cmpmask"] = np.ascontiguousarray(m.reshape(ST, P, NCMP).transpose(1, 0, 2))
    c["cmpvalid"] = np.ascontiguousarray((t >= CMP_LEN - 1).astype(np.float32).reshape(ST, P).T)
    inv = np.float32(10000.0) ** (-np.arange(0, 32, 2, dtype=np.float32) / np.float32(32))
    ang = np.stack([(t // 64)[:, None].astype(np.float32) * inv, (t % 64)[:, None].astype(np.float32) * inv], 1)
    co, si = np.cos(ang), np.sin(ang)
    full = np.stack([np.stack([co, co], 2), np.stack([-si, si], 2)], 1).reshape(SEQ, 2, HD)
    c["rope"] = np.ascontiguousarray(full.reshape(ST, P, 2, HD).transpose(1, 0, 2, 3)).astype(np.float32)
    y, p = np.arange(384)[None, :], np.arange(P)[:, None]
    band = np.where((y - p >= 0) & (y - p <= 256), 0.0, NEG)
    c["band"] = np.concatenate([np.zeros((P, CTX)), band, np.zeros((P, CTX))], 1).astype(np.float32)
    s, t = np.arange(P)[:, None], np.arange(P)[None, :]
    g = np.zeros((P, 2, 7, P), np.float32)
    for lv in range(7):
        h = 1 << lv
        same = (s // (2 * h)) == (t // (2 * h))
        g[:, 0, lv] = same & ((s // h) % 2 == 0) & ((t // h) % 2 == 1)
        g[:, 1, lv] = same & ((s // h) % 2 == 1) & ((t // h) % 2 == 0)
    c["glamask"] = g
    c["iota"] = np.tile(np.arange(P, dtype=np.float32), (P, 1))
    c["token"] = np.ascontiguousarray(np.arange(NT * P, dtype=np.float32).reshape(NT, P).T)
    c["before"] = np.triu(np.ones((P, P), np.float32), 1)
    return c


class Tally:

    def __init__(self, sem):
        self.sem, self.total = sem, 0

    def reserve(self, n):
        base = self.total
        self.total += n
        return base


class Chain:

    def __init__(self, eng, sem):
        self.eng, self.sem, self.n = eng, sem, 0

    def step(self, ins):
        ins.then_inc(self.sem, 1)
        self.n += 1

    def wait(self):
        if self.n:
            self.eng.wait_ge(self.sem, self.n)


class Banks:

    def __init__(self, k, owners, first=0, count=8, lane=0):
        self.k, self.owners, self.first, self.count = k, owners, first, count
        self.full_sem, self.taken_sems = k.lanes[lane]
        self.full = self.full_sem.reserve(len(owners))
        self.base = {e: self.taken_sems[e].reserve(sum(o == e for o in owners)) for e in ("act", "dve")}

    def bank(self, u):
        return self.k.ps[:, self.first + u % self.count, :]

    def may_fill(self, pe, u):
        if u >= self.count:
            self.taken(pe, u - self.count)

    def taken(self, eng, v):
        o = self.owners[v]
        eng.wait_ge(self.taken_sems[o].sem, self.base[o] + self.owners[:v + 1].count(o))

    def filled(self, ins):
        ins.then_inc(self.full_sem.sem, 1)

    def await_full(self, eng, u):
        eng.wait_ge(self.full_sem.sem, self.full + u + 1)

    def take(self, u, ins):
        ins.then_inc(self.taken_sems[self.owners[u]].sem, 1)


class K:
    pass


class Stage:

    def __init__(self, k):
        self.k = k

    def tensor(self, pe):
        pass

    def vector(self, dve, ch):
        pass

    def scalar(self, act, ch):
        pass

    def gpsimd(self, pool, ch):
        pass


def alternate(n):
    return ["act" if i % 2 else "dve" for i in range(n)]


class Ring:
    def __init__(self, k):
        self.k, self.loads, self.next = k, [], 0
        self.landed_at, self.count = [], [0] * SLOTS

    def plan(self, parts):
        r = len(self.loads) % SLOTS
        self.count[r] += 16 * len(parts)
        self.landed_at.append(self.count[r])
        self.loads.append(parts)
        return len(self.loads) - 1

    def slot(self, n):
        return self.k.ring[:, n % SLOTS, :]

    def await_landed(self, pe, n):
        pe.wait_ge(self.k.landed[n % SLOTS], self.landed_at[n])

    def released(self, ins):
        ins.then_inc(self.k.weights_used, 1)

    def fill(self, sp):
        for n, parts in enumerate(self.loads):
            if parts is None:
                continue
            if isinstance(parts, ExpertLoads):
                parts.fill(sp)
                continue
            if n >= SLOTS:
                sp.wait_ge(self.k.weights_used, n - SLOTS + 1)
            for place, src in parts:
                sp.dma_start(place(self.slot(n)), src).then_inc(self.k.landed[n % SLOTS], 16)


def plan_columns(k, w, k0, kn, c0, cn):
    src = w[k0 * P:(k0 + kn) * P, c0:c0 + cn].rearrange("(c p) n -> p c n", p=P)
    return k.rg.plan([(lambda s: s[:, 0:kn * cn].rearrange("p (c n) -> p c n", c=kn), src)])


class Linear(Stage):

    def __init__(self, k, lhs, nk, w, width, tiles, take, owners=None, rows=P):
        super().__init__(k)
        self.lhs, self.tiles, self.take_fn, self.nk, self.rows = lhs, tiles, take, nk, rows
        self.blocks = []
        for c0 in range(0, width, 512):
            cn = min(512, width - c0)
            slots = [(k0, min(4, nk - k0), plan_columns(k, w, k0, min(4, nk - k0), c0, cn)) for k0 in range(0, nk, 4)]
            self.blocks.append((c0, cn, slots))
        n = len(self.blocks) * len(tiles)
        self.banks = Banks(k, owners or alternate(n))

    def tensor(self, pe):
        k, u0 = self.k, 0
        for c0, cn, slots in self.blocks:
            for si, (k0, kn, n) in enumerate(slots):
                k.rg.await_landed(pe, n)
                w = k.rg.slot(n)[:, 0:kn * cn].rearrange("p (c n) -> p c n", c=kn)
                for i, t in enumerate(self.tiles):
                    if si == 0:
                        self.banks.may_fill(pe, u0 + i)
                    for c in range(kn):
                        last = pe.matmul(self.banks.bank(u0 + i)[0:self.rows, 0:cn], self.lhs(k0 + c, t), w[:, c, :],
                                         start=(k0 + c == 0), stop=(k0 + c == self.nk - 1))
                    if si == len(slots) - 1 and i < len(self.tiles) - 1:
                        self.banks.filled(last)
                if si == len(slots) - 1:
                    self.banks.filled(last)
                    pe.drain().then_inc(k.weights_used, 1)
                else:
                    k.rg.released(last)
            u0 += len(self.tiles)

    def _take(self, eng, name, ch):
        u = 0
        for c0, cn, _ in self.blocks:
            for t in self.tiles:
                if self.banks.owners[u] == name:
                    self.banks.await_full(eng, u)
                    self.banks.take(u, self.take_fn(eng, name, ch, t, c0, cn, self.banks.bank(u)[:, 0:cn]))
                u += 1

    def vector(self, dve, ch):
        self._take(dve, "dve", ch)

    def scalar(self, act, ch):
        self._take(act, "act", ch)


def copy(eng, name, out, src, scale=None):
    if name == "act":
        return eng.activation(out, src, ACT.Copy, scale=1.0 if scale is None else scale)
    if scale is None:
        return eng.tensor_copy(out, src)
    return eng.tensor_scalar(out, src, scale, None, ALU.mult)


class Norm(Stage):

    def __init__(self, k, sets):
        super().__init__(k)
        self.sets = sets
        self.tiles = [t for ts, _, _ in sets for t in ts]
        self.units = [(i, c) for i in range(len(sets)) for c in range(DK)]
        self.banks = Banks(k, alternate(len(self.units)))
        self.sq = k.norm_squares.reserve(len(self.tiles))
        self.rt = k.norm_roots.reserve(1)
        self.hn = k.norm_rows.reserve(len(self.tiles))

    def scalar(self, act, ch):
        k = self.k
        for i, t in enumerate(self.tiles):
            act.activation(k.HN[:, t, :], k.X[:, t, :], ACT.Square,
                           accum_out=k.ss[:, t:t + 1]).then_inc(k.norm_squares.sem, 1)
        act.wait_ge(k.norm_mean.sem, self.mean + 1)
        t0, t1 = self.tiles[0], self.tiles[-1] + 1
        act.activation(k.ss2[:, t0:t1], k.ss2[:, t0:t1], ACT.Sqrt).then_inc(k.norm_roots.sem, 1)
        self._take(act, "act")

    def vector(self, dve, ch):
        k = self.k
        t0, t1 = self.tiles[0], self.tiles[-1] + 1
        dve.wait_ge(k.norm_squares.sem, self.sq + len(self.tiles))
        dve.tensor_scalar(k.ss2[:, t0:t1], k.ss[:, t0:t1], 1.0 / D, EPS, ALU.mult, ALU.add).then_inc(k.norm_mean.sem, 1)
        dve.wait_ge(k.norm_roots.sem, self.rt + 1)
        ch.step(dve.reciprocal(k.rstd[:, t0:t1], k.ss2[:, t0:t1]))
        ch.wait()
        for i, t in enumerate(self.tiles):
            dve.tensor_scalar(k.HN[:, t, :], k.X[:, t, :], k.rstd[:, t:t + 1], None, ALU.mult).then_inc(k.norm_rows.sem, 1)
        self._take(dve, "dve")

    def tensor(self, pe):
        k = self.k
        for u, (i, c) in enumerate(self.units):
            ts = self.sets[i][0]
            if c == 0:
                pe.wait_ge(k.norm_rows.sem, self.hn + self.tiles.index(ts[-1]) + 1)
            self.banks.may_fill(pe, u)
            for j, t in enumerate(ts):
                last = pe.transpose(self.banks.bank(u)[:, j * P:(j + 1) * P], k.HN[:, t, c * P:(c + 1) * P], k.ident[:, :])
            self.banks.filled(last)

    def _take(self, eng, name):
        k = self.k
        for u, (i, c) in enumerate(self.units):
            if self.banks.owners[u] != name:
                continue
            ts, gain, shift = self.sets[i]
            out = k.HT[:, c, ts[0] * P:(ts[-1] + 1) * P]
            src = self.banks.bank(u)[:, 0:len(ts) * P]
            self.banks.await_full(eng, u)
            if name == "act":
                ins = eng.activation(out, src, ACT.Identity, scale=gain(c), bias=shift(c) if shift else 0.0)
            elif shift:
                ins = eng.tensor_scalar(out, src, gain(c), shift(c), ALU.mult, ALU.add)
            else:
                ins = eng.tensor_scalar(out, src, gain(c), None, ALU.mult)
            self.banks.take(u, ins)


def norm_stage(k, sets):
    s = Norm(k, sets)
    s.mean = k.norm_mean.reserve(1)
    return s


class Transposes(Stage):

    def __init__(self, k, units):
        super().__init__(k)
        self.units = units
        self.banks = Banks(k, alternate(len(units)))

    def tensor(self, pe):
        for u, (src, rows, tiles, dst, scale) in enumerate(self.units):
            self.banks.may_fill(pe, u)
            for j, t in enumerate(tiles):
                last = pe.transpose(self.banks.bank(u)[0:rows, j * P:(j + 1) * P], src(t), self.k.ident[:, :])
            self.banks.filled(last)

    def _take(self, eng, name):
        for u, (src, rows, tiles, dst, scale) in enumerate(self.units):
            if self.banks.owners[u] == name:
                self.banks.await_full(eng, u)
                self.banks.take(u, copy(eng, name, dst, self.banks.bank(u)[0:rows, 0:len(tiles) * P], scale))

    def vector(self, dve, ch):
        self._take(dve, "dve")

    def scalar(self, act, ch):
        self._take(act, "act")


class Attention(Stage):

    def __init__(self, k, jobs):
        super().__init__(k)
        self.jobs = jobs
        n = len(jobs)
        self.s_full = k.scores_full.reserve(n)
        self.s_top = k.scores_topped.reserve(n)
        self.p_done = k.probs_done.reserve(n)
        self.t_full = k.probsT_full.reserve(n)
        self.t_out = k.probsT_out.reserve(n)
        self.o_full = k.out_full.reserve(n)
        self.o_out = k.out_taken.reserve(n)
        for j in jobs:
            j["nk"] = sum(x[1] for x in j["keys"])

    def S(self, j):
        b = 2 * (j % 2)
        return self.k.ps[:, b:b + 2, :].rearrange("p a b -> p (a b)")

    def T(self, j):
        b = 4 + 2 * (j % 2)
        return self.k.ps[:, b:b + 2, :].rearrange("p a b -> p (a b)")

    def O(self, j):
        return self.k.ps[:, 5 + 2 * (j % 2), 320:320 + HD]

    def tensor(self, pe):
        k, jobs = self.k, self.jobs
        for i in range(len(jobs) + 2):
            if i < len(jobs):
                J = jobs[i]
                if i >= 2:
                    pe.wait_ge(k.probs_done.sem, self.p_done + i - 1)
                    pe.wait_ge(k.scores_topped.sem, self.s_top + i - 1)
                at = 0
                for kT, n in J["keys"]:
                    done = 0
                    while done < n:
                        m = min(n - done, 512 - at % 512)
                        last = pe.matmul(self.S(i)[:, at:at + m], J["q"], kT[:, done:done + m], start=True, stop=True)
                        done += m
                        at += m
                last.then_inc(k.scores_full.sem, 1)
            if 1 <= i <= len(jobs):
                j = i - 1
                J = jobs[j]
                pe.wait_ge(k.probs_done.sem, self.p_done + j + 1)
                if j >= 2:
                    pe.wait_ge(k.out_taken.sem, self.o_out + j - 1)
                at = 0
                for v, kn in J["values"]:
                    last = pe.transpose(self.T(j)[0:kn, at * P:(at + 1) * P], k.Pb[:, j % 2, at * P:at * P + kn], k.ident[:, :])
                    at += 1
                last.then_inc(k.probsT_full.sem, 1)
            if i >= 2:
                j = i - 2
                J = jobs[j]
                pe.wait_ge(k.probsT_out.sem, self.t_out + j + 1)
                for a, (v, kn) in enumerate(J["values"]):
                    last = pe.matmul(self.O(j), k.PT[0:kn, j % 2, a * P:(a + 1) * P], v,
                                     start=(a == 0), stop=(a == len(J["values"]) - 1))
                last.then_inc(k.out_full.sem, 1)

    def scalar(self, act, ch):
        k, jobs = self.k, self.jobs
        for i in range(len(jobs) + 1):
            if i < len(jobs):
                J = jobs[i]
                act.wait_ge(k.scores_topped.sem, self.s_top + i + 1)
                if i >= 2:
                    act.wait_ge(k.probsT_full.sem, self.t_full + i - 1)
                src = k.Pb[:, i % 2, 0:J["nk"]] if J["bias"] is not None else self.S(i)[:, 0:J["nk"]]
                if J["sink"] is not None:
                    ch.step(act.activation(k.es[:, i % 4:i % 4 + 1], J["sink"], ACT.Exp, bias=k.nm[:, i % 4:i % 4 + 1]))
                act.activation(k.Pb[:, i % 2, 0:J["nk"]], src, ACT.Exp, bias=k.nm[:, i % 4:i % 4 + 1],
                               accum_out=k.den[:, i % 4:i % 4 + 1]).then_inc(k.probs_done.sem, 1)
            if i >= 1:
                j = i - 1
                J = jobs[j]
                act.wait_ge(k.probsT_full.sem, self.t_full + j + 1)
                if j >= 2:
                    act.wait_ge(k.out_full.sem, self.o_full + j - 1)
                kn = J["values"][0][1]
                n = P * len(J["values"])
                act.activation(k.PT[0:kn, j % 2, 0:n], self.T(j)[0:kn, 0:n], ACT.Copy).then_inc(k.probsT_out.sem, 1)

    def vector(self, dve, ch):
        k, jobs = self.k, self.jobs
        for i in range(len(jobs) + 2):
            if i < len(jobs):
                J = jobs[i]
                c = slice(i % 4, i % 4 + 1)
                if J.get("load"):
                    dve.wait_ge(*J["load"])
                dve.wait_ge(k.scores_full.sem, self.s_full + i + 1)
                if i >= 2:
                    dve.wait_ge(k.probsT_full.sem, self.t_full + i - 1)
                if J["bias"] is not None:
                    ins = dve.tensor_tensor_reduce(out=k.Pb[:, i % 2, 0:J["nk"]], in0=self.S(i)[:, 0:J["nk"]],
                                                   in1=J["bias"], scale=1.0, scalar=-3e38, op0=ALU.add, op1=ALU.max,
                                                   accum_out=k.mx[:, c])
                else:
                    ins = dve.tensor_reduce(k.mx[:, c], self.S(i)[:, 0:J["nk"]], AXX, ALU.max)
                ch.step(ins)
                ch.wait()
                if J["sink"] is not None:
                    ins = dve.tensor_scalar(k.nm[:, c], k.mx[:, c], J["sink"], -1.0, ALU.max, ALU.mult)
                else:
                    ins = dve.tensor_scalar(k.nm[:, c], k.mx[:, c], -1.0, None, ALU.mult)
                ins.then_inc(k.scores_topped.sem, 1)
                if J.get("frees"):
                    ch.step(dve.tensor_copy(k.mx[:, c], k.mx[:, c]))
                    dve.drain().then_inc(k.bias_used.sem, 1)
            if 1 <= i <= len(jobs):
                j = i - 1
                J = jobs[j]
                c = slice(j % 4, j % 4 + 1)
                dve.wait_ge(k.probs_done.sem, self.p_done + j + 1)
                if J["sink"] is not None:
                    ch.step(dve.tensor_tensor(k.den[:, c], k.den[:, c], k.es[:, c], ALU.add))
                    ch.wait()
                ch.step(dve.reciprocal(k.rd[:, c], k.den[:, c]))
                if J["gate"] is not None:
                    ch.wait()
                    ch.step(dve.tensor_tensor(k.rd[:, c], k.rd[:, c], J["gate"], ALU.mult))
            if i >= 2:
                j = i - 2
                J = jobs[j]
                c = slice(j % 4, j % 4 + 1)
                dve.wait_ge(k.out_full.sem, self.o_full + j + 1)
                ch.wait()
                if J["first"]:
                    ins = dve.tensor_scalar(J["out"], self.O(j), k.rd[:, c], None, ALU.mult)
                else:
                    dve.wait_ge(k.out_taken.sem, self.o_out + j)
                    ins = dve.scalar_tensor_tensor(J["out"], self.O(j), k.rd[:, c], J["out"], ALU.mult, ALU.add)
                ins.then_inc(k.out_taken.sem, 1)


class Load(Stage):

    def __init__(self, k, pairs):
        super().__init__(k)
        self.pairs = pairs
        self.base = k.small_landed.reserve(16 * len(pairs))

    def gpsimd(self, pool, ch):
        for dst, src in self.pairs:
            pool.dma_start(dst, src).then_inc(self.k.small_landed.sem, 16)
        pool.wait_ge(self.k.small_landed.sem, self.base + 16 * len(self.pairs))


class ModVectors(Stage):

    def __init__(self, k, A):
        super().__init__(k)
        self.silu = k.step_done.reserve(1)
        self.rows = k.Z[0:2, 0:2 * 6144].rearrange("p (l n) -> p l n", l=2)
        self.layers = []
        for l in range(2):
            self.layers.append(Linear(k, lambda c, t: k.sc[:, c, :], DK, A["mod_w_2"][l], 6144, [0],
                                      self.take(l), owners=["dve"] * 12, rows=2))

    def take(self, l):
        k = self.k

        def fn(eng, name, ch, t, c0, cn, ps):
            return eng.tensor_tensor(self.rows[:, l, c0:c0 + cn], ps[0:2, :], k.modb(l)[:, c0:c0 + cn], ALU.add)
        return fn

    def scalar(self, act, ch):
        k = self.k
        act.activation(k.sc[:, :, :], k.cc[:, :, :], ACT.Silu).then_inc(k.step_done.sem, 1)

    def tensor(self, pe):
        pe.wait_ge(self.k.step_done.sem, self.silu + 1)
        self.layers[0].tensor(pe)
        self.layers[0].banks.taken(pe, 11)
        self.layers[1].tensor(pe)

    def vector(self, dve, ch):
        for d in range(2):
            dve.tensor_copy(self.k.glamask[:, d], self.k.maskf[:, d])
        for lin in self.layers:
            lin.vector(dve, ch)


class ModColumns(Stage):

    def __init__(self, k, rows, dram):
        super().__init__(k)
        self.rows, self.dram = rows, dram
        self.stored = k.small_landed.reserve(32)
        self.banks = Banks(k, ["dve", "dve"])
        self.n = 48

    def tensor(self, pe):
        for l in range(2):
            for c in range(self.n):
                last = pe.transpose(self.banks.bank(l)[:, 2 * c:2 * c + 2], self.rows[:, l, c * P:(c + 1) * P],
                                    self.k.ident[0:2, 0:2])
            self.banks.filled(last)

    def vector(self, dve, ch):
        k = self.k
        for l in range(2):
            self.banks.await_full(dve, l)
            ins = dve.tensor_copy(k.mc[:, l, :, :].rearrange("p n r -> p (n r)"), self.banks.bank(l)[:, 0:2 * self.n])
            self.banks.take(l, ins)
            self.banks.taken(dve, l)
            for w, m in ((0, 1), (1, 4)):
                for r in range(2):
                    dve.scalar_tensor_tensor(k.mg[:, l, w, r, :], k.mc[:, l, m * DK:(m + 1) * DK, r], 1.0,
                                             k.gains[:, 2 + 2 * w + l, :], ALU.add, ALU.mult)

    def gpsimd(self, pool, ch):
        k = self.k
        for l in range(2):
            pool.dma_start(self.dram[l], self.rows[:, l, :]).then_inc(k.small_landed.sem, 16)
        pool.wait_ge(k.small_landed.sem, self.stored + 32)


class BiasRows(Stage):

    def __init__(self, k, table, hot, dram, spread):
        super().__init__(k)
        self.table, self.hot, self.dram, self.spread = table, hot, dram, spread
        self.banks = Banks(k, ["dve"] * 4)
        self.stored = k.small_landed.reserve(16)
        self.units = [(s, c0, min(512, ROW - c0)) for s in range(2) for c0 in (0, 512)]

    def tensor(self, pe):
        for u, (s, c0, cn) in enumerate(self.units):
            self.banks.filled(pe.matmul(self.banks.bank(u)[0:8, 0:cn], self.table[:, 8 * s:8 * s + 8],
                                        self.hot[:, s, c0:c0 + cn], start=True, stop=True))

    def vector(self, dve, ch):
        for u, (s, c0, cn) in enumerate(self.units):
            self.banks.await_full(dve, u)
            self.banks.take(u, dve.tensor_copy(self.buf[:, s, c0:c0 + cn], self.banks.bank(u)[0:8, 0:cn]))

    def gpsimd(self, pool, ch):
        self.banks.taken(pool, 3)
        pool.dma_start(self.dram.rearrange("(a h) n -> h a n", a=2), self.buf).then_inc(self.k.small_landed.sem, 16)
        pool.wait_ge(self.k.small_landed.sem, self.stored + 16)
        rows = bass.AP(tensor=self.dram.tensor, offset=self.dram.offset, ap=[[ROW, 16], [0, P], [1, ROW]])
        pool.dma_start(self.spread, rows).then_inc(self.k.bias_spread, 16)


class Compress(Stage):

    def __init__(self, k, A, kraw, vraw):
        super().__init__(k)
        self.raw = [kraw, vraw]
        self.slots = []
        for w1 in (A["cmp_k_w1"][0], A["cmp_v_w1"][0]):
            for l0 in (0, 16):
                src = w1[l0:l0 + 16].rearrange("l d h -> d l h")
                parts = [((lambda s, g=g: s[64 * g:64 * g + 64, :].rearrange("p (l h) -> p l h", l=16)), src) for g in range(2)]
                self.slots.append(k.rg.plan(parts))
        self.blk_ready = k.step_done.reserve(2)
        self.hid_full = k.psum_full.reserve(2)
        self.hid_done = k.gates_done.reserve(2)
        self.kc_full = k.psum_full.reserve(2)
        self.blk = [k.cmpblk(i) for i in range(2)]
        self.hid = k.cmphid

    def tensor(self, pe):
        k = self.k
        for i in range(2):
            pe.wait_ge(k.step_done.sem, self.blk_ready + i + 1)
            for half in range(2):
                n = self.slots[2 * i + half]
                k.rg.await_landed(pe, n)
                w = k.rg.slot(n).rearrange("p (l h) -> p l h", l=16)
                for l in range(16):
                    for g in range(2):
                        ll = 16 * half + l
                        last = pe.matmul(k.ps[:, 2 * i + g, 0:NCMP], w[64 * g:64 * g + 64, l, :],
                                         self.blk[i][64 * g:64 * g + 64, :, ll], start=(ll == 0), stop=(ll == 31))
                k.rg.released(last)
            pe.drain().then_inc(k.psum_full.sem, 1)
        pe.wait_ge(k.gates_done.sem, self.hid_done + 2)
        for g in range(2):
            last = pe.matmul(k.ps[64 * g:64 * g + 64, 4, 0:NCMP], k.w2[:, 0, :], self.hid[:, 0, g * NCMP:(g + 1) * NCMP],
                             start=True, stop=True)
        last.then_inc(k.psum_full.sem, 1)
        for g in range(2):
            last = pe.matmul(k.ps[0:NCMP, 5, g * HD:(g + 1) * HD], self.hid[:, 1, g * NCMP:(g + 1) * NCMP], k.w2[:, 1, :],
                             start=True, stop=True)
        last.then_inc(k.psum_full.sem, 1)

    def vector(self, dve, ch):
        k = self.k
        for i in range(2):
            c16 = self.raw[i].rearrange("p (c l) -> p c l", l=CMP_STRIDE)
            pos = k.posT[:, :].unsqueeze(1)
            dve.tensor_tensor(self.blk[i][:, :, 0:16], c16[:, 0:NCMP, :], pos[:, :, 0:16].to_broadcast((P, NCMP, 16)), ALU.add)
            dve.tensor_tensor(self.blk[i][:, :, 16:32], c16[:, 1:NCMP + 1, :], pos[:, :, 16:32].to_broadcast((P, NCMP, 16)), ALU.add)
            dve.drain().then_inc(k.step_done.sem, 1)
        dve.wait_ge(k.psum_full.sem, self.kc_full + 1)
        dve.tensor_copy(k.kcmp[:, :], k.ps[:, 4, 0:NCMP])
        dve.wait_ge(k.psum_full.sem, self.kc_full + 2)
        dve.tensor_copy(k.vcmp[0:NCMP, :], k.ps[0:NCMP, 5, 0:2 * HD])

    def scalar(self, act, ch):
        k = self.k
        for i in range(2):
            act.wait_ge(k.psum_full.sem, self.hid_full + i + 1)
            for g in range(2):
                act.activation(self.hid[:, i, g * NCMP:(g + 1) * NCMP], k.ps[:, 2 * i + g, 0:NCMP],
                               ACT.Gelu_apprx_tanh, bias=k.b1[:, i:i + 1])
            act.drain().then_inc(k.gates_done.sem, 1)


class Bias(Stage):

    def __init__(self, k, jobs_of, heads, dram):
        super().__init__(k)
        self.heads, self.dram = heads, dram
        self.landed = k.bias_landed.reserve(16 * len(heads))
        self.used = k.bias_used.reserve(len(heads))
        jobs = []
        for i, h in enumerate(heads):
            js = jobs_of(h, k.bias[:, i % 2, :])
            js[0]["load"] = (k.bias_landed.sem, self.landed + 16 * (i + 1))
            js[-1]["frees"] = True
            jobs += js
        self.att = Attention(k, jobs)

    def gpsimd(self, pool, ch):
        k = self.k
        pool.wait_ge(k.bias_spread, 16)
        for i, h in enumerate(self.heads):
            if i >= 2:
                pool.wait_ge(k.bias_used.sem, self.used + i - 1)
            src = bass.AP(tensor=self.dram.tensor, offset=self.dram.offset + h * P * ROW + 127, ap=[[ROW - 1, P], [1, 512]])
            pool.dma_start(k.bias[:, i % 2, :], src).then_inc(k.bias_landed.sem, 16)
            pool.wait_ge(k.bias_landed.sem, self.landed + 16 * (i + 1))

    def tensor(self, pe):
        self.att.tensor(pe)

    def vector(self, dve, ch):
        self.att.vector(dve, ch)

    def scalar(self, act, ch):
        self.att.scalar(act, ch)


class Sigmoids(Stage):

    def __init__(self, k):
        super().__init__(k)
        self.done = k.step_done.reserve(1)

    def scalar(self, act, ch):
        k = self.k
        act.activation(k.gate3[:, :, :], k.Zb(IN_W)[:, :, GL:GL + 24], ACT.Sigmoid).then_inc(k.step_done.sem, 1)

    def vector(self, dve, ch):
        k = self.k
        dve.wait_ge(k.step_done.sem, self.done + 1)
        g = k.gate3[:, :, :].rearrange("p t (h b) -> p t h b", b=3)[:, :, :, 0]
        v = k.cmpvalid[:, :].unsqueeze(2).to_broadcast((P, ST, 8))
        dve.tensor_tensor(g, g, v, ALU.mult)


class HeadNorm(Stage):

    def __init__(self, k, zw, parts):
        super().__init__(k)
        self.zw, self.parts = zw, parts
        self.asked = k.norm_mean.reserve(len(parts))
        self.got = k.norm_roots.reserve(len(parts))

    def scalar(self, act, ch):
        k = self.k
        for i, (tiles, c0, heads, groups) in enumerate(self.parts):
            act.wait_ge(k.norm_mean.sem, self.asked + i + 1)
            n = len(tiles) * heads
            act.activation(k.hstat[:, 0:n], k.hstat[:, 0:n], ACT.Sqrt).then_inc(k.norm_roots.sem, 1)

    def vector(self, dve, ch):
        k = self.k
        z = k.Zb(self.zw)
        for i, (tiles, c0, heads, groups) in enumerate(self.parts):
            n = len(tiles) * heads
            ch.wait()
            for a, t in enumerate(tiles):
                x = z[:, t, c0:c0 + heads * HD]
                ch.step(dve.tensor_tensor(k.tmp[:, 0:heads * HD], x, x, ALU.mult))
                ch.wait()
                ch.step(dve.tensor_reduce(k.hstat[:, a * heads:(a + 1) * heads],
                                          k.tmp[:, 0:heads * HD].rearrange("p (h d) -> p h d", d=HD), AXX, ALU.add))
                ch.wait()
            dve.tensor_scalar(k.hstat[:, 0:n], k.hstat[:, 0:n], 1.0 / HD, EPS, ALU.mult, ALU.add).then_inc(k.norm_mean.sem, 1)
            dve.wait_ge(k.norm_roots.sem, self.got + i + 1)
            ch.step(dve.reciprocal(k.hstat[:, 0:n], k.hstat[:, 0:n]))
            ch.wait()
            for a, t in enumerate(tiles):
                x = z[:, t, c0:c0 + heads * HD].rearrange("p (h d) -> p h d", d=HD)
                r = k.hstat[:, a * heads:(a + 1) * heads].unsqueeze(2).to_broadcast((P, heads, HD))
                ch.step(dve.tensor_tensor(x, x, r, ALU.mult))
                ch.wait()
                h0 = 0
                for hn, gain in groups:
                    xs = x[:, h0:h0 + hn, :]
                    ch.step(dve.tensor_tensor(xs, xs, gain.unsqueeze(1).to_broadcast((P, hn, HD)), ALU.mult))
                    h0 += hn
                ch.wait()
                if t >= ST:
                    continue
                a2 = k.tmp[:, 0:heads * HD].rearrange("p (h d) -> p h d", d=HD)
                b2 = k.tmp[:, 1152:1152 + heads * HD].rearrange("p (h d) -> p h d", d=HD)
                ch.step(dve.tensor_tensor(a2, x, k.rope[:, t, 0, :].unsqueeze(1).to_broadcast((P, heads, HD)), ALU.mult))
                for ax in range(2):
                    for hf in range(2):
                        o = 32 * ax + 16 * hf
                        s = 32 * ax + 16 * (1 - hf)
                        ch.step(dve.tensor_tensor(b2[:, :, o:o + 16], x[:, :, s:s + 16],
                                                  k.rope[:, t, 1, o:o + 16].unsqueeze(1).to_broadcast((P, heads, 16)), ALU.mult))
                ch.wait()
                ch.step(dve.tensor_tensor(x, a2, b2, ALU.add))
                ch.wait()


class RowNorm(Stage):

    def __init__(self, k, tiles, gain):
        super().__init__(k)
        self.tiles, self.gain = tiles, gain
        self.sq = k.norm_squares.reserve(len(tiles))
        self.mean = k.norm_mean.reserve(1)
        self.rt = k.norm_roots.reserve(1)

    def scalar(self, act, ch):
        k = self.k
        for t in self.tiles:
            act.activation(k.HN[:, t, :], k.X[:, t, :], ACT.Square,
                           accum_out=k.ss[:, t:t + 1]).then_inc(k.norm_squares.sem, 1)
        act.wait_ge(k.norm_mean.sem, self.mean + 1)
        n = len(self.tiles)
        act.activation(k.ss2[:, 0:n], k.ss2[:, 0:n], ACT.Sqrt).then_inc(k.norm_roots.sem, 1)

    def vector(self, dve, ch):
        k = self.k
        n = len(self.tiles)
        dve.wait_ge(k.norm_squares.sem, self.sq + n)
        dve.tensor_scalar(k.ss2[:, 0:n], k.ss[:, 0:n], 1.0 / D, EPS, ALU.mult, ALU.add).then_inc(k.norm_mean.sem, 1)
        dve.wait_ge(k.norm_roots.sem, self.rt + 1)
        ch.step(dve.reciprocal(k.rstd[:, 0:n], k.ss2[:, 0:n]))
        ch.wait()
        for t in self.tiles:
            dve.scalar_tensor_tensor(k.X[:, t, :], k.X[:, t, :], k.rstd[:, t:t + 1], self.gain, ALU.mult, ALU.mult)


class GlaGates(Stage):

    def __init__(self, k):
        super().__init__(k)
        self.units = [(d, p, t0, n) for d in range(2) for p in range(2) for t0, n in ((0, SEQ), (SEQ, CTX))]
        self.banks = Banks(k, ["dve"] * 8)
        self.s = k.step_done.reserve(2)

    def tensor(self, pe):
        k = self.k
        for u, (d, p, t0, n) in enumerate(self.units):
            self.banks.filled(pe.matmul(self.banks.bank(u)[:, 0:n], k.gw[:, d, p * P:(p + 1) * P],
                                        k.lrT[:, t0:t0 + n], start=True, stop=True))

    def scalar(self, act, ch):
        k = self.k
        act.wait_ge(k.step_done.sem, self.s + 1)
        for d in range(2):
            e, z = k.gA if d == 0 else k.gB, k.gb[:, d]
            ch.step(act.activation(e, z, ACT.Abs))
            ch.wait()
            ch.step(act.activation(e, e, ACT.Exp, scale=-1.0))
            ch.wait()
            ch.step(act.activation(e, e, ACT.Ln, bias=1.0))
        ch.wait()
        act.drain().then_inc(k.step_done.sem, 1)

    def vector(self, dve, ch):
        k = self.k
        ch.step(dve.memset(k.gC[:, :, :], 1.0))
        ch.wait()
        ch.step(dve.memset(k.gC.rearrange("p a (n t) -> p (a n) t", t=P)[:, :, 0:1], 0.0))
        for u, (d, p, t0, n) in enumerate(self.units):
            self.banks.await_full(dve, u)
            self.banks.take(u, dve.tensor_scalar(k.gb[:, d, p, t0:t0 + n], self.banks.bank(u)[:, 0:n],
                                                 k.gateb[:, 2 * d + p:2 * d + p + 1], None, ALU.add))
        dve.drain().then_inc(k.step_done.sem, 1)
        dve.wait_ge(k.step_done.sem, self.s + 2)
        for d in range(2):
            e, z = (k.gA, k.gB)[d], k.gb[:, d]
            ch.step(dve.scalar_tensor_tensor(z, z, 0.0, e, ALU.min, ALU.subtract))
            ch.wait()
            ch.step(dve.tensor_scalar(z, z, 1.0 / 16.0, None, ALU.mult))
            ch.wait()
            flat = lambda a: a.rearrange("p a n -> p (a n)")
            ch.step(dve.tensor_tensor_scan(flat(e), flat(k.gC), flat(z), 0.0, ALU.mult, ALU.add))
            ch.wait()
            if d == 0:
                ch.step(dve.tensor_copy(z, e))
            else:
                ch.step(dve.tensor_tensor(z, z, e, ALU.subtract))
                ch.wait()
                zt = z.rearrange("p a (n t) -> p (a n) t", t=P)
                et = e.rearrange("p a (n t) -> p (a n) t", t=P)[:, :, P - 1:P].to_broadcast((P, 12, P))
                ch.step(dve.tensor_tensor(zt, zt, et, ALU.add))
            ch.wait()


class GlaScores(Stage):

    def __init__(self, k, d):
        super().__init__(k)
        self.d = d
        self.banks = Banks(k, ["dve"] * 48)
        self.diff = k.gla_diff.reserve(7)
        self.exp = k.gla_exp.reserve(7)
        self.kpart = k.gla_k.reserve(7)
        self.qk = k.gla_qk.reserve(7)

    def half(self, x, h, side):
        return x.rearrange("p a (n s t) -> p (a n) s t", s=2, t=h)[:, :, side, :]

    def tensor(self, pe):
        k = self.k
        for lv in range(-1, 7):
            if lv >= 0:
                pe.wait_ge(k.gla_qk.sem, self.qk + lv + 1)
                pe.wait_ge(k.gla_k.sem, self.kpart + lv + 1)
            for v in range(NT):
                u, odd = (lv + 1) * NT + v, v % 2
                self.banks.may_fill(pe, u)
                for j in range(4):
                    r, p, t = slice(64 * odd, 64 * odd + 64), j % 2, 2 * (v // 2) + j // 2
                    c = slice(t * P, (t + 1) * P)
                    if lv < 0:
                        a, b = k.gkT[r, p, c], k.gqT[r, p, c]
                    else:
                        x = (k.gB, k.gC)[lv % 2]
                        a = b = x[r, p, c]
                    last = pe.matmul(self.banks.bank(u)[:, j * P:(j + 1) * P], a, b, start=True, stop=True)
                self.banks.filled(last)

    def scalar(self, act, ch):
        k = self.k
        for lv in range(7):
            act.wait_ge(k.gla_diff.sem, self.diff + lv + 1)
            act.activation(k.gA, k.gA, ACT.Exp).then_inc(k.gla_exp.sem, 1)

    def gpsimd(self, pool, ch):
        k = self.k
        s_side = self.d
        for lv in range(7):
            h = 1 << lv
            pool.wait_ge(k.gla_exp.sem, self.exp + lv + 1)
            if lv >= 2:
                self.banks.taken(pool, (lv - 1) * NT + NT - 1)
            x = (k.gB, k.gC)[lv % 2]
            pool.tensor_tensor(self.half(x, h, s_side), self.half(k.gkT, h, s_side), self.half(k.gA, h, s_side),
                               ALU.mult).then_inc(k.gla_k.sem, 1)

    def vector(self, dve, ch):
        k, d = self.k, self.d
        b = k.gb[:, d]
        t_side, s_side = 1 - d, d

        def prepare(lv):
            h = 1 << lv
            if lv >= 1:
                dve.wait_ge(k.gla_k.sem, self.kpart + lv)
            seam = self.half(b, h, s_side)[:, :, h - 1:h] if d == 0 else self.half(b, h, s_side)[:, :, 0:1]
            seam = seam.to_broadcast((P, 2 * NT * P // (2 * h), h))
            ch.wait()
            dve.tensor_tensor(self.half(k.gA, h, t_side), self.half(b, h, t_side), seam, ALU.subtract)
            dve.tensor_tensor(self.half(k.gA, h, s_side), seam, self.half(b, h, s_side), ALU.subtract)
            dve.drain().then_inc(k.gla_diff.sem, 1)
            dve.wait_ge(k.gla_exp.sem, self.exp + lv + 1)
            x = (k.gB, k.gC)[lv % 2]
            if lv >= 2:
                dve.wait_ge(k.psum_full.sem, self.banks.full + lv * NT)
            ch.step(dve.tensor_tensor(self.half(x, h, t_side), self.half(k.gqT, h, t_side), self.half(k.gA, h, t_side), ALU.mult))
            ch.wait()
            dve.drain().then_inc(k.gla_qk.sem, 1)

        prepare(0)
        for lv in range(-1, 7):
            if 0 <= lv < 6:
                prepare(lv + 1)
            for v in range(NT):
                u = (lv + 1) * NT + v
                self.banks.await_full(dve, u)
                for a in range(2):
                    ps = self.banks.bank(u)[:, 256 * a:256 * a + 256].rearrange("p (h t) -> p h t", h=2)
                    acc = k.gacc[:, 2 * (v // 2) + a, v % 2]
                    if lv < 0:
                        ins = dve.tensor_tensor(acc, ps, k.ident[:, :].unsqueeze(1).to_broadcast((P, 2, P)), ALU.mult)
                        continue
                    if v == 0 and a == 0:
                        self.banks.taken(dve, u - 1)
                    ins = dve.copy_predicated(acc, k.glamask[:, d, lv, :].unsqueeze(1).to_broadcast((P, 2, P)), ps)
                self.banks.take(u, dve.drain())


class GlaDecayed(Stage):

    def __init__(self, k, d):
        super().__init__(k)
        self.d = d
        self.s1 = k.gla_diff.reserve(1)
        self.s2 = k.gla_exp.reserve(2)
        self.s3 = k.gla_qk.reserve(2)
        self.banks = Banks(k, alternate(2 * NT))

    def scalar(self, act, ch):
        k, d = self.k, self.d
        act.activation(k.gA, k.gb[:, d], ACT.Exp).then_inc(k.gla_exp.sem, 1)
        act.wait_ge(k.gla_diff.sem, self.s1 + 1)
        act.activation(k.gC, k.gC, ACT.Exp).then_inc(k.gla_exp.sem, 1)
        act.wait_ge(k.gla_qk.sem, self.s3 + 2)
        self._take(act, "act")

    def vector(self, dve, ch):
        k, d = self.k, self.d
        b = k.gb[:, d]
        bt = b.rearrange("p a (n t) -> p (a n) t", t=P)
        end = bt[:, :, P - 1:P] if d == 0 else bt[:, :, 0:1]
        ct = k.gC.rearrange("p a (n t) -> p (a n) t", t=P)
        dve.tensor_tensor(ct, end.to_broadcast((P, 12, P)), bt, ALU.subtract).then_inc(k.gla_diff.sem, 1)
        dve.wait_ge(k.gla_exp.sem, self.s2 + 1)
        at = k.gA.rearrange("p a (n t) -> p (a n) t", t=P)
        dve.tensor_copy(k.gdecay[:, :].unsqueeze(2), at[:, :, P - 1:P] if d == 0 else at[:, :, 0:1])
        dve.tensor_tensor(k.gB, k.gqT, k.gA, ALU.mult)
        dve.wait_ge(k.gla_exp.sem, self.s2 + 2)
        dve.tensor_tensor(k.gC, k.gkT, k.gC, ALU.mult)
        dve.drain().then_inc(k.gla_qk.sem, 2)
        dve.wait_ge(k.gla_qk.sem, self.s3 + 2)
        self._take(dve, "dve")

    def tensor(self, pe):
        k = self.k
        pe.wait_ge(k.gla_qk.sem, self.s3 + 2)
        for u in range(2 * NT):
            t, p = u // 2, u % 2
            self.banks.may_fill(pe, u)
            self.banks.filled(pe.transpose(self.banks.bank(u)[:, 0:P], k.gC[:, p, t * P:(t + 1) * P], k.ident[:, :]))

    def _take(self, eng, name):
        for u in range(2 * NT):
            t, p = u // 2, u % 2
            if self.banks.owners[u] == name:
                self.banks.await_full(eng, u)
                self.banks.take(u, copy(eng, name, self.k.gkh[:, t, p, :], self.banks.bank(u)[:, 0:P]))


class GlaScan(Stage):

    def __init__(self, k, d):
        super().__init__(k)
        self.d = d
        self.order = [4, 5, 0, 1, 2, 3] if d == 0 else [5, 4, 3, 2, 1, 0]
        self.o = Banks(k, ["dve"] * (2 * NT), 4, 4, lane=1)
        self.s = Banks(k, ["dve"] * NT, 2, 2)

    def tensor(self, pe):
        k = self.k
        z = k.Zb(EV_W)
        for i, t in enumerate(self.order):
            v = lambda h: z[:, t, GV + h * GDV:GV + (h + 1) * GDV]
            self.s.may_fill(pe, i)
            for h in range(GH):
                r = 64 * (h % 2)
                last = pe.matmul(self.s.bank(i)[r:r + 64, (h // 2) * P:(h // 2) * P + GDV],
                                 k.gkh[:, t, h // 2, r:r + 64], v(h), start=True, stop=True)
            self.s.filled(last)
            if i:
                self.s.taken(pe, i - 1)
            for odd in range(2):
                self.o.may_fill(pe, 2 * i + odd)
                for p in range(2):
                    r = slice(64 * odd, 64 * odd + 64)
                    out = self.o.bank(2 * i + odd)[:, p * GDV:(p + 1) * GDV]
                    last = pe.matmul(out, k.gacc[:, t, odd, p, :], v(2 * p + odd), start=True, stop=(i == 0))
                    if i:
                        last = pe.matmul(out, k.gB[r, p, t * P:(t + 1) * P], k.gS[r, (i - 1) % 2, p, :],
                                         start=False, stop=True)
                self.o.filled(last)

    def vector(self, dve, ch):
        k = self.k

        def outputs(i):
            t = self.order[i]
            for odd in range(2):
                self.o.await_full(dve, 2 * i + odd)
                to = k.gO[:, t, :].rearrange("p (a o n) -> p a o n", a=2, o=2)[:, :, odd, :]
                new = self.o.bank(2 * i + odd)[:, 0:2 * GDV].rearrange("p (a n) -> p a n", a=2)
                if self.d == 0:
                    ins = dve.tensor_copy(to, new)
                else:
                    ins = dve.tensor_tensor(to, new, to, ALU.add)
                self.o.take(2 * i + odd, ins)

        for i, t in enumerate(self.order):
            if i:
                outputs(i - 1)
                self.s.taken(dve, i - 1)
            self.s.await_full(dve, i)
            for p in range(2):
                new = self.s.bank(i)[:, p * P:(p + 1) * P]
                if i == 0:
                    dve.tensor_copy(k.gS[:, 0, p, :], new)
                else:
                    dve.scalar_tensor_tensor(k.gS[:, i % 2, p, :], k.gS[:, (i - 1) % 2, p, :],
                                             k.gdecay[:, p * NT + t:p * NT + t + 1], new, ALU.mult, ALU.add)
            self.s.take(i, dve.drain())
        outputs(NT - 1)


class GlaOutput(Stage):

    def __init__(self, k):
        super().__init__(k)
        self.s = k.step_done.reserve(2)
        self.r = k.norm_roots.reserve(1)

    def scalar(self, act, ch):
        k = self.k
        z = k.Zb(EV_W)
        act.activation(z[:, :, GR:GR + 512], z[:, :, GR:GR + 512], ACT.Silu).then_inc(k.step_done.sem, 1)
        act.wait_ge(k.step_done.sem, self.s + 2)
        act.activation(k.hstat[:, 0:NT * GH], k.hstat[:, 0:NT * GH], ACT.Sqrt).then_inc(k.norm_roots.sem, 1)

    def vector(self, dve, ch):
        k = self.k
        z = k.Zb(EV_W)
        n = NT * GH
        o = k.gO.rearrange("p t (h d) -> p (t h) d", d=GDV)
        sq = k.T[:, 0:n * GDV].rearrange("p (n d) -> p n d", d=GDV)
        st = k.hstat[:, 0:n]
        ch.step(dve.tensor_tensor(sq, o, o, ALU.mult))
        ch.wait()
        ch.step(dve.tensor_reduce(st, sq, AXX, ALU.add))
        ch.wait()
        ch.step(dve.tensor_scalar(st, st, 1.0 / GDV, EPS, ALU.mult, ALU.add))
        ch.wait()
        dve.wait_ge(k.step_done.sem, self.s + 1)
        dve.drain().then_inc(k.step_done.sem, 1)
        dve.wait_ge(k.norm_roots.sem, self.r + 1)
        ch.step(dve.reciprocal(st, st))
        ch.wait()
        ch.step(dve.tensor_tensor(o, o, st.unsqueeze(2).to_broadcast((P, n, GDV)), ALU.mult))
        ch.wait()
        ch.step(dve.tensor_tensor(o, o, k.ggain[:, :].unsqueeze(1).to_broadcast((P, n, GDV)), ALU.mult))
        ch.wait()
        dve.tensor_tensor(z[:, :, 0:512], k.gO, z[:, :, GR:GR + 512], ALU.mult)


class Router(Stage):

    def __init__(self, k, l, tiles, rows):
        super().__init__(k)
        self.l, self.tiles, self.rows_out = l, tiles, rows
        self.banks = Banks(k, ["dve"] * len(tiles), 0, 6)
        self.rows = Banks(k, ["act"] * (2 * len(tiles)), 6, 2, lane=1)
        self.e = k.step_done.reserve(4)
        self.stored = k.rows_stored.reserve(16 * len(tiles))
        self.consts = k.small_landed.reserve(48 + 16 * (1 + (len(tiles) > ST)))

    def gpsimd(self, pool, ch):
        k = self.k
        loads = [(k.mo.iota, k.C["iota"]), (k.mo.token, k.C["token"]), (k.mo.before, k.C["before"])]
        loads += k.gate_loads(self.l, 5, 1 + (len(self.tiles) > ST))
        for dst, src in loads:
            pool.dma_start(dst, src).then_inc(k.small_landed.sem, 16)
        pool.wait_ge(k.small_landed.sem, self.consts + 16 * len(loads))

    def tensor(self, pe):
        k = self.k
        for u, t in enumerate(self.tiles):
            for c in range(DK):
                last = pe.matmul(self.banks.bank(u)[:, 0:20], k.HT[:, c, t * P:(t + 1) * P], k.rw[:, self.l, c, :],
                                 start=(c == 0), stop=(c == DK - 1))
            self.banks.filled(last)
        for v in range(2 * len(self.tiles)):
            t, hf = self.tiles[v // 2], v % 2
            self.rows.may_fill(pe, v)
            for c in range(4):
                last = pe.transpose(self.rows.bank(v)[:, c * P:(c + 1) * P],
                                    k.HT[:, 4 * hf + c, t * P:(t + 1) * P], k.ident[:, :])
            self.rows.filled(last)

    def scalar(self, act, ch):
        k, n = self.k, len(self.tiles)

        def rows_of(i):
            for hf in range(2):
                v = 2 * i + hf
                self.rows.await_full(act, v)
                self.rows.take(v, act.activation(k.HN[:, i, hf * 512:(hf + 1) * 512], self.rows.bank(v), ACT.Copy))
            self.rows.taken(act, 2 * i + 1)
            t = self.tiles[i]
            act.dma_start(self.rows_out[t * P:(t + 1) * P, :], k.HN[:, i, :]).then_inc(k.rows_stored.sem, 16)

        for i in range(2):
            act.wait_ge(k.step_done.sem, self.e + 2 * i + 1)
            x = k.rG[:, 0:n, :] if i == 0 else k.rE[:, 0:n, :]
            act.activation(x, x, ACT.Exp).then_inc(k.step_done.sem, 1)
            for j in range(i * n // 2, (i + 1) * n // 2):
                rows_of(j)
        act.wait_ge(k.rows_stored.sem, self.stored + 16 * n)

    def vector(self, dve, ch):
        k, n = self.k, len(self.tiles)

        def do(ins):
            ch.step(ins)
            ch.wait()

        for u, t in enumerate(self.tiles):
            self.banks.await_full(dve, u)
            self.banks.take(u, dve.tensor_tensor(k.rL[:, u, :], self.banks.bank(u)[:, 0:20], k.rb[:, self.l, :], ALU.add))
            self.banks.taken(dve, u)
        m, left = k.rs[:, 0, 0:n], k.rs[:, 2, 0:n]

        def over4(x):
            return x.unsqueeze(2).to_broadcast((P, n, 4))

        def first_max(x, onehot):
            do(dve.tensor_reduce(m, x, AXX, ALU.max))
            do(dve.tensor_tensor(onehot, x, over4(m), ALU.is_equal))
            do(dve.memset(left, 1.0))
            for j in range(4):
                do(dve.tensor_tensor(onehot[:, :, j], onehot[:, :, j], left, ALU.mult))
                do(dve.tensor_tensor(left, left, onehot[:, :, j], ALU.subtract))

        first_max(k.rL[:, 0:n, 0:4], k.rO[:, 0:n, :])
        do(dve.tensor_tensor(k.rG[:, 0:n, :], k.rL[:, 0:n, 0:4], over4(m), ALU.subtract))
        dve.drain().then_inc(k.step_done.sem, 1)
        E = k.rE[:, 0:n, :]
        for g in range(4):
            lg = k.rL[:, 0:n, 4 + 4 * g:8 + 4 * g]
            hot = k.rO[:, 0:n, g:g + 1].to_broadcast((P, n, 4))
            if g == 0:
                do(dve.tensor_tensor(E, lg, hot, ALU.mult))
            else:
                do(dve.tensor_tensor(k.rA[:, 0:n, :], lg, hot, ALU.mult))
                do(dve.tensor_tensor(E, E, k.rA[:, 0:n, :], ALU.add))
        do(dve.tensor_reduce(m, E, AXX, ALU.max))
        do(dve.tensor_tensor(E, E, over4(m), ALU.subtract))
        dve.wait_ge(k.step_done.sem, self.e + 2)
        dve.drain().then_inc(k.step_done.sem, 1)
        do(dve.tensor_reduce(k.rs[:, 3, 0:n], k.rG[:, 0:n, :], AXX, ALU.add))
        do(dve.reciprocal(k.rs[:, 3, 0:n], k.rs[:, 3, 0:n]))
        dve.wait_ge(k.step_done.sem, self.e + 4)
        a, b = k.rA[:, 0:n, :], k.rB[:, 0:n, :]
        first_max(E, a)
        do(dve.scalar_tensor_tensor(k.rG[:, 0:n, :], a, -2.0, E, ALU.mult, ALU.add))
        first_max(k.rG[:, 0:n, :], b)
        wa, wb = k.mo.weight[:, 0, 0:n], k.mo.weight[:, 1, 0:n]
        for x, w in ((a, wa), (b, wb)):
            do(dve.tensor_tensor(k.rG[:, 0:n, :], x, E, ALU.mult))
            do(dve.tensor_reduce(w, k.rG[:, 0:n, :], AXX, ALU.add))
        do(dve.tensor_tensor(m, wa, wb, ALU.add))
        do(dve.reciprocal(m, m))
        do(dve.tensor_tensor(m, m, k.rs[:, 3, 0:n], ALU.mult))
        dve.tensor_tensor(wa, wa, m, ALU.mult)
        dve.tensor_tensor(wb, wb, m, ALU.mult)
        for i, x in enumerate((a, b)):
            for g in range(4):
                dve.tensor_tensor(k.mo.chosen[:, i, 0:n, 4 * g:4 * g + 4], x,
                                  k.rO[:, 0:n, g:g + 1].to_broadcast((P, n, 4)), ALU.mult)


def tiles_bound(tokens):
    return (2 * tokens - NEXP) // P + NEXP


class Dispatch(Stage):

    def __init__(self, k, n):
        super().__init__(k)
        self.n, self.m = n, tiles_bound(n * P)
        self.banks = Banks(k, ["dve"] * 3)
        self.hot = k.step_done.reserve(2)
        self.ready = k.lists_ready.reserve(1)

    def tensor(self, pe):
        k, n, mo = self.k, self.n, self.k.mo
        pe.wait_ge(k.step_done.sem, self.hot + 1)
        both = mo.either[:, 0:n, :].rearrange("p n e -> p (n e)")
        self.banks.filled(pe.matmul(self.banks.bank(0)[:, 0:16 * n], mo.before, both, start=True, stop=True))
        self.banks.filled(pe.matmul(self.banks.bank(1)[:, 0:16 * n], mo.ones, both, start=True, stop=True))
        pe.wait_ge(k.step_done.sem, self.hot + 2)
        for u in range(2 * n):
            last = pe.matmul(self.banks.bank(2)[:, 0:self.m], mo.row_hot[:, u, :], mo.tile_hot[:, u, 0:self.m],
                             start=(u == 0), stop=(u == 2 * n - 1))
        self.banks.filled(last)

    def vector(self, dve, ch):
        k, n, mo, m = self.k, self.n, self.k.mo, self.m

        def do(ins):
            ch.step(ins)
            ch.wait()

        def over_tokens(x):
            return x.unsqueeze(1).to_broadcast((P, n, NEXP))
        either, rank, before, whole, tile, tmp = (x[:, 0:n, :] for x in (mo.either, mo.rank, mo.prior, mo.whole, mo.tile, mo.tmp))
        dve.tensor_tensor(either, mo.chosen[:, 0, 0:n, :], mo.chosen[:, 1, 0:n, :], ALU.add)
        do(dve.memset(mo.ones, 1.0))
        dve.drain().then_inc(k.step_done.sem, 1)
        do(dve.memset(before[:, 0, :], 0.0))
        self.banks.await_full(dve, 1)
        total = self.banks.bank(1)[:, 0:16 * n].rearrange("p (n e) -> p n e", n=n)
        for i in range(1, n):
            do(dve.tensor_tensor(before[:, i, :], total[:, i - 1, :], before[:, i - 1, :], ALU.add))
        self.banks.take(0, dve.tensor_tensor(rank, self.banks.bank(0)[:, 0:16 * n].rearrange("p (n e) -> p n e", n=n),
                                             before, ALU.add))
        self.banks.take(1, dve.tensor_tensor(mo.count, total[:, n - 1, :], before[:, n - 1, :], ALU.add))
        self.banks.taken(dve, 1)
        do(dve.tensor_scalar(mo.tiles, mo.count, 0.0, None, ALU.is_gt))
        for i in range(1, n):
            do(dve.scalar_tensor_tensor(mo.tiles, mo.count, float(P * i), mo.tiles, ALU.is_gt, ALU.add))
        do(dve.tensor_tensor_scan(mo.end, mo.ones[:, 0:NEXP], mo.tiles, 0.0, ALU.mult, ALU.add))
        do(dve.tensor_tensor(mo.first, mo.end, mo.tiles, ALU.subtract))
        do(dve.tensor_scalar(whole, rank, float(P), None, ALU.is_ge))
        for i in range(2, n):
            do(dve.tensor_scalar(tmp, rank, float(P * i), None, ALU.is_ge))
            do(dve.tensor_tensor(whole, whole, tmp, ALU.add))
        do(dve.tensor_tensor(tile, whole, over_tokens(mo.first), ALU.add))
        do(dve.tensor_scalar(tmp, whole, -float(P), None, ALU.mult))
        do(dve.tensor_tensor(rank, rank, tmp, ALU.add))
        for i in range(2):
            for x, to in ((tile, mo.at_tile), (rank, mo.at_row)):
                do(dve.tensor_tensor(tmp, mo.chosen[:, i, 0:n, :], x, ALU.mult))
                do(dve.tensor_reduce(to[:, i, 0:n], tmp, AXX, ALU.add))
        for i in range(2):
            for t in range(n):
                dve.tensor_scalar(mo.row_hot[:, n * i + t, :], mo.iota, mo.at_row[:, i, t:t + 1], None, ALU.is_equal)
                dve.tensor_scalar(mo.tile_hot[:, n * i + t, 0:m], mo.iota[:, 0:m], mo.at_tile[:, i, t:t + 1],
                                  mo.token[:, t:t + 1], ALU.is_equal, ALU.mult)
        dve.drain().then_inc(k.step_done.sem, 1)
        ended = mo.ended[:, 0:m, :]
        do(dve.tensor_tensor(ended, mo.iota[:, 0:m].unsqueeze(2).to_broadcast((P, m, NEXP)),
                             mo.end.unsqueeze(1).to_broadcast((P, m, NEXP)), ALU.is_ge))
        do(dve.tensor_reduce(mo.expert[:, 0:m], ended, AXX, ALU.add))
        do(dve.tensor_scalar(mo.expert[:, 0:m], mo.expert[:, 0:m], float(NEXP - 1), None, ALU.min))
        dve.tensor_copy(k.tile_expert[:, 0:m], mo.expert[:, 0:m])
        do(dve.scalar_tensor_tensor(mo.at_row[:, :, 0:n], mo.at_tile[:, :, 0:n], float(P), mo.at_row[:, :, 0:n], ALU.mult, ALU.add))
        dve.tensor_copy(k.token_rows[:, :, 0:n], mo.at_row[:, :, 0:n])
        dve.drain().then_inc(k.lists_ready.sem, 1)
        self.banks.await_full(dve, 2)
        self.banks.take(2, dve.tensor_copy(k.row_token[:, 0:m], self.banks.bank(2)[:, 0:m]))


class ExpertLoads:

    def __init__(self, k, l, m, A, ready):
        self.k, self.m, self.ready = k, m, ready
        self.w = [A[n][l].rearrange("g e d n -> (g e) d n") for n in ("exp_w_gate_2", "exp_w_up_2", "exp_w_down_2")]
        self.n0 = len(k.rg.loads)
        for t in range(m):
            for j in range(3):
                r = len(k.rg.loads) % SLOTS
                k.rg.count[r] += (32, 32, 16)[j]
                k.rg.landed_at.append(k.rg.count[r])
                k.rg.loads.append(self if t + j == 0 else None)

    def landed(self, pe, b, p, j):
        n = self.n0 + 3 * p + j
        pe.wait_ge(self.k.landed[n % SLOTS], self.k.rg.landed_at[n] + b * (32, 32, 16)[j])

    def slot(self, p, j):
        return self.k.rg.slot(self.n0 + 3 * p + j)

    def load(self, sp, b, p):
        k = self.k
        e = sp.value_load(k.tile_expert[0:1, bass.ds(2 * b + p, 1)], min_val=0, max_val=NEXP - 1)
        gate, up, down = (w[bass.ds(e, 1)] for w in self.w)
        for j in range(3):
            n = self.n0 + 3 * p + j
            sem, slot = k.landed[n % SLOTS], self.slot(p, j)
            sp.wait_ge(k.weights_used, n - SLOTS + 1 + 6 * b)
            if j < 2:
                to = slot.rearrange("p (c a n) -> p c a n", c=4, a=2)
                for i, w in enumerate((gate, up)):
                    src = w[:, j * 512:(j + 1) * 512, :].rearrange("o (c p) n -> p (o c) n", p=P)
                    sp.dma_start(to[:, :, i, :], src).then_inc(sem, 16)
            else:
                sp.dma_start(slot.rearrange("p (c n) -> p c n", c=2),
                             down.rearrange("o (c p) n -> p (o c) n", p=P)).then_inc(sem, 16)

    def fill(self, sp):
        sp.wait_ge(self.k.lists_ready.sem, self.ready + 1)
        with sp.Fori(0, self.m // 2) as b:
            self.load(sp, b, 0)
            self.load(sp, b, 1)
        if self.m % 2:
            self.load(sp, self.m // 2, 0)


class Experts(Stage):

    def __init__(self, k, l, n, A, dispatch, rows, y):
        super().__init__(k)
        self.m, self.rows, self.y = dispatch.m, rows, y
        self.w = ExpertLoads(k, l, self.m, A, dispatch.ready)
        m = self.m
        def per_tile(name):
            return k.moe_sems[name].sem, k.moe_sems[name].reserve(m)
        self.x_transposed, self.x_out_act, self.x_out_dve = per_tile("x_transposed"), per_tile("x_out_act"), per_tile("x_out_dve")
        self.gu_full, self.silu_ready, self.hid_ready = per_tile("gu_full"), per_tile("silu_ready"), per_tile("hid_ready")
        self.hid_transposed, self.hid_out = per_tile("hid_transposed"), per_tile("hid_out")
        self.y_full, self.y_out_act, self.y_out_dve = per_tile("y_full"), per_tile("y_out_act"), per_tile("y_out_dve")
        self.x_landed = [(k.x_landed[p].sem, k.x_landed[p].reserve(16 * ((m + 1 - p) // 2))) for p in range(2)]
        self.y_stored = [(k.y_stored[p].sem, k.y_stored[p].reserve(16 * ((m + 1 - p) // 2))) for p in range(2)]

    @staticmethod
    def after(eng, s, tiles):
        eng.wait_ge(s[0], s[1] + tiles)

    def run(self, eng, prologue, step, epilogue):
        prologue()
        for b in range(2):
            step(b, 0, False)
            step(b, 1, False)
        with eng.Fori(2, (self.m - 1) // 2) as b:
            step(b, 0, False)
            step(b, 1, False)
        for t in range(2 * ((self.m - 1) // 2), self.m):
            step(t // 2, t % 2, t == self.m - 1)
        epilogue(self.m // 2, self.m % 2)

    def tensor(self, pe):
        k, w = self.k, self.w
        ps, mo = k.ps, k.mo

        def x_transposes(b, p):
            t = 2 * b + p
            pe.wait_ge(self.x_landed[p][0], self.x_landed[p][1] + 16 * b + 16)
            for c in range(DK):
                last = pe.transpose(ps[:, 2 + c // 4, (c % 4) * P:(c % 4 + 1) * P], mo.xg[:, p, c * P:(c + 1) * P], k.ident[:, :])
            last.then_inc(self.x_transposed[0], 1)

        def down(b, p):
            t = 2 * b + p
            w.landed(pe, b, p, 2)
            self.after(pe, self.hid_out, t + 1)
            if not (isinstance(t, int) and t == 0):
                self.after(pe, self.y_out_act, t)
                self.after(pe, self.y_out_dve, t)
            wd = w.slot(p, 2).rearrange("p (c n) -> p c n", c=2)
            for hf in range(2):
                for c in range(2):
                    last = pe.matmul(ps[:, 5 + hf, :], mo.hidT[:, p, c, :], wd[:, c, hf * 512:(hf + 1) * 512],
                                     start=(c == 0), stop=(c == 1))
            last.then_inc(self.y_full[0], 1)

        def step(b, p, final):
            t = 2 * b + p
            peeled = isinstance(t, int)
            w.landed(pe, b, p, 0)
            w.landed(pe, b, p, 1)
            self.after(pe, self.x_out_act, t + 1)
            self.after(pe, self.x_out_dve, t + 1)
            if not (peeled and t < 2):
                self.after(pe, self.hid_ready, t - 1)
            for c in range(DK):
                g = w.slot(p, c // 4).rearrange("p (c n) -> p c n", c=4)
                last = pe.matmul(ps[:, p, :], mo.xT[:, p, c, :], g[:, c % 4, :], start=(c == 0), stop=(c == DK - 1))
            last.then_inc(self.gu_full[0], 1)
            if not final:
                x_transposes(b + (p == 1), 1 - p)
            first = peeled and t == 0
            if not first:
                down(b - (p == 0), 1 - p)
            pe.drain().then_inc(k.weights_used, 2 if first else 3)
            self.after(pe, self.hid_ready, t + 1)
            for c in range(2):
                last = pe.transpose(ps[:, 4 + 3 * p, c * P:(c + 1) * P], mo.hid[:, p, c * P:(c + 1) * P], k.ident[:, :])
            last.then_inc(self.hid_transposed[0], 1)

        def epilogue(b, p):
            down(b - (p == 0), 1 - p)
            pe.drain().then_inc(k.weights_used, 1)
        self.run(pe, lambda: x_transposes(0, 0), step, epilogue)

    def y_buffer_free(self, eng, b, p):
        if not (isinstance(b, int) and b == 0):
            eng.wait_ge(self.y_stored[p][0], self.y_stored[p][1] + 16 * b)

    def scalar(self, act, ch):
        k, mo, ps = self.k, self.k.mo, self.k.ps

        def x_out(b, p):
            self.after(act, self.x_transposed, 2 * b + p + 1)
            act.activation(mo.xT[:, p, 0:4, :].rearrange("p c n -> p (c n)"), ps[:, 2, :], ACT.Copy).then_inc(self.x_out_act[0], 1)

        def y_out(b, p):
            self.after(act, self.y_full, 2 * b + p + 1)
            self.y_buffer_free(act, b, p)
            act.activation(mo.ysb[:, p, 0:512], ps[:, 5, :], ACT.Copy).then_inc(self.y_out_act[0], 1)

        def y_store(b, p):
            t = 2 * b + p
            self.after(act, self.y_out_act, t + 1)
            self.after(act, self.y_out_dve, t + 1)
            to = self.y[bass.ds(t, 1)].rearrange("o p n -> p (o n)")
            act.dma_start(to, mo.ysb[:, p, :]).then_inc(self.y_stored[p][0], 16)

        def step(b, p, final):
            t = 2 * b + p
            peeled = isinstance(t, int)
            self.after(act, self.gu_full, t + 1)
            if not (peeled and t < 2):
                self.after(act, self.hid_ready, t - 1)
            act.activation(mo.silu[:, p, :], ps[:, p, 0:EXH], ACT.Silu).then_inc(self.silu_ready[0], 1)
            if not final:
                x_out(b + (p == 1), 1 - p)
            first = peeled and t == 0
            if not first:
                y_out(b - (p == 0), 1 - p)
            self.after(act, self.hid_transposed, t + 1)
            act.activation(mo.hidT[:, p].rearrange("p c n -> p (c n)"), ps[:, 4 + 3 * p, 0:EXH], ACT.Copy).then_inc(self.hid_out[0], 1)
            if not first:
                y_store(b - (p == 0), 1 - p)

        def epilogue(b, p):
            y_out(b - (p == 0), 1 - p)
            y_store(b - (p == 0), 1 - p)
            for q in range(2):
                act.wait_ge(self.y_stored[q][0], self.y_stored[q][1] + 16 * ((self.m + 1 - q) // 2))
        self.run(act, lambda: x_out(0, 0), step, epilogue)

    def vector(self, dve, ch):
        k, mo, ps = self.k, self.k.mo, self.k.ps

        def x_out(b, p):
            self.after(dve, self.x_transposed, 2 * b + p + 1)
            dve.tensor_copy(mo.xT[:, p, 4:8, :].rearrange("p c n -> p (c n)"), ps[:, 3, :]).then_inc(self.x_out_dve[0], 1)

        def y_out(b, p):
            self.after(dve, self.y_full, 2 * b + p + 1)
            self.y_buffer_free(dve, b, p)
            dve.tensor_copy(mo.ysb[:, p, 512:1024], ps[:, 6, :]).then_inc(self.y_out_dve[0], 1)

        def step(b, p, final):
            t = 2 * b + p
            peeled = isinstance(t, int)
            self.after(dve, self.silu_ready, t + 1)
            if not (peeled and t < 2):
                self.after(dve, self.hid_transposed, t - 1)
            dve.tensor_tensor(mo.hid[:, p, :], ps[:, p, EXH:2 * EXH], mo.silu[:, p, :], ALU.mult).then_inc(self.hid_ready[0], 1)
            if not final:
                x_out(b + (p == 1), 1 - p)
            if not (peeled and t == 0):
                y_out(b - (p == 0), 1 - p)
        self.run(dve, lambda: x_out(0, 0), step, lambda b, p: y_out(b - (p == 0), 1 - p))

    def gpsimd(self, pool, ch):
        k = self.k

        def gather(t):
            if t >= 2:
                self.after(pool, self.x_transposed, t - 1)
            pool.indirect_dma_start(k.mo.xg[:, t % 2, :], None, self.rows,
                                    bass.IndirectOffsetOnAxis(ap=k.row_token[:, t:t + 1], axis=0)
                                    ).then_inc(self.x_landed[t % 2][0], 16)
        for t in range(self.m):
            gather(t)


class Combine(Stage):

    def __init__(self, k, tiles, y):
        super().__init__(k)
        self.tiles, self.y = tiles, y
        n = len(tiles)
        self.landed = [k.x_landed[p].reserve(32 * ((n + 1 - p) // 2)) for p in range(2)]
        self.half = k.half_done.reserve(n)
        self.done = k.both_done.reserve(n)

    def gpsimd(self, pool, ch):
        k, mo = self.k, self.k.mo
        for i, t in enumerate(self.tiles):
            if i >= 2:
                pool.wait_ge(k.both_done.sem, self.done + i - 1)
            for s in range(2):
                pool.indirect_dma_start(mo.yg[:, i % 2, s, :], None, self.y.rearrange("m p n -> (m p) n"),
                                        bass.IndirectOffsetOnAxis(ap=k.token_rows[:, s, i:i + 1], axis=0)
                                        ).then_inc(k.x_landed[i % 2].sem, 16)

    def rows_landed(self, eng, i):
        eng.wait_ge(self.k.x_landed[i % 2].sem, self.landed[i % 2] + 32 * (i // 2) + 32)

    def scalar(self, act, ch):
        k, mo = self.k, self.k.mo
        for i, t in enumerate(self.tiles):
            self.rows_landed(act, i)
            if i >= 2:
                act.wait_ge(k.both_done.sem, self.done + i - 1)
            act.activation(mo.sum[:, i % 2, :], mo.yg[:, i % 2, 0, :], ACT.Identity,
                           scale=mo.weight[:, 0, i:i + 1]).then_inc(k.half_done.sem, 1)

    def vector(self, dve, ch):
        k, mo = self.k, self.k.mo
        for i, t in enumerate(self.tiles):
            self.rows_landed(dve, i)
            dve.wait_ge(k.half_done.sem, self.half + i + 1)
            g = k.gatebc[:, 0 if t < ST else 1, :]
            acc = mo.sum[:, i % 2, :]
            ch.step(dve.scalar_tensor_tensor(acc, mo.yg[:, i % 2, 1, :], mo.weight[:, 1, i:i + 1], acc, ALU.mult, ALU.add))
            ch.wait()
            ch.step(dve.tensor_tensor(acc, acc, g, ALU.mult))
            ch.wait()
            dve.tensor_tensor(k.X[:, t, :], k.X[:, t, :], acc, ALU.add).then_inc(k.both_done.sem, 1)


class Gated(Stage):

    def __init__(self, k, blocks, tiles):
        super().__init__(k)
        self.tiles = tiles
        self.slots = []
        for pair in blocks:
            s = []
            for k0 in (0, 4):
                parts = [((lambda s, i=i: s.rearrange("p (c a n) -> p c a n", c=4, a=2)[:, :, i, :]),
                          w[k0 * P:(k0 + 4) * P, :].rearrange("(c p) n -> p c n", p=P)) for i, w in enumerate(pair)]
                s.append(k.rg.plan(parts))
            self.slots.append(s)
        n = self.n = len(blocks) * len(tiles)
        self.gu = Banks(k, ["dve"] * n)
        self.silu = k.silu_done.reserve(n)

    def tensor(self, pe):
        k, T = self.k, len(self.tiles)
        for i in range(self.n):
            j, t = i // T, self.tiles[i % T]
            s = self.slots[j]
            if i % T == 0:
                k.rg.await_landed(pe, s[0])
                k.rg.await_landed(pe, s[1])
            self.gu.may_fill(pe, i)
            for c in range(DK):
                w = k.rg.slot(s[c // 4]).rearrange("p (c n) -> p c n", c=4)
                last = pe.matmul(self.gu.bank(i), k.HT[:, c, t * P:(t + 1) * P], w[:, c % 4, :],
                                 start=(c == 0), stop=(c == DK - 1))
            self.gu.filled(last)
            if i % T == T - 1:
                pe.drain().then_inc(k.weights_used, 2)

    def scalar(self, act, ch):
        k = self.k
        for i in range(self.n):
            self.gu.await_full(act, i)
            if i >= 2:
                self.gu.taken(act, i - 2)
            act.activation(k.silub[:, i % 2, :], self.gu.bank(i)[:, 0:EXH], ACT.Silu).then_inc(k.silu_done.sem, 1)

    def vector(self, dve, ch):
        k, T = self.k, len(self.tiles)
        for i in range(self.n):
            j, t = i // T, self.tiles[i % T]
            self.gu.await_full(dve, i)
            dve.wait_ge(k.silu_done.sem, self.silu + i + 1)
            self.gu.take(i, dve.tensor_tensor(k.Zb(FFN)[:, t, j * EXH:(j + 1) * EXH], self.gu.bank(i)[:, EXH:2 * EXH],
                                              k.silub[:, i % 2, :], ALU.mult))


def two_blocks(nc, A, C, out, scratch, upto=None, dumps=None):
    ctx = ExitStack()
    with ctx:
        k = K()

        def sb(name, shape, dt=F32):
            return ctx.enter_context(nc.sbuf_tensor(name, shape, dt))

        def sem(name):
            return ctx.enter_context(nc.semaphore(name))

        def tally(name):
            return Tally(sem(name))

        k.ring = sb("ring", [P, SLOTS, SLOT])
        k.X = sb("X", [P, NT, D])
        k.HT = sb("HT", [P, DK, NT * P])
        k.Z = sb("Z", [P, NT * EV_W])
        k.T = sb("T", [P, 22 * 512])
        k.ps = ctx.enter_context(nc.psum_tensor("ps", [P, 8, 512], F32))
        k.ident = sb("ident", [P, P])
        k.cmpmask = sb("cmpmask", [P, ST, NCMP])
        k.cmpvalid = sb("cmpvalid", [P, ST])
        k.glamask = sb("glamask", [P, 2, 7, P], U8)
        k.gains = sb("gains", [P, 6, DK])
        k.mc = sb("mc", [P, 2, 48, 2])
        k.mg = sb("mg", [P, 2, 2, 2, DK])
        k.cc = sb("cc", [P, DK, 2])
        k.sc = sb("sc", [P, DK, 2])
        k.hgain = sb("hgain", [P, 4, HD])
        k.ggain = sb("ggain", [P, GDV])
        k.gateb = sb("gateb", [P, 4])
        k.b1 = sb("b1", [P, 2])
        k.w2 = sb("w2", [P, 2, HD])
        k.posT = sb("posT", [P, CMP_LEN])
        k.sink = sb("sink", [P, SWA_HEADS])
        k.rw = sb("rw", [P, 2, DK, 20])
        k.rb = sb("rb", [P, 2, 20])
        k.gw = sb("gw", [32, 2, 256])
        k.kcmp = sb("kcmp", [P, NCMP])
        k.vcmp = sb("vcmp", [32, 2 * HD])
        k.gate3 = sb("gate3", [P, ST, 24])
        k.row_token = sb("row_token", [P, tiles_bound(NT * P)], U32)
        k.token_rows = sb("token_rows", [P, 2, NT], U32)
        k.tile_expert = sb("tile_expert", [P, tiles_bound(NT * P)], I32)
        k.rL = sb("rL", [P, NT, 20])
        k.rG, k.rE, k.rO, k.rA, k.rB = (sb(n, [P, NT, 4]) for n in ("rG", "rE", "rO", "rA", "rB"))
        k.rs = sb("rs", [P, 4, NT])
        k.ss, k.ss2, k.rstd = (sb(n, [P, 8]) for n in ("ss", "ss2", "rstd"))
        k.hstat = sb("hstat", [P, 72])
        k.mx, k.nm, k.den, k.rd, k.es = (sb(n, [P, 4]) for n in ("mx", "nm", "den", "rd", "es"))
        k.gdecay = sb("gdecay", [P, 2 * NT])

        def Zb(w):
            n = min(NT, NT * EV_W // w)
            return k.Z[:, 0:n * w].rearrange("p (t w) -> p t w", w=w)
        k.Zb = Zb
        T = k.T
        k.HN = T[:, 0:NT * D].rearrange("p (t n) -> p t n", n=D)
        qkT = T[:, 0:14 * SEQ].rearrange("p (b n) -> p b n", n=SEQ)
        k.Pb = T[:, 7168:8704].rearrange("p (a n) -> p a n", a=2)
        k.PT = T[:, 8704:10240].rearrange("p (a n) -> p a n", a=2)
        k.bias = T[:, 10240:11264].rearrange("p (a n) -> p a n", a=2)
        k.tmp = T[:, 0:2304]
        k.rope = T[:, 9600:10112].rearrange("p (t a n) -> p t a n", t=ST, a=2)
        band = T[:, 10240:11136]
        k.cmpblk = lambda i: T[:, 8192 + i * 992:8192 + (i + 1) * 992].rearrange("p (n l) -> p n l", l=32)
        k.cmphid = T[:, 10176:10300].rearrange("p (a n) -> p a n", a=2)
        rawT = T[:, 7168:8192].rearrange("p (a n) -> p a n", a=2)

        def g3(o):
            return T[:, o:o + 1536].rearrange("p (a n) -> p a n", a=2)
        k.gqT, k.gkT = g3(0), g3(1536)
        k.gb = T[:, 3072:6144].rearrange("p (d a n) -> p d a n", d=2, a=2)
        k.gA, k.gB, k.gC = g3(6144), g3(7680), g3(9216)
        k.lrT = T[0:32, 6144:6912]
        k.gkh = T[:, 6144:7680].rearrange("p (t a n) -> p t a n", t=NT, a=2)
        k.gS = T[:, 10752:11264].rearrange("p (b a n) -> p b a n", b=2, a=2)
        hflat = k.HT[:, :, :].rearrange("p c n -> p (c n)")
        k.gacc = hflat[:, 0:3072].rearrange("p (t o a n) -> p t o a n", t=NT, o=2, a=2)
        k.gO = hflat[:, 3072:6144].rearrange("p (t n) -> p t n", t=NT)
        k.silub = T[:, 6144:6656].rearrange("p (a n) -> p a n", a=2)
        k.gatebc = T[:, 8192:10240].rearrange("p (a n) -> p a n", a=2)
        k.gtmp = T[:, 0:512]
        hidT = T[:, :].rearrange("p (c n) -> p c n", n=SEQ)
        rowgain = T[:, 8192:9216]
        k.maskf = T[:, 9472:11264].rearrange("p (d l n) -> p d l n", d=2, l=7)
        k.modb = lambda l: T[0:2, 0:6144] if l == 0 else hflat[0:2, 0:6144]

        mo = k.mo = K()
        at = [0]

        def zb(size, pattern=None, **dims):
            x = k.Z[:, at[0]:at[0] + size]
            at[0] += size
            return x.rearrange(pattern, **dims) if pattern else x
        mo.chosen = zb(2 * NT * NEXP, "p (a n e) -> p a n e", a=2, n=NT)
        mo.either, mo.rank, mo.prior, mo.whole, mo.tile, mo.tmp = (zb(NT * NEXP, "p (n e) -> p n e", n=NT) for _ in range(6))
        mo.count, mo.tiles, mo.end, mo.first = (zb(NEXP) for _ in range(4))
        mo.at_tile, mo.at_row, mo.weight = (zb(2 * NT, "p (a n) -> p a n", a=2) for _ in range(3))
        mo.iota, mo.before, mo.ones, mo.token = zb(P), zb(P), zb(P), zb(NT)
        bound = tiles_bound(NT * P)
        mo.ended = zb(bound * NEXP, "p (m e) -> p m e", e=NEXP)
        mo.expert = zb(bound)
        mo.row_hot = zb(2 * NT * P, "p (u n) -> p u n", u=2 * NT)
        mo.tile_hot = zb(2 * NT * bound, "p (u n) -> p u n", u=2 * NT)
        mo.ysb = zb(2 * D, "p (a n) -> p a n", a=2)
        mo.yg = zb(4 * D, "p (a s n) -> p a s n", a=2, s=2)
        mo.silu, mo.hid = (zb(2 * EXH, "p (a n) -> p a n", a=2) for _ in range(2))
        mo.hidT = zb(2 * EXH, "p (a c n) -> p a c n", a=2, c=2)
        mo.xg = T[:, 0:2 * D].rearrange("p (a n) -> p a n", a=2)
        mo.xT = T[:, 2 * D:4 * D].rearrange("p (a c n) -> p a c n", a=2, c=DK)
        mo.sum = T[:, 0:2 * D].rearrange("p (a n) -> p a n", a=2)

        k.landed = [sem(f"weights_landed_{i}") for i in range(SLOTS)]
        k.weights_used = sem("weights_used")
        k.stage_done = sem("stage_done")
        k.bias_spread = sem("bias_spread")
        k.step_done, k.small_landed = tally("step_done"), tally("small_landed")
        k.norm_squares, k.norm_mean = tally("norm_squares"), tally("norm_mean")
        k.norm_roots, k.norm_rows = tally("norm_roots"), tally("norm_rows")
        k.scores_full, k.scores_topped, k.probs_done = tally("scores_full"), tally("scores_topped"), tally("probs_done")
        k.probsT_full, k.probsT_out = tally("probsT_full"), tally("probsT_out")
        k.out_full, k.out_taken = tally("out_full"), tally("out_taken")
        k.bias_landed, k.bias_used, k.gates_done = tally("bias_landed"), tally("bias_used"), tally("gates_done")
        k.gla_diff, k.gla_exp, k.gla_k, k.gla_qk = tally("gla_diff"), tally("gla_exp"), tally("gla_k"), tally("gla_qk")
        k.rows_stored, k.lists_ready = tally("rows_stored"), tally("lists_ready")
        k.moe_sems = {n: tally("moe_" + n) for n in ("x_transposed", "x_out_act", "x_out_dve", "gu_full", "silu_ready", "hid_ready",
                                                     "hid_transposed", "hid_out", "y_full", "y_out_act", "y_out_dve")}
        k.x_landed = [tally(f"rows_landed_{p}") for p in range(2)]
        k.y_stored = [tally(f"y_stored_{p}") for p in range(2)]
        k.half_done, k.both_done = tally("half_done"), tally("both_done")
        k.silu_done = tally("silu_done")
        k.lanes = [(tally(f"psum_full_{i}"), {"act": tally(f"psum_taken_by_scalar_{i}"), "dve": tally(f"psum_taken_by_vector_{i}")})
                   for i in range(3)]
        k.psum_full = k.lanes[0][0]
        dve_order, act_order, pool_order = sem("vector_order"), sem("scalar_order"), sem("gpsimd_order")
        k.rg = Ring(k)
        stages = []
        add = stages.append

        def bc(ap, n, off=0, parts=P):
            return bass.AP(tensor=ap.tensor, offset=ap.offset + off, ap=[[0, parts], [1, n]])

        table = T[0:33, 7424:7440]
        hot = T[0:33, 6144:6144 + 2 * ROW].rearrange("p (a n) -> p a n", a=2)
        pairs = [(k.ident[:, :], C["ident"]), (k.cmpmask[:, :, :], C["cmpmask"]), (k.cmpvalid[:, :], C["cmpvalid"]),
                 (k.maskf, C["glamask"]), (k.gains[:, :, :], A["gains"]), (k.cc[:, :, :], A["cc"]),
                 (k.gateb[:, :], A["gateb"]), (k.b1[:, :], A["b1"]), (k.posT[:, :], A["posT"]),
                 (k.X[:, 0:ST, :], A["x"][0].rearrange("(t p) n -> p t n", p=P)),
                 (k.X[:, ST:NT, :], A["ctx_2"][0].rearrange("(t p) n -> p t n", p=P)),
                 (k.ggain[:, :], bc(A["gla_out_norm_2"], GDV)), (k.sink[:, :], bc(A["swa_sink_2"], SWA_HEADS)),
                 (k.w2[:, 0, :], A["cmp_k_w2"][0]), (k.w2[:, 1, :], A["cmp_v_w2"][0]), (k.gw[:, :, :], A["gw"]),
                 (table, A["table"]), (hot, C["hot"]),
                 (k.modb(0), bc(A["mod_b_2"], 6144, 0, 2)), (k.modb(1), bc(A["mod_b_2"], 6144, 6144, 2))]
        for i, n in enumerate(("att_q_norm_2", "att_k_norm_2", "swa_q_norm_2", "swa_k_norm_2")):
            pairs.append((k.hgain[:, i, :], bc(A[n], HD)))
        for l in range(2):
            pairs += [(k.rw[:, l, :, 0:4], A["router_group_w_2"][l].rearrange("(c p) n -> p c n", p=P)),
                      (k.rw[:, l, :, 4:20], A["router_expert_w_2"][l].rearrange("(c p) n -> p c n", p=P)),
                      (k.rb[:, l, 0:4], bc(A["router_group_b_2"], 4, 4 * l)),
                      (k.rb[:, l, 4:20], bc(A["router_expert_b_2"], 16, 16 * l))]
        add(Load(k, pairs))

        mods = ModVectors(k, A)
        add(mods)
        rows = BiasRows(k, table, hot, scratch["bias"], scratch["spread"])
        rows.buf = T[0:8, 7440:7440 + 2 * ROW].rearrange("p (a n) -> p a n", a=2)
        add(rows)
        add(ModColumns(k, mods.rows, scratch["mods"]))

        seq, allt, ctxt = list(range(ST)), list(range(NT)), list(range(ST, NT))

        def cols_of(ts):
            return slice(ts[0] * P, (ts[-1] + 1) * P)

        def gain(i):
            return lambda c: k.gains[:, i, c:c + 1]

        def hT(c, t):
            return k.HT[:, c, t * P:(t + 1) * P]

        def to_z(w, off=0):
            z = k.Zb(w)
            return lambda eng, name, ch, t, c0, cn, ps: copy(eng, name, z[:, t, off + c0:off + c0 + cn], ps)

        def cols(z, c, n=P):
            return lambda t: z[:, t, c:c + n]

        def head_pair(z, c0, r):
            return cols(z, c0 + r * P)

        scale = HD ** -0.5
        add(norm_stage(k, [(seq, gain(0), None)]))
        add(Linear(k, hT, DK, A["w_in"][0], IN_W, seq, to_z(IN_W)))
        z = k.Zb(IN_W)
        units = [(cols(z, AQ + b * P), P, seq, qkT[:, b, :], scale) for b in range(4)]
        units += [(cols(z, AK + b * P), P, seq, qkT[:, 4 + b, :], None) for b in range(4)]
        units += [(head_pair(z, BQ, r), P, seq, qkT[:, 8 + r, :], scale) for r in range(4)]
        units += [(cols(z, KSL), P, seq, qkT[:, 12, :], None), (cols(z, KW), P, seq, qkT[:, 13, :], None),
                  (cols(z, KC), P, seq, rawT[:, 0, :], None), (cols(z, VC), P, seq, rawT[:, 1, :], None)]
        add(Transposes(k, units))
        add(Sigmoids(k))
        add(Compress(k, A, rawT[:, 0, :], rawT[:, 1, :]))

        def first_jobs(h, tile):
            jobs = []
            for i in range(ST):
                n = (i + 1) * P
                base = dict(bias=tile[:, 384 - i * P:512], sink=None, gate=None, first=True)
                if h < A_HEADS:
                    r = slice(64 * (h % 2), 64 * (h % 2) + 64)
                    jobs.append(dict(base, q=qkT[r, h // 2, i * P:n], keys=[(qkT[r, 4 + h // 2, 0:n], n)],
                                     values=[(z[:, t, AV + h * HD:AV + (h + 1) * HD], P) for t in range(i + 1)],
                                     out=z[:, i, AQ + h * HD:AQ + (h + 1) * HD]))
                    continue
                hb = h - A_HEADS
                g, rr = hb // 4, hb % 4
                r = slice(64 * g, 64 * g + 64)
                q = qkT[r, 8 + rr, i * P:n]
                at = BQ + (2 * rr + g) * HD
                o = z[:, i, at:at + HD]
                gates = [k.gate3[:, i, hb * 3 + b:hb * 3 + b + 1] for b in range(3)]
                jobs.append(dict(base, q=q, keys=[(k.kcmp[r, :], NCMP)], values=[(k.vcmp[0:NCMP, g * HD:(g + 1) * HD], NCMP)],
                                 bias=k.cmpmask[:, i, :], gate=gates[0], out=o))
                for b, kk, vv in ((1, 12, VSL), (2, 13, VW)):
                    jobs.append(dict(base, q=q, keys=[(qkT[r, kk, 0:n], n)], gate=gates[b], first=False,
                                     values=[(z[:, t, vv + g * HD:vv + (g + 1) * HD], P) for t in range(i + 1)], out=o))
            return jobs
        add(Bias(k, first_jobs, list(range(16)), scratch["spread"]))

        def mixT_units(w, starts, tiles):
            zz = k.Zb(w)
            return [(cols(zz, c0), P, ts, k.HT[:, c, cols_of(ts)], None) for c, c0 in enumerate(starts)
                    for ts in ([t for t in tiles if t < ST], [t for t in tiles if t >= ST]) if ts]
        add(Transposes(k, mixT_units(IN_W, [AQ + P * b for b in range(4)] + [BQ + P * b for b in range(4)], seq)))

        def residual(eng, name, ch, t, c0, cn, ps):
            x = k.X[:, t, c0:c0 + cn]
            return eng.tensor_tensor(x, ps, x, ALU.add)
        add(Linear(k, hT, DK, A["w_out"][0], D, seq, residual, ["dve"] * 8))

        add(norm_stage(k, [(seq, gain(1), None)]))
        wg, wu = A["w_gate"][0], A["w_up"][0]
        add(Gated(k, [(wg[:, j * EXH:(j + 1) * EXH], wu[:, j * EXH:(j + 1) * EXH]) for j in range(FFN // EXH)], seq))
        zf = k.Zb(FFN)
        add(Transposes(k, [(cols(zf, c * P), P, seq, hidT[:, c, :], None) for c in range(FFN // P)]))
        add(Linear(k, lambda c, t: hidT[:, c, t * P:(t + 1) * P], FFN // P, A["w_down"][0], D, seq, residual, ["dve"] * 8))
        add(Load(k, [(rowgain, bc(A["norm_f_g"], D))]))
        add(RowNorm(k, seq, rowgain))

        def mod_sets(l, w, both):
            m = (0, 3)[w]

            def col(buf, r, at):
                return lambda c: buf[:, at + c, r:r + 1]

            def gcol(r):
                return lambda c: k.mg[:, l, w, r, c:c + 1]
            sets = [(seq, gcol(0), col(k.mc[:, l], 0, m * DK))]
            return sets + ([(ctxt, gcol(1), col(k.mc[:, l], 1, m * DK))] if both else [])

        def gated_take(eng, name, ch, t, c0, cn, ps):
            g = k.gatebc[:, 0 if t < ST else 1, c0:c0 + cn]
            x = k.X[:, t, c0:c0 + cn]
            ch.wait()
            ch.step(eng.tensor_tensor(k.gtmp[:, 0:cn], ps, g, ALU.mult))
            ch.wait()
            ch.step(eng.tensor_tensor(x, x, k.gtmp[:, 0:cn], ALU.add))
            return eng.drain()

        def gate_loads(l, m, n):
            return [(k.gatebc[:, r, :], bc(scratch["mods"], D, (l * 2 + r) * 6144 + m * D)) for r in range(n)]

        k.gate_loads, k.C = gate_loads, C

        def moe(l, tiles):
            both = len(tiles) > ST
            add(norm_stage(k, mod_sets(l, 1, both)))
            h, y = scratch["h"][l], scratch["y"][l]
            add(Router(k, l, tiles, h))
            dispatch = Dispatch(k, len(tiles))
            add(dispatch)
            add(Experts(k, l, len(tiles), A, dispatch, h, y))
            add(Combine(k, tiles, y))

        add(norm_stage(k, mod_sets(0, 0, True)))
        add(Linear(k, hT, DK, A["ev_w_in_2"][0], EV_W, allt, to_z(EV_W)))
        ze = k.Zb(EV_W)
        units = []
        for ts in (seq, ctxt):
            c = cols_of(ts)
            for p in range(2):
                units.append((cols(ze, GQ + p * P), P, ts, k.gqT[:, p, c], GDK ** -0.5))
                units.append((cols(ze, GK + p * P), P, ts, k.gkT[:, p, c], None))
            units.append((cols(ze, LR, 32), 32, ts, k.lrT[:, c], None))
        add(Transposes(k, units))
        add(GlaGates(k))
        for d in range(2):
            add(GlaScores(k, d))
            add(GlaDecayed(k, d))
            add(GlaScan(k, d))
        add(GlaOutput(k))
        add(Load(k, [(k.rope, C["rope"])]))
        qk_gain = [(8, k.hgain[:, 0, :]), (2, k.hgain[:, 1, :])]
        add(HeadNorm(k, EV_W, [(seq, EQ, 10, qk_gain), (ctxt, EQ, 10, qk_gain)]))
        eqT = T[:, 0:4 * 768].rearrange("p (b n) -> p b n", n=768)
        ekT = T[:, 3072:3840]
        units = []
        for ts in (seq, ctxt):
            units += [(head_pair(ze, EQ, r), P, ts, eqT[:, r, cols_of(ts)], scale) for r in range(4)]
            units.append((cols(ze, EK), P, ts, ekT[:, cols_of(ts)], None))
        add(Transposes(k, units))
        jobs = []
        for h in range(8):
            g, rr = h // 4, h % 4
            r = slice(64 * g, 64 * g + 64)
            for i in allt:
                ks = [(ekT[r, 0:768], 768)] if i < ST else [(ekT[r, 512:768], 256)]
                jobs.append(dict(q=eqT[r, rr, i * P:(i + 1) * P], keys=ks, bias=None, sink=None, gate=None, first=True,
                                 values=[(ze[:, t, EVV + g * HD:EVV + (g + 1) * HD], P) for t in (allt if i < ST else ctxt)],
                                 out=ze[:, i, EQ + (2 * rr + g) * HD:EQ + (2 * rr + g + 1) * HD]))
        add(Attention(k, jobs))
        add(Transposes(k, mixT_units(EV_W, [P * b for b in range(4)] + [EQ + P * b for b in range(4)], allt)))
        add(Load(k, gate_loads(0, 2, 2)))
        add(Linear(k, hT, DK, A["ev_w_out_2"][0], D, allt, gated_take, ["dve"] * 12))
        moe(0, allt)

        add(norm_stage(k, mod_sets(1, 0, True)))
        add(Linear(k, hT, DK, A["od_w_in_2"][0][:, 0:1024], 1024, seq, to_z(OD_W)))
        add(Linear(k, hT, DK, A["od_w_in_2"][0][:, 1024:OD_W], 256, allt, to_z(OD_W, 1024)))
        zo = k.Zb(OD_W)
        add(Load(k, [(k.rope, C["rope"])]))
        add(HeadNorm(k, OD_W, [(seq, OQ, 18, [(16, k.hgain[:, 2, :]), (2, k.hgain[:, 3, :])]),
                               (ctxt, OK_, 2, [(2, k.hgain[:, 3, :])])]))
        oqT = T[:, 0:8 * SEQ].rearrange("p (b n) -> p b n", n=SEQ)
        okT = T[:, 4096:4864]
        units = [(head_pair(zo, OQ, r), P, seq, oqT[:, r, :], scale) for r in range(8)]
        units += [(cols(zo, OK_), P, ts, okT[:, cols_of(ts)], None) for ts in (seq, ctxt)]
        add(Load(k, [(band, C["band"])]))
        add(Transposes(k, units))
        jobs = []
        for h in range(SWA_HEADS):
            g, rr = h // 8, h % 8
            r = slice(64 * g, 64 * g + 64)
            for i in seq:
                ts = [t for t in (i - 1, i, i + 1) if 0 <= t < ST]
                n = len(ts) * P
                near, far = [(okT[r, cols_of(ts)], n)], [(okT[r, SEQ:SEQ + CTX], CTX)]
                keys, vt, bias = (near + far, ts + ctxt, band[:, CTX + P:896]) if i == 0 else (far + near, ctxt + ts, band[:, 0:CTX + n])
                jobs.append(dict(q=oqT[r, rr, i * P:(i + 1) * P], keys=keys, bias=bias, sink=k.sink[:, h:h + 1], gate=None,
                                 first=True, values=[(zo[:, t, OV + g * HD:OV + (g + 1) * HD], P) for t in vt],
                                 out=zo[:, i, (2 * rr + g) * HD:(2 * rr + g + 1) * HD]))
        add(Attention(k, jobs))
        add(Transposes(k, mixT_units(OD_W, [P * b for b in range(8)], seq)))
        add(Load(k, gate_loads(1, 2, 1)))
        add(Linear(k, hT, DK, A["od_w_out_2"][0], D, seq, gated_take, ["dve"] * 8))
        moe(1, seq)
        if upto is not None:
            stages = stages[:upto]
            k.small_landed = tally("dumped")
            k.rg.loads = k.rg.loads[:dumps["loads"](k, stages)] if "loads" in dumps else k.rg.loads
        result = Load(k, [(out[0].rearrange("(t p) n -> p t n", p=P), k.X[:, 0:ST, :])] + (dumps["pairs"](k) if dumps else []))
        stages.append(result)

        def meet(eng, i):
            eng.drain().then_inc(k.stage_done, 1)
            eng.wait_ge(k.stage_done, 4 * (i + 1))

        block = ctx.enter_context(nc.Block())

        @block.sync
        def _(sp):
            k.rg.fill(sp)

        @block.tensor
        def _(pe):
            for i, s in enumerate(stages):
                s.tensor(pe)
                meet(pe, i)

        @block.vector
        def _(dve):
            ch = Chain(dve, dve_order)
            for i, s in enumerate(stages):
                s.vector(dve, ch)
                meet(dve, i)

        @block.scalar
        def _(act):
            ch = Chain(act, act_order)
            for i, s in enumerate(stages):
                s.scalar(act, ch)
                meet(act, i)

        @block.gpsimd
        def _(pool):
            ch = Chain(pool, pool_order)
            for i, s in enumerate(stages):
                s.gpsimd(pool, ch)
                meet(pool, i)
        return stages


RAW = ["x", "ctx_2", "w_in", "cmp_k_w1", "cmp_k_w2", "cmp_v_w1", "cmp_v_w2", "w_out", "w_gate", "w_up", "w_down",
       "norm_f_g", "mod_w_2", "mod_b_2", "ev_w_in_2", "ev_w_out_2", "gla_out_norm_2", "att_q_norm_2", "att_k_norm_2",
       "od_w_in_2", "od_w_out_2", "swa_sink_2", "swa_q_norm_2", "swa_k_norm_2", "router_group_w_2", "router_group_b_2",
       "router_expert_w_2", "router_expert_b_2", "exp_w_gate_2", "exp_w_up_2", "exp_w_down_2"]


def lay_out(inputs):
    a = {n: np.ascontiguousarray(inputs[n]) for n in RAW}

    def by_pair(w, at, per, axis):
        w = np.asarray(w)
        idx = np.arange(w.shape[axis])
        idx[at:at + 2 * per * HD] = at + np.arange(2 * per * HD).reshape(2, per, HD).transpose(1, 0, 2).ravel()
        return np.ascontiguousarray(np.take(w, idx, axis))
    a["w_in"] = by_pair(a["w_in"], BQ, 4, 2)
    a["w_out"] = by_pair(a["w_out"], 512, 4, 1)
    a["ev_w_in_2"] = by_pair(a["ev_w_in_2"], EQ, 4, 2)
    a["ev_w_out_2"] = by_pair(a["ev_w_out_2"], 512, 4, 1)
    a["od_w_in_2"] = by_pair(a["od_w_in_2"], OQ, 8, 2)
    a["od_w_out_2"] = by_pair(a["od_w_out_2"], 0, 8, 1)

    def column(v):
        return np.asarray(v).reshape(DK, P).T
    a["gains"] = np.ascontiguousarray(np.stack(
        [column(inputs["norm1_g"][0]), column(inputs["norm2_g"][0])]
        + [column(inputs["norm_mix_2"][l]) for l in range(2)] + [column(inputs["norm_ffn_2"][l]) for l in range(2)], 1))
    a["cc"] = np.ascontiguousarray(np.stack([column(inputs["c_2"][0]), column(inputs["c_ctx_2"])], 2))
    a["gateb"] = np.ascontiguousarray(np.asarray(inputs["gla_gate_b_2"]).reshape(4, P).T)
    a["b1"] = np.ascontiguousarray(np.stack([inputs["cmp_k_b1"][0], inputs["cmp_v_b1"][0]], 1))
    pos = np.asarray(inputs["cmp_pos"][0]).T
    a["posT"] = np.ascontiguousarray(np.concatenate([pos, pos], 0))
    gw = np.zeros((32, 2, 256), np.float32)
    for d in range(2):
        gw[16 * d:16 * d + 16, d] = inputs["gla_gate_w_2"][0, d]
    a["gw"] = gw
    a["table"] = np.ascontiguousarray(np.concatenate([inputs["rel_bias"], np.ones((1, 16), np.float32)], 0))
    return a


def build(nc, inputs, upto=None, dumps=None):
    arrays, A, C = {}, {}, {}
    for dst, src, tag in ((A, lay_out(inputs), "in"), (C, shape_constants(), "const")):
        for n, v in src.items():
            arrays[f"{tag}_{n}"] = v
            dst[n] = nc.dram_tensor(f"{tag}_{n}", v.shape, mybir.dt.from_np(v.dtype), kind="ExternalInput").ap()
    out = nc.dram_tensor("out_x", (1, SEQ, D), F32, kind="ExternalOutput").ap()
    scratch = {"bias": nc.dram_tensor("bias_rows", (16, ROW), F32, kind="Internal").ap(),
               "spread": nc.dram_tensor("bias_spread", (16, P, ROW), F32, kind="Internal").ap(),
               "h": [nc.dram_tensor(f"moe_rows_{l}", (n * P, D), F32, kind="Internal").ap() for l, n in enumerate((NT, ST))],
               "y": [nc.dram_tensor(f"moe_out_{l}", (tiles_bound(n * P), P, D), F32, kind="Internal").ap()
                     for l, n in enumerate((NT, ST))],
               "mods": nc.dram_tensor("mod_rows", (2, 2, 6144), F32, kind="Internal").ap()}
    d = dumps(nc) if dumps else None
    stages = two_blocks(nc, A, C, out, scratch, upto, d)
    return arrays, stages


def kernel(**inputs):
    import concourse.bacc as bacc
    from concourse.bass_utils import run_bass_kernel_spmd

    nc = bacc.Bacc("TRN2", target_bir_lowering=False, num_devices=1)
    arrays, _ = build(nc, inputs)
    r = run_bass_kernel_spmd(nc, [arrays], core_ids=[0])
    return r.results[0]["out_x"]
```
